# Optimizing a Trainium2 kernel written in Bass

```python
import math
import jax
import jax.numpy as jnp
from jax import lax
import numpy as np

D_MODEL = 2048
BATCH = 1
SEQ = 512
DEPTH = 1
DEC_BATCH = 8
DEC_SEQ = 4
PAST_LEN = 2048
PAGE_SIZE = 128

HEAD_DIM = 128
A_WIDTH = D_MODEL // 2
B_WIDTH = D_MODEL // 4
C_WIDTH = D_MODEL - A_WIDTH - B_WIDTH
MIX_WIDTH = A_WIDTH + B_WIDTH + C_WIDTH
A_HEADS = A_WIDTH // HEAD_DIM
A_KV_HEADS = A_HEADS // 4
A_GROUP = A_HEADS // A_KV_HEADS
CMP_LEN = 32
CMP_STRIDE = 16
CMP_HIDDEN = 2 * HEAD_DIM
SLC_LEN = 64
SLC_TOP = 16
WINDOW = 512
FORCE_SCORE = 1e6
POOL_WINDOWS = (2, 4, 8, 16)
B_GROUPS = len(POOL_WINDOWS)
B_GROUP_DIM = B_WIDTH // B_GROUPS
POOL_BUF = max(POOL_WINDOWS) - 1
C_HEADS = C_WIDTH // HEAD_DIM
IDX_HEADS = 4
IDX_DIM = 64
IDX_TOPK_MAX = 256
N_BUCKETS = 32
MAX_DISTANCE = 128
BIAS_HEADS = A_HEADS + C_HEADS
Q_BLOCK = 128
EPS = 1e-6
IN_SIZES = (A_WIDTH, 6 * A_KV_HEADS * HEAD_DIM, 3 * A_HEADS, A_WIDTH,
            B_WIDTH, B_WIDTH,
            C_WIDTH, 2 * HEAD_DIM, IDX_HEADS * IDX_DIM, IDX_DIM, IDX_HEADS, C_WIDTH)
N_IN = sum(IN_SIZES)
N_PAGES = PAST_LEN // PAGE_SIZE
N_POOL_PAGES = (5 * DEC_BATCH * N_PAGES) // 4
WIN_BUF = min(WINDOW, PAST_LEN)

kernel_name = 'hybrid_nsa_pool_dsa_decode_step'

def rms_norm(x, g):
    xf = x.astype(jnp.float32)
    y = xf * lax.rsqrt(jnp.mean(xf * xf, axis=-1, keepdims=True) + EPS)
    return (y * g.astype(jnp.float32)).astype(x.dtype)

def masked_softmax(s, mask):
    s = jnp.where(mask, s.astype(jnp.float32), -jnp.inf)
    m = jnp.max(s, axis=-1, keepdims=True)
    m = jnp.where(jnp.isfinite(m), m, 0.0)
    e = jnp.where(mask, jnp.exp(s - m), 0.0)
    return e / jnp.maximum(jnp.sum(e, axis=-1, keepdims=True), 1e-30)

def t5_bucket(rel):
    rel = jnp.maximum(rel, 0)
    exact = N_BUCKETS // 2
    relf = jnp.maximum(rel, exact).astype(jnp.float32)
    log_b = exact + (jnp.log(relf / exact) / math.log(MAX_DISTANCE / exact) * (N_BUCKETS - exact)).astype(jnp.int32)
    return jnp.where(rel < exact, rel, jnp.minimum(log_b, N_BUCKETS - 1))

def split_columns(z):
    out = []
    off = 0
    for size in IN_SIZES:
        out.append(z[..., off:off + size])
        off += size
    return out

def prepare(x, c, norm_g, w_ada, b_ada, w_in, a_qnorm, a_knorm, c_qnorm, c_knorm):
    mod = jax.nn.silu(c) @ w_ada + b_ada
    shift, scale, gate = jnp.split(mod, 3, axis=-1)
    h = rms_norm(x, norm_g) * (1.0 + scale[:, None]) + shift[:, None]
    (a_q, a_kv, a_gate, a_silu, b_in, b_silu,
     c_q, c_kv, c_iq, c_ik, c_iw, c_silu) = split_columns(h @ w_in)
    B, T = x.shape[:2]
    kv = a_kv.reshape(B, T, 6, A_KV_HEADS, HEAD_DIM)
    a_rows = jnp.stack([kv[:, :, 0], kv[:, :, 1], rms_norm(kv[:, :, 2], a_knorm[1]), kv[:, :, 3]], axis=2)
    win_rows = jnp.stack([rms_norm(kv[:, :, 4], a_knorm[2]), kv[:, :, 5]], axis=2)
    ckv = c_kv.reshape(B, T, 2, HEAD_DIM)
    c_rows = jnp.stack([rms_norm(ckv[:, :, 0], c_knorm), ckv[:, :, 1]], axis=2)
    return {
        'gate': gate,
        'a_q': rms_norm(a_q.reshape(B, T, A_HEADS, HEAD_DIM), a_qnorm),
        'a_gate': a_gate.reshape(B, T, 3, A_HEADS),
        'a_rows': a_rows,
        'win_rows': win_rows,
        'b_in': b_in,
        'c_q': rms_norm(c_q.reshape(B, T, C_HEADS, HEAD_DIM), c_qnorm),
        'c_rows': c_rows,
        'c_iq': c_iq.reshape(B, T, IDX_HEADS, IDX_DIM),
        'c_kidx': c_ik,
        'c_iw': c_iw,
        'silu': (a_silu, b_silu, c_silu),
    }

def finish(x, gate, o_a, o_b, o_c, silu_parts, w_out):
    a_s, b_s, c_s = silu_parts
    mixed = jnp.concatenate([o_a * jax.nn.silu(a_s), o_b * jax.nn.silu(b_s), o_c * jax.nn.silu(c_s)], axis=-1)
    return x + gate[:, None] * (mixed @ w_out)

def compress(x, pe, w1, b1, w2, b2):
    B, L = x.shape[:2]
    r = CMP_LEN // CMP_STRIDE
    n_chunk = L // CMP_STRIDE
    nc = n_chunk - r + 1
    ch = x[:, :n_chunk * CMP_STRIDE].reshape(B, n_chunk, CMP_STRIDE, A_KV_HEADS, HEAD_DIM)
    w1p = w1.reshape(r, CMP_STRIDE, HEAD_DIM, CMP_HIDDEN)
    pep = pe.reshape(r, CMP_STRIDE, HEAD_DIM)
    hid = b1
    for p in range(r):
        part = jnp.einsum('bcskd,sdh->bckh', ch + pep[p][:, None, :], w1p[p])
        hid = hid + part[:, p:p + nc]
    return jax.nn.gelu(hid) @ w2 + b2

def to_blocks(x):
    B, L = x.shape[:2]
    ns = -(-L // SLC_LEN)
    x = jnp.pad(x, ((0, 0), (0, ns * SLC_LEN - L), (0, 0), (0, 0)))
    return x.reshape(B, ns, SLC_LEN, A_KV_HEADS, HEAD_DIM).transpose(0, 3, 1, 2, 4)

def nsa_keyside(a_all, pe, w1, b1, w2, b2, knorm_cmp):
    k_cmp = rms_norm(compress(a_all[:, :, 0], pe[0], w1[0], b1[0], w2[0], b2[0]), knorm_cmp)
    v_cmp = compress(a_all[:, :, 1], pe[1], w1[1], b1[1], w2[1], b2[1])
    e_pos = jnp.arange(k_cmp.shape[1]) * CMP_STRIDE + CMP_LEN - 1
    return k_cmp, v_cmp, e_pos, to_blocks(a_all[:, :, 2]), to_blocks(a_all[:, :, 3])

def slc_importance(p_imp, ns):
    nc = p_imp.shape[-1]
    r1 = SLC_LEN // CMP_STRIDE
    r2 = CMP_LEN // CMP_STRIDE
    pad_r = max(r1 * ns - nc + r1, 0)
    p = jnp.pad(p_imp, [(0, 0)] * (p_imp.ndim - 1) + [(r2 - 1, pad_r)])
    acc = jnp.zeros(p_imp.shape[:-1] + (ns,), jnp.float32)
    for m in range(r1):
        for n in range(r2):
            o = m + n
            acc = acc + p[..., o:o + r1 * ns].reshape(p.shape[:-1] + (ns, r1))[..., 0]
    return acc

def nsa_core(q, gate, q_pos, kc, vc, e_pos, ks_blk, vs_blk, kw, vw, w_pos, rel_a):
    B, Tq = q.shape[:2]
    scale = HEAD_DIM ** -0.5
    qg = q.reshape(B, Tq, A_KV_HEADS, A_GROUP, HEAD_DIM)

    def pair_bias(rel):
        return rel_a[t5_bucket(rel)].reshape(rel.shape + (A_KV_HEADS, A_GROUP)).transpose(0, 2, 3, 1)

    rel_c = q_pos[:, None] - e_pos[None, :]
    s_c = jnp.einsum('btkgd,bnkd->btkgn', qg, kc).astype(jnp.float32) * scale + pair_bias(rel_c)[None]
    p_c = masked_softmax(s_c, (rel_c >= 0)[None, :, None, None, :])
    o_c = jnp.einsum('btkgn,bnkd->btkgd', p_c.astype(vc.dtype), vc)

    ns = ks_blk.shape[2]
    p_slc = slc_importance(p_c.sum(axis=3), ns)
    blk = jnp.arange(ns)[None, :]
    cur = (q_pos // SLC_LEN)[:, None]
    visible = blk <= cur
    forced = (blk == 0) | (blk == cur) | (blk == cur - 1)
    score = jnp.where(visible[None, :, None, :], jnp.where(forced[None, :, None, :], FORCE_SCORE, p_slc), -jnp.inf)
    top_v, top_i = lax.top_k(score, min(SLC_TOP, ns))
    idx = top_i.transpose(0, 2, 1, 3)
    ok_blk = jnp.isfinite(top_v).transpose(0, 2, 1, 3)
    gather = jax.vmap(jax.vmap(lambda a, i: a[i]))
    k_s = gather(ks_blk, idx)
    v_s = gather(vs_blk, idx)
    rel_s = q_pos[None, None, :, None, None] - (idx[..., None] * SLC_LEN + jnp.arange(SLC_LEN))
    ok_s = ok_blk[..., None] & (rel_s >= 0)
    tbl = rel_a.reshape(N_BUCKETS, A_KV_HEADS, A_GROUP).transpose(1, 0, 2)
    bias_s = jax.vmap(lambda t, r: t[r], in_axes=(0, 1), out_axes=1)(tbl, t5_bucket(rel_s))
    qt = qg.transpose(0, 2, 1, 3, 4)
    s_s = jnp.einsum('bktgd,bktnsd->bktgns', qt, k_s).astype(jnp.float32) * scale + bias_s.transpose(0, 1, 2, 5, 3, 4)
    n_sel = idx.shape[-1] * SLC_LEN
    p_s = masked_softmax(s_s.reshape(B, A_KV_HEADS, Tq, A_GROUP, n_sel), ok_s.reshape(B, A_KV_HEADS, Tq, 1, n_sel))
    o_s = jnp.einsum('bktgm,bktmd->btkgd', p_s.astype(vs_blk.dtype), v_s.reshape(B, A_KV_HEADS, Tq, n_sel, HEAD_DIM))

    rel_w = q_pos[:, None] - w_pos[None, :]
    ok_w = (rel_w >= 0) & (rel_w <= WINDOW) & (w_pos >= 0)[None, :]
    s_w = jnp.einsum('btkgd,bskd->btkgs', qg, kw).astype(jnp.float32) * scale + pair_bias(rel_w)[None]
    p_w = masked_softmax(s_w, ok_w[None, :, None, None, :])
    o_w = jnp.einsum('btkgs,bskd->btkgd', p_w.astype(vw.dtype), vw)

    g = jax.nn.sigmoid(gate.astype(jnp.float32)).reshape(B, Tq, 3, A_KV_HEADS, A_GROUP, 1)
    o = g[:, :, 0] * o_c + g[:, :, 1] * o_s + g[:, :, 2] * o_w
    return o.reshape(B, Tq, A_WIDTH).astype(q.dtype)

def dsa_core(q, qi, wi, q_pos, k, v, kidx, rel_c):
    B, Tq = q.shape[:2]
    L = k.shape[1]
    n_keep = min(IDX_TOPK_MAX, L // 4)
    rel = q_pos[:, None] - jnp.arange(L)[None, :]
    dots = jax.nn.relu(jnp.einsum('bthd,bsd->bths', qi, kidx).astype(jnp.float32))
    score = jnp.einsum('bth,bths->bts', wi.astype(jnp.float32), dots)
    score = jnp.where((rel >= 0)[None], score, -jnp.inf)
    top_v, top_i = lax.top_k(score, n_keep)
    take = jax.vmap(lambda a, i: a[i])
    k_g = take(k, top_i)
    v_g = take(v, top_i)
    bias = rel_c[t5_bucket(q_pos[None, :, None] - top_i)]
    s = jnp.einsum('bthd,btkd->bthk', q, k_g).astype(jnp.float32) * HEAD_DIM ** -0.5 + bias.transpose(0, 1, 3, 2)
    p = masked_softmax(s, jnp.isfinite(top_v)[:, :, None, :])
    o = jnp.einsum('bthk,btkd->bthd', p.astype(v.dtype), v_g)
    return o.reshape(B, Tq, C_WIDTH)

def pool_mix(u_ext, pos0, w_pool, scale):
    B = u_ext.shape[0]
    T = u_ext.shape[1] - POOL_BUF
    uf = u_ext.astype(jnp.float32)
    cs = jnp.pad(jnp.cumsum(uf, axis=1), ((0, 0), (1, 0), (0, 0)))
    pos = pos0 + jnp.arange(T)
    cur = uf[:, POOL_BUF:]
    groups = []
    for g, w in enumerate(POOL_WINDOWS):
        c0, c1 = g * B_GROUP_DIM, (g + 1) * B_GROUP_DIM
        win_sum = cs[:, POOL_BUF + 1:POOL_BUF + 1 + T, c0:c1] - cs[:, POOL_BUF + 1 - w:POOL_BUF + 1 - w + T, c0:c1]
        cnt = jnp.minimum(pos + 1, w).astype(jnp.float32)
        groups.append(win_sum / cnt[None, :, None] - cur[:, :, c0:c1])
    d = jnp.stack(groups, axis=2)
    y = jnp.einsum('btgc,gcd->btgd', d, w_pool.astype(jnp.float32)).reshape(B, T, B_WIDTH) * scale.astype(jnp.float32)
    return y.astype(u_ext.dtype)

def prompt_layer(x, c, rel_a, rel_c, lw):
    (norm_g, w_ada, b_ada, w_in, w_out, a_qnorm, a_knorm, cmp_pe, cmp_w1, cmp_b1,
     cmp_w2, cmp_b2, pool_w, pool_scale, c_qnorm, c_knorm) = lw
    P = prepare(x, c, norm_g, w_ada, b_ada, w_in, a_qnorm, a_knorm, c_qnorm, c_knorm)
    B, T = x.shape[:2]
    kc, vc, e_pos, ks_blk, vs_blk = nsa_keyside(P['a_rows'], cmp_pe, cmp_w1, cmp_b1, cmp_w2, cmp_b2, a_knorm[0])
    win_pad = jnp.pad(P['win_rows'], ((0, 0), (WINDOW, 0), (0, 0), (0, 0), (0, 0)))
    c_k, c_v = P['c_rows'][:, :, 0], P['c_rows'][:, :, 1]

    def query_block(b):
        b0 = b * Q_BLOCK
        take = lambda a: lax.dynamic_slice_in_dim(a, b0, Q_BLOCK, axis=1)
        q_pos = b0 + jnp.arange(Q_BLOCK)
        wb = lax.dynamic_slice_in_dim(win_pad, b0, WINDOW + Q_BLOCK, axis=1)
        w_pos = b0 - WINDOW + jnp.arange(WINDOW + Q_BLOCK)
        o_a = nsa_core(take(P['a_q']), take(P['a_gate']), q_pos, kc, vc, e_pos, ks_blk, vs_blk,
                       wb[:, :, 0], wb[:, :, 1], w_pos, rel_a)
        o_c = dsa_core(take(P['c_q']), take(P['c_iq']), take(P['c_iw']), q_pos, c_k, c_v, P['c_kidx'], rel_c)
        return o_a, o_c

    o_a, o_c = lax.map(query_block, jnp.arange(T // Q_BLOCK))
    unblock = lambda o: jnp.swapaxes(o, 0, 1).reshape(B, T, o.shape[-1])
    o_b = pool_mix(jnp.pad(P['b_in'], ((0, 0), (POOL_BUF, 0), (0, 0))), 0, pool_w, pool_scale)
    y = finish(x, P['gate'], unblock(o_a), o_b, unblock(o_c), P['silu'], w_out)
    return y, P['a_rows'], P['c_rows'], P['c_kidx'], P['win_rows'][:, -min(WINDOW, T):], P['b_in'][:, -POOL_BUF:]

def sample_layer(x, c, cache_a, cache_c, cache_ci, win_buf, pool_buf, page_table, rel_a, rel_c, lw):
    (norm_g, w_ada, b_ada, w_in, w_out, a_qnorm, a_knorm, cmp_pe, cmp_w1, cmp_b1,
     cmp_w2, cmp_b2, pool_w, pool_scale, c_qnorm, c_knorm) = lw
    P = prepare(x, c, norm_g, w_ada, b_ada, w_in, a_qnorm, a_knorm, c_qnorm, c_knorm)
    Bd, T = x.shape[:2]
    past = page_table.shape[1] * PAGE_SIZE

    def gather_pages(cache):
        return cache[page_table].reshape((Bd, past) + cache.shape[2:])

    a_all = jnp.concatenate([gather_pages(cache_a), P['a_rows']], axis=1)
    kc, vc, e_pos, ks_blk, vs_blk = nsa_keyside(a_all, cmp_pe, cmp_w1, cmp_b1, cmp_w2, cmp_b2, a_knorm[0])
    w_all = jnp.concatenate([win_buf, P['win_rows']], axis=1)
    n_buf = win_buf.shape[1]
    q_pos = past + jnp.arange(T)
    w_pos = past - n_buf + jnp.arange(n_buf + T)
    o_a = nsa_core(P['a_q'], P['a_gate'], q_pos, kc, vc, e_pos, ks_blk, vs_blk,
                   w_all[:, :, 0], w_all[:, :, 1], w_pos, rel_a)
    c_all = jnp.concatenate([gather_pages(cache_c), P['c_rows']], axis=1)
    ci_all = jnp.concatenate([gather_pages(cache_ci), P['c_kidx']], axis=1)
    o_c = dsa_core(P['c_q'], P['c_iq'], P['c_iw'], q_pos, c_all[:, :, 0], c_all[:, :, 1], ci_all, rel_c)
    u_ext = jnp.concatenate([pool_buf, P['b_in']], axis=1)
    o_b = pool_mix(u_ext, past, pool_w, pool_scale)
    y = finish(x, P['gate'], o_a, o_b, o_c, P['silu'], w_out)
    return y, P['a_rows'], P['c_rows'], P['c_kidx'], w_all[:, -n_buf:], u_ext[:, -POOL_BUF:]

def setup_inputs(seed: int = 0) -> dict:
    key = jax.random.key(seed)
    ks = jax.random.split(key, 32)
    f32 = jnp.float32

    def nrm(k, shape, s=1.0):
        return s * jax.random.normal(k, shape, f32)

    def gain(k, shape):
        return 1.0 + 0.05 * jax.random.normal(k, shape, f32)

    page_table = jax.random.permutation(ks[7], N_POOL_PAGES)[:DEC_BATCH * N_PAGES].reshape(DEC_BATCH, N_PAGES).astype(jnp.int32)
    return {
        'x_prompt': nrm(ks[0], (BATCH, SEQ, D_MODEL)),
        'x_sample': nrm(ks[1], (DEC_BATCH, DEC_SEQ, D_MODEL)),
        'cache_a_kv': nrm(ks[2], (DEPTH, N_POOL_PAGES, PAGE_SIZE, 4, A_KV_HEADS, HEAD_DIM)),
        'cache_c_kv': nrm(ks[3], (DEPTH, N_POOL_PAGES, PAGE_SIZE, 2, HEAD_DIM)),
        'cache_c_kidx': nrm(ks[4], (DEPTH, N_POOL_PAGES, PAGE_SIZE, IDX_DIM)),
        'state_a_win': nrm(ks[5], (DEPTH, DEC_BATCH, WIN_BUF, 2, A_KV_HEADS, HEAD_DIM)),
        'state_b_pool': nrm(ks[6], (DEPTH, DEC_BATCH, POOL_BUF, B_WIDTH)),
        'page_table': page_table,
        'c_prompt': nrm(ks[8], (BATCH, D_MODEL)),
        'c_sample': nrm(ks[9], (DEC_BATCH, D_MODEL)),
        'rel_bias': nrm(ks[10], (N_BUCKETS, BIAS_HEADS), 0.2),
        'norm_g': gain(ks[11], (DEPTH, D_MODEL)),
        'w_ada': nrm(ks[12], (DEPTH, D_MODEL, 3 * D_MODEL), 0.5 * D_MODEL ** -0.5),
        'b_ada': nrm(ks[13], (DEPTH, 3 * D_MODEL), 0.01),
        'w_in': nrm(ks[14], (DEPTH, D_MODEL, N_IN), D_MODEL ** -0.5),
        'w_out': nrm(ks[15], (DEPTH, MIX_WIDTH, D_MODEL), MIX_WIDTH ** -0.5),
        'a_qnorm': gain(ks[16], (DEPTH, HEAD_DIM)),
        'a_knorm': gain(ks[17], (DEPTH, 3, HEAD_DIM)),
        'a_cmp_pe': nrm(ks[18], (DEPTH, 2, CMP_LEN, HEAD_DIM), 0.1),
        'a_cmp_w1': nrm(ks[19], (DEPTH, 2, CMP_LEN * HEAD_DIM, CMP_HIDDEN), (CMP_LEN * HEAD_DIM) ** -0.5),
        'a_cmp_b1': nrm(ks[20], (DEPTH, 2, CMP_HIDDEN), 0.01),
        'a_cmp_w2': nrm(ks[21], (DEPTH, 2, CMP_HIDDEN, HEAD_DIM), CMP_HIDDEN ** -0.5),
        'a_cmp_b2': nrm(ks[22], (DEPTH, 2, HEAD_DIM), 0.01),
        'b_pool_w': nrm(ks[23], (DEPTH, B_GROUPS, B_GROUP_DIM, B_GROUP_DIM), B_GROUP_DIM ** -0.5),
        'b_scale': 1.0 + 0.1 * jax.random.normal(ks[24], (DEPTH, B_WIDTH), f32),
        'c_qnorm': gain(ks[25], (DEPTH, HEAD_DIM)),
        'c_knorm': gain(ks[26], (DEPTH, HEAD_DIM)),
    }

def reference(x_prompt, x_sample, cache_a_kv, cache_c_kv, cache_c_kidx, state_a_win, state_b_pool, page_table,
              c_prompt, c_sample, rel_bias, norm_g, w_ada, b_ada, w_in, w_out, a_qnorm, a_knorm,
              a_cmp_pe, a_cmp_w1, a_cmp_b1, a_cmp_w2, a_cmp_b2, b_pool_w, b_scale, c_qnorm, c_knorm):
    rel_a = rel_bias[:, :A_HEADS]
    rel_c = rel_bias[:, A_HEADS:]
    y_prompt, y_sample = x_prompt, x_sample
    a_kv_p, a_kv_s, c_kv_p, c_kv_s, c_kidx_p, c_kidx_s = [], [], [], [], [], []
    a_win_p, a_win_s, b_pool_p, b_pool_s = [], [], [], []
    for l in range(DEPTH):
        lw = (norm_g[l], w_ada[l], b_ada[l], w_in[l], w_out[l], a_qnorm[l], a_knorm[l],
              a_cmp_pe[l], a_cmp_w1[l], a_cmp_b1[l], a_cmp_w2[l], a_cmp_b2[l],
              b_pool_w[l], b_scale[l], c_qnorm[l], c_knorm[l])
        y_prompt, akv, ckv, cki, awin, bpool = prompt_layer(y_prompt, c_prompt, rel_a, rel_c, lw)
        a_kv_p.append(akv)
        c_kv_p.append(ckv)
        c_kidx_p.append(cki)
        a_win_p.append(awin)
        b_pool_p.append(bpool)
        y_sample, akv, ckv, cki, awin, bpool = sample_layer(
            y_sample, c_sample, cache_a_kv[l], cache_c_kv[l], cache_c_kidx[l], state_a_win[l], state_b_pool[l],
            page_table, rel_a, rel_c, lw)
        a_kv_s.append(akv)
        c_kv_s.append(ckv)
        c_kidx_s.append(cki)
        a_win_s.append(awin)
        b_pool_s.append(bpool)
    return (y_prompt, y_sample,
            jnp.stack(a_kv_p), jnp.stack(a_kv_s),
            jnp.stack(c_kv_p), jnp.stack(c_kv_s),
            jnp.stack(c_kidx_p), jnp.stack(c_kidx_s),
            jnp.stack(a_win_p), jnp.stack(a_win_s),
            jnp.stack(b_pool_p), jnp.stack(b_pool_s))


_drawn_inputs = setup_inputs


def setup_inputs(seed=0):
    import zlib

    import numpy as np

    out = dict(_drawn_inputs(seed))
    spreads = {}
    factors = {'cache_a_kv': 8.0,
     'cache_c_kv': 5.769,
     'cache_c_kidx': 6.023,
     'rel_bias': 8.0,
     'b_ada': 4.309,
     'a_qnorm': 8.0,
     'a_cmp_pe': 8.0,
     'a_cmp_b1': 8.0,
     'a_cmp_b2': 8.0,
     'b_scale': 6.567,
     'c_qnorm': 8.0}
    for name, (base, spread) in spreads.items():
        noise = np.random.default_rng([zlib.crc32(name.encode()), seed]).standard_normal(out[name].shape)
        drawn = base * np.exp(spread * noise) if base else spread * noise
        out[name] = jnp.asarray(drawn.astype(out[name].dtype))
    for name, factor in factors.items():
        out[name] = (out[name] * factor).astype(out[name].dtype)
    return out
```

```python
from contextlib import ExitStack
import math

import numpy as np

import concourse.bass as bass
from concourse import mybir

F32 = mybir.dt.float32
I32 = mybir.dt.int32
ACT = mybir.ActivationFunctionType
ALU = mybir.AluOpType
AX = mybir.AxisListType

P = 128
D = 2048
KD = D // P
T = 512
QT = T // P
DB, DT = 8, 4
TS = DB * DT
TT = T + TS
HALF = TT // 2
PAST, PAGE = 2048, 128
NPG = PAST // PAGE
NPOOL = 5 * DB * NPG // 4
HD = 128
AH, KVH, G = 8, 2, 4
CH = 4
IH, ID = 4, 64
WIN = 512
NB_, MAXD = 32, 128
LS = PAST + TS
NCS = (PAST + DT) // 16 - 1
NCP = T // 16 - 1
NSB = 33
TOPB = 16
KEEP_P, KEEP_S = 128, 256
EPS = 1e-6
NEG = -1e30
FLOOR = -1e29
MARK = -3e38
FORCE = 1e6
SCALE = HD ** -0.5
XOFF = PAST + DT - 1
XL = 2184
TX0 = XOFF - 384 - 127
TXL = 640
SX = 2052

C_AQ, C_AKV, C_GATE, C_ASIL, C_BIN, C_BSIL = 0, 1024, 2560, 2584, 3608, 4120
C_CQ, C_CKV, C_IQ, C_IK, C_IW, C_CSIL = 4632, 5144, 5400, 5656, 5720, 5724
CW = 256

V_BADA, V_G, V_BSC, V_B1, V_B2, V_AQ, V_CQ, V_AK, V_CK = 0, 48, 64, 68, 72, 74, 75, 76, 79
NV = 80
K_ID, K_ONE, K_GRP, K_WM, K_BM, K_WIN, K_DIAG, K_RC, K_M2, K_M3, K_FB = 0, 128, 256, 384, 512, 544, 548, 676, 740, 744, 748
K_EPS = 748 + 33
NK = K_EPS + 1
NSMALL = 24
HREADY = 2 * KD


def bucket(rel):
    rel = np.maximum(rel, 0)
    exact = NB_ // 2
    relf = np.maximum(rel, exact).astype(np.float32)
    lb = exact + (np.log(relf / np.float32(exact)) / np.float32(math.log(MAXD / exact)) * np.float32(NB_ - exact)).astype(np.int32)
    return np.where(rel < exact, rel, np.minimum(lb, NB_ - 1))


def shape_constants():
    c = np.zeros((P, NK), np.float32)
    p = np.arange(P)
    c[:, K_ID:K_ID + P] = np.eye(P)
    c[:, K_ONE:K_ONE + P] = 1.0
    c[:, K_GRP:K_GRP + P] = p[:, None] // 4 == p[None] // 4
    pb, pi, pt = p // 16, p // 4 % 4, p % 4
    qb, qt, qg = p // 16, p // 4 % 4, p % 4
    c[:, K_WM:K_WM + P] = (pb[:, None] == qb[None]) & (pt[:, None] == qt[None])
    k = np.arange(TS)
    c[:, K_BM:K_BM + TS] = np.where((k[None] // DT == qb[:, None]) & (k[None] % DT <= qt[:, None]), 0.0, NEG)
    c[:, K_WIN:K_WIN + 4] = np.where(np.arange(4)[None] < qt[:, None], NEG, 0.0)
    c[:, K_DIAG:K_DIAG + P] = np.where(p[None] <= p[:, None], 0.0, NEG)
    for g in range(4):
        c[:, K_RC + 16 * g:K_RC + 16 * g + 16] = 1.0 / np.minimum(np.arange(16) + 1, 2 << g)
    c[:, K_M2:K_M2 + 4] = np.arange(4)[None] == pi[:, None]
    c[:, K_M3:K_M3 + 4] = np.arange(4)[None] == qg[:, None]
    c[:, K_EPS] = EPS
    c[:, [K_FB, K_FB + 31, K_FB + 32]] = FORCE
    e = np.zeros((TS, 2 * P), np.float32)
    kb, kt = k // DT, k % DT
    e[:, :P] = (kb[:, None] == qb[None]) & (kt[:, None] == qt[None])
    e[:, P:] = (kb[:, None] == pb[None]) & (kt[:, None] == pt[None])
    rel = XOFF - np.arange(XL)
    oh = np.zeros((NB_ + 1, XL), np.float32)
    oh[bucket(rel), np.arange(XL)] = (rel >= 0)
    oh[NB_] = np.where(rel < 0, NEG, 0.0)
    return {"constants": c, "expanders": e, "bucket_rows": oh}


def plan_projection():
    chunks, jobs = [], []

    def rows(kind, parts):
        chunks.append(parts)
        jobs.extend((kind, 0, t, len(chunks) - 1) for t in range(QT + 1))

    def cols(kind, first, blocks):
        for b in range(0, blocks, 2):
            chunks.append([(first + b * P, CW)])
            jobs.extend((kind, b + j, j, len(chunks) - 1) for j in range(2))

    rows("small", [(C_GATE, 24), (C_IK, ID + IH)])
    cols("iq", C_IQ, 2)
    rows("ckv", [(C_CKV, CW)])
    for n, kind in enumerate(("kcmp", "vcmp", "kslc", "vslc", "kwin", "vwin")):
        rows(kind, [(C_AKV + n * CW, CW)])
    cols("cq", C_CQ, CH)
    cols("aq", C_AQ, AH)
    cols("bin", C_BIN, 4)
    cols("bsil", C_BSIL, 4)
    cols("asil", C_ASIL, AH)
    cols("csil", C_CSIL, 4)
    return chunks, jobs


ROW_KINDS = ("small", "ckv", "kcmp", "vcmp", "kslc", "vslc", "kwin", "vwin")
SIL_AT = {"asil": 0, "bsil": 8, "csil": 12}


class Count:

    def __init__(self, eng, sem):
        self.eng, self.sem, self.n = eng, sem, 0

    def __call__(self, ins):
        ins.then_inc(self.sem, 1)
        self.n += 1
        return self.n

    def wait(self):
        self.eng.wait_ge(self.sem, self.n)

    def link(self, ins):
        self(ins)
        self.wait()


def build(nc, I, O, debug=None):
    chunks, jobs = plan_projection()
    njobs = len(jobs)
    with ExitStack() as ctx:
        sems = {}

        def sem(name):
            sems[name] = ctx.enter_context(nc.semaphore(name))
            return sems[name]

        top = [16512]
        hi = [top[0]]

        def sb(name, rows, words, dt=F32, at=None):
            where = top[0] if at is None else at
            words_r = -(-words // 8) * 8
            t = nc.alloc_sbuf_tensor_at(name, [rows, words], dt, offset=where)
            if at is None:
                top[0] += 4 * words_r
                assert top[0] <= 229344, (name, top[0])
            return t

        def region(start):
            pos = [start]

            def place(name, rows, words, dt=F32):
                t = sb(name, rows, words, dt, at=pos[0])
                pos[0] += 4 * (-(-words // 8) * 8)
                assert pos[0] <= 229344, (name, pos[0])
                return t
            return place, pos

        con = sb("con", P, NK)
        expd = sb("expd", TS, 2 * P)
        vecT = sb("vecT", P, NV)
        peT = sb("peT", P, 64)
        modT = sb("modT", P, 48 * 9)
        ascale = sb("ascale", P, KD * 9)
        gk = sb("gk", P, 4 * P)
        relb = sb("relb", NB_ + 1, 12)
        gateP = sb("gateP", P, QT * 24)
        gateS0 = sb("gateS0", TS, 24)
        gateS = sb("gateS", P, 6)
        gateS1 = sb("gateS1", P, 24)
        iwP = sb("iwP", P, QT * 4)
        iwS = sb("iwS", TS, 4)
        wiS = sb("wiS", P, 4)
        zq = sb("zq", P, 3 * DB * 32)
        qf = sb("qf", P, 3 * P)
        zi = sb("zi", ID, DB * 32)
        qfi = sb("qfi", ID, P)
        ksN = sb("ksN", P, 5 * TS)
        kiN = sb("kiN", P, TS)
        vN = sb("vN", TS, 2 * CW)
        cvN = sb("cvN", TS, P)
        wsel = sb("wsel", P, P)
        maskC = sb("maskC", P, 256 + 384 + 512)
        wpool = sb("wpool", P, 4 * P)
        ptab = sb("ptab", 1, DB * NPG, I32)
        st = sb("st", P, 64)
        b1e = sb("b1e", P, 4)
        mix = sb("mix", P, KD * TT)
        base_free = top[0]

        data, dpos = region(base_free)
        aqT = data("aqT", P, AH * T)
        cqT = data("cqT", P, CH * T)
        kslcT = data("kslcT", P, KVH * T)
        kwinT = data("kwinT", P, KVH * T)
        ckT = data("ckT", P, T)
        vnat = data("vnat", P, QT * 2 * CW)
        cvnat = data("cvnat", P, QT * P)
        kcP = data("kcP", P, KVH * 32)
        vcP = data("vcP", 32, KVH * P)
        cmpT = data("cmpT", P, 2 * KVH * T)
        xrow = [sb(f"xrow{i}", P, D, at=base_free + i * 4 * D) for i in range(2)]
        crow = sb("crow", 9, D, at=base_free + 2 * 4 * D)
        vrow = sb("vrow", NV, P, at=base_free + 3 * 4 * D)
        prow = sb("prow", 64, P, at=base_free + 3 * 4 * D + 4 * P)
        cT = sb("cT", P, KD * 9 * 2, at=base_free + 3 * 4 * D + 8 * P)
        btmp = sb("btmp", 12, XL, at=base_free + 3 * 4 * D + 8 * P + 1280)
        ohr = sb("ohr", NB_ + 1, XL, at=base_free + 3 * 4 * D + 8 * P + 1280 + 4 * XL)
        bst = sb("bst", DB * 15, 512, at=base_free + 3 * 4 * D + 8 * P + 1280 + 8 * XL)
        assert 2048 + 3 * 4 * D + 8 * P + 1280 + 8 * XL <= dpos[0] - base_free

        big0 = dpos[0]
        big, bpos = region(big0)
        hT = big("hT", P, KD * TT)
        wbuf = [big(f"wbuf{i}", P, KD * CW) for i in range(2)]
        big_end = bpos[0]
        ext, epos = region(big_end)
        iqh = ext("iqh", ID, 2 * TS)
        iqT = ext("iqT", P, 2 * TT)
        ikT = ext("ikT", P, T)
        bT = ext("bT", P, 4 * (16 + T))
        bS = ext("bS", P, 4 * DB * 20)
        stage = [ext(f"stage{i}", P, CW) for i in range(4)]
        sq = ext("sq", P, TT)
        rs = ext("rs", P, TT)
        wk = ext("wk", P, T)
        w1p, _ = region(big0)
        w1P = [w1p(f"w1P{i}", P, 32 * 256) for i in range(2)]
        w2p, _ = region(big_end)
        w2P = w2p("w2P", P, 2 * 2 * P)
        hidP = w2p("hidP", P, 4 * 64)
        cxP = w2p("cxP", P, 3 * 64)
        att, apos = region(big0)
        bias = att("bias", P, 12 * T)
        SP_ = [att(f"SP{i}", P, 1056) for i in range(3)]
        PTP = [att(f"PTP{i}", P, 1152) for i in range(2)]
        as_ = att("as_", P, 64)
        smp, spos = region(base_free)
        kc = smp("kc", P, DB * KVH * P)
        vc = smp("vc", P, DB * KVH * P)
        wrk = smp("wrk", P, LS)
        s2 = spos[0]
        cm, _ = region(s2)
        w1S = [cm(f"w1S{i}", P, 32 * 256) for i in range(2)]
        xt = [cm(f"xt{i}", P, 2 * PAST) for i in range(2)]
        xnat = [cm(f"xnat{i}", P, 4 * 256) for i in range(4)]
        hid = [cm(f"hid{i}", P, 2 * 256) for i in range(1)]
        w2S = cm("w2S", P, 2 * 2 * P)
        cx = cm("cx", P, 2 * 256)
        ix, _ = region(s2)
        ixn = [ix(f"ixn{i}", P, 4 * ID) for i in range(8)]
        ixT = [ix(f"ixT{i}", ID, 512) for i in range(4)]
        ixr = ix("ixr", P, LS)
        at_, tpos = region(s2)
        sbias = [at_(f"sbias{i}", P, SX) for i in range(3)]
        nbias = at_("nbias", P, 3 * TS)
        kn = [at_(f"kn{i}", P, 512) for i in range(8)]
        kT = [at_(f"kT{i}", P, 512) for i in range(4)]
        vr = [at_(f"vr{i}", P, NPG * P) for i in range(4)]
        sS = at_("sS", P, LS)
        sW = at_("sW", P, WIN + TS)
        sC = at_("sC", P, P)
        pT = at_("pT", P, 23 * P)
        imp = at_("imp", P, 5 * 40)
        bmask = at_("bmask", P, 2 * NSB)
        us = at_("us", P, 64)
        ou, _ = region(base_free)
        wo = [ou(f"wo{i}", P, KD * CW) for i in range(3)]
        yT = [ou(f"yT{i}", P, TT) for i in range(4)]
        xres = ou("xres", P, 5 * D)
        yrow = [ou(f"yrow{i}", P, 5 * CW) for i in range(2)]
        tmp, _ = region(big0)
        pls = tmp("pls", P, 1400)
        prw = tmp("prw", TS, 1024)

        ident = con[:, K_ID:K_ID + P]
        ones = con[:, K_ONE:K_ONE + P]

        bank = [ctx.enter_context(nc.psum_tensor(f"bank{i}", [P, 512], F32)) for i in range(8)]

        d_rows = nc.dram_tensor("bias_rows", (12, XL), F32).ap()
        d_rep = nc.dram_tensor("bias_repeated", (P, 12 * TXL), F32).ap()
        d_smp = nc.dram_tensor("bias_sample", (3, 16, SX), F32).ap()

        s_con = sem("s_con")
        s_x = [sem(f"s_x{i}") for i in range(2)]
        x_free = sem("x_free")
        dve = sem("dve")
        act_ = sem("act_")
        ph_pe, ph_act, ph_dve, ph_pool = (sem(n) for n in ("ph_pe", "ph_act", "ph_dve", "ph_pool"))
        ixp_d, ixp_r, ixp_a, r_std, g_e, gs_in, iqh_in, pl_y2, pst_t, pst_ev, un_w, h_copied = (
            sem(n) for n in ("ixp_d", "ixp_r", "ixp_a", "r_std", "g_e", "gs_in", "iqh_in", "pl_y2", "pst_t", "pst_ev", "un_w", "h_copied"))
        su_tr = sem("su_tr")
        su_ev = sem("su_ev")
        c_T = sem("c_T")
        c_e = sem("c_e")
        c_s = sem("c_s")
        b_ps = sem("b_ps")
        b_ev = sem("b_ev")
        b_dma = sem("b_dma")
        x_ss = sem("x_ss")
        x_std = sem("x_std")
        x_n = sem("x_n")
        x_tr = sem("x_tr")
        x_ev = sem("x_ev")
        w_in_ = [sem(f"w_in{i}") for i in range(2)]
        w_free = sem("w_free")
        ada_ps = sem("ada_ps")
        h_ready = sem("h_ready")
        m_done = sem("m_done")
        m_free = sem("m_free")
        n_sq = sem("n_sq")
        n_sum = sem("n_sum")
        n_std = sem("n_std")
        st_rdy = sem("st_rdy")
        a_done = sem("a_done")
        a_free = sem("a_free")
        st_out = [sem(f"st_out{i}") for i in range(4)]
        sil_e = sem("sil_e")
        d_out = sem("d_out")
        o_rdy = sem("o_rdy")
        ix_ps = sem("ix_ps")
        ix_rl = sem("ix_rl")
        ix_us = sem("ix_us")
        pl_d = sem("pl_d")
        pl_y = sem("pl_y")
        pl_t = sem("pl_t")
        pl_c = sem("pl_c")
        w1_in = sem("w1_in")
        cp_ps = sem("cp_ps")
        cp_ev = sem("cp_ev")
        at_in = sem("at_in")
        q_ps = sem("q_ps")
        q_s = sem("q_s")
        q_e = sem("q_e")
        q_p = sem("q_p")
        q_t = sem("q_t")
        q_ta = sem("q_ta")
        q_td = sem("q_td")
        q_o = sem("q_o")
        q_m = sem("q_m")
        si_ps = sem("si_ps")
        si_ev = sem("si_ev")
        kb_in = [sem(f"kb_in{i}") for i in range(8)]
        kb_tr = sem("kb_tr")
        kb_a = sem("kb_a")
        kb_d = sem("kb_d")
        kb_mm = sem("kb_mm")
        xn_in = [sem(f"xn_in{i}") for i in range(4)]
        xn_tr = sem("xn_tr")
        xt_a = sem("xt_a")
        xt_d = sem("xt_d")
        hd_ps = sem("hd_ps")
        hd_ev = sem("hd_ev")
        kc_ps = sem("kc_ps")
        kc_x = sem("kc_x")
        kc_sum = sem("kc_sum")
        kc_std = sem("kc_std")
        kc_ok = sem("kc_ok")
        w1s_in = sem("w1s_in")
        sb_in = sem("sb_in")
        vr_in = [sem(f"vr_in{i}") for i in range(4)]
        pv_b = sem("pv_b")
        un_ps = sem("un_ps")
        un_s = sem("un_s")
        un_m = sem("un_m")
        un_e = sem("un_e")
        un_p = sem("un_p")
        un_t = sem("un_t")
        un_te = sem("un_te")
        un_o = sem("un_o")
        un_x = sem("un_x")
        im_ps = sem("im_ps")
        im_in = sem("im_in")
        im_bc = sem("im_bc")
        wo_in = [sem(f"wo_in{i}") for i in range(3)]
        xr_in = sem("xr_in")
        y_ps = sem("y_ps")
        y_ev = sem("y_ev")
        y_tr = sem("y_tr")
        y_fin = sem("y_fin")
        y_out = sem("y_out")
        block = ctx.enter_context(nc.Block())

        def v3(tensor, pattern, /, **k):
            return tensor[:, :].rearrange(pattern, **k)

        hT3 = v3(hT, "p (k t) -> p k t", t=TT)
        mix3 = v3(mix, "p (k t) -> p k t", t=TT)
        mod3 = v3(modT, "p (n b) -> p n b", b=9)
        asc3 = v3(ascale, "p (n b) -> p n b", b=9)
        aqT3 = v3(aqT, "p (h t) -> p h t", t=T)
        cqT3 = v3(cqT, "p (h t) -> p h t", t=T)
        iqT3 = v3(iqT, "p (h t) -> p h t", t=TT)
        bT3 = v3(bT, "p (g t) -> p g t", t=16 + T)
        bS4 = v3(bS, "p (g b t) -> p g b t", g=4, t=20)
        cmp4 = v3(cmpT, "p (c h t) -> p c h t", c=2, h=KVH)
        vnat3 = v3(vnat, "p (i c) -> p i c", c=2 * CW)
        zq4 = v3(zq, "p (u b r) -> p u b r", u=3, b=DB)
        qf3 = v3(qf, "p (u r) -> p u r", u=3)
        MOFF = (0, 0, 256, 640)

        idx_of = {}
        for j, (kind, b, t, c) in enumerate(jobs):
            idx_of[(kind, b, t)] = j
        normT = [j for j, (k, b, t, c) in enumerate(jobs) if k in ("cq", "aq")]
        staged = [j for j, (k, b, t, c) in enumerate(jobs) if k in ("small", "ckv", "kcmp", "vcmp", "kslc", "kwin")]
        turned = [j for j in staged if not (jobs[j][0] in ("kcmp", "vcmp") and jobs[j][2] == QT)]
        silj = [j for j, (k, b, t, c) in enumerate(jobs) if k in SIL_AT]
        rownorm = [j for j, (k, b, t, c) in enumerate(jobs) if k in ("ckv", "kslc", "kwin")]

        def turns(j):
            return 2 if jobs[j][0] in ("kcmp", "vcmp", "kslc", "kwin") else 1

        def width(t):
            return P if t < QT else TS

        def wchunk(c, w):
            return wbuf[c % 2][:, 0:KD * w].rearrange("p (k n) -> p k n", n=w)

        cwidth = [sum(w for _, w in parts) for parts in chunks]
        cparts = [len(parts) for parts in chunks]
        NADA = 3 * D // CW
        need, count = {}, [0, 0]
        for n in range(NADA + len(chunks)):
            parts = 1 if n < NADA else cparts[n - NADA]
            count[n % 2] += 16 * parts
            need[n] = count[n % 2]

        def w_of(n):
            return need[NADA + n] if n >= 0 else None


        turned_set, staged_set = set(turned), set(staged)
        last_job = {c: j for j, (_, _, _, c) in enumerate(jobs)}
        ix_slot, n_ = {}, 0
        for i in range(1, QT):
            for x in range(4):
                ix_slot[idx_of[("kcmp", 0, 0)] + 8 * (i - 1) + x] = ("dots", i, x, n_)
                ix_slot[idx_of[("kcmp", 0, 0)] + 8 * (i - 1) + 4 + x] = ("topk", i, x)
                n_ += 1
        units = [("A", i, h) for i in range(QT) for h in range(AH)] + [("C", i, h) for i in range(QT) for h in range(CH)]
        NUA = QT * AH
        sblocks = []
        for u in range(3):
            if u < 2:
                sblocks += [(u, "win", b, 0) for b in range(DB)]
            sblocks += [(u, "slc", b, q) for b in range(DB) for q in range(4)]
        kneed, kc_ = [], [0] * 8
        for m in range(32 + len(sblocks)):
            kc_[m % 8] += 16 if m >= 32 and sblocks[m - 32][1] == "win" else 64
            kneed.append(kc_[m % 8])
        vneed, vc_ = [], [0] * 4
        for m, k_ in enumerate(([64] * 2 + [256] * 8) * 2 + [256] * 8):
            vc_[m % 4] += k_
            vneed.append(vc_[m % 4])

        def pgroups(u):
            t = [(sS[:, i * P:(i + 1) * P], P) for i in range(16)] + [(sS[:, PAST:LS], TS)]
            if u < 2:
                t += [(sW[:, i * P:(i + 1) * P], P) for i in range(4)] + [(sW[:, WIN:WIN + TS], TS), (sC[:, 0:NCS], NCS)]
            return [t[i:i + 4] for i in range(0, len(t), 4)]

        kb_gt, g_ = list(range(32)), 32
        for u in range(3):
            nb_ = 40 if u < 2 else 32
            kb_gt += range(g_, g_ + nb_)
            g_ += nb_ + (6 if u < 2 else 5)

        def bc(ap, n):
            return ap.unsqueeze(2).broadcast_to([ap.shape[0], ap.shape[1], n])

        def after(eng, n):
            eng.wait_ge(ph_pe, n)
            eng.wait_ge(ph_act, n)
            eng.wait_ge(ph_dve, n)
            if n == 1:
                eng.wait_ge(ph_pool, 1)

        def turned_to(kind, t, x):
            a, w = t * P, width(t)
            if kind == "small":
                return ikT[:, a:a + P] if t < QT else kiN[:, :]
            if kind == "ckv":
                return ckT[:, a:a + P] if t < QT else ksN[:, 4 * TS:5 * TS]
            if kind in ("kcmp", "vcmp"):
                return cmp4[:, 0 if kind == "kcmp" else 1, x, a:a + P]
            o = 0 if kind == "kslc" else 2
            return (kslcT, kwinT)[o // 2][:, x * T + a:x * T + a + P] if t < QT else ksN[:, (o + x) * TS:(o + x + 1) * TS]

        def evac_x(eng, A, t):
            w = width(t)
            for q in range(4):
                g = 4 * t + q
                eng.wait_ge(x_tr, g + 1)
                eng.copy(hT3[:, 4 * q:4 * q + 4, t * P:t * P + w], bank[g % 4][:, 0:4 * w].rearrange("p (k t) -> p k t", k=4)).then_inc(x_ev, 1)

        def take_rows(eng, copy, x, s):
            n, q, h = x // 8, x % 8 // 2, x % 2
            eng.wait_ge(xn_tr, x + 1)
            if n >= 2:
                eng.wait_ge(hd_ps, n - 1)
            o = v3(xt[n % 2], "p (h s c) -> p h c s", h=2, s=16)[:, h, 32 * q:32 * q + 32, :]
            copy(o, bank[4 + x % 2][:, :].rearrange("p (c s) -> p c s", s=16)).then_inc(s, 1)

        def take_p(eng, copy, u, gi, src, s):
            if u >= 1:
                eng.wait_ge(pv_b, (10, 20)[u - 1])
            b, i = bank[5 + (s is kb_d)], 0
            while i < len(src):
                j = i
                while j < len(src) and src[j][1] == src[i][1]:
                    j += 1
                r = src[i][1]
                last = copy(pT[0:r, (4 * gi + i) * P:(4 * gi + j) * P], b[0:r, i * P:j * P])
                i = j
            last.then_inc(s, 1)

        def unit_exps(eng, A, u, when):
            if when == "early":
                eng.wait_ge(un_w, u + 1)
                A(sC[:, 0:NCS], sC[:, 0:NCS], ACT.Exp, bias=us[:, 4:5], accum_out=us[:, 8:9])
                A(sW[:, :], sW[:, :], ACT.Exp, bias=us[:, 5:6], accum_out=us[:, 9:10]).then_inc(un_e, 1)
            else:
                eng.wait_ge(un_s, u + 1)
                A(sS[:, :], sS[:, :], ACT.Exp, bias=us[:, 6:7], accum_out=us[:, 10:11]).then_inc(un_e, 1)

        def early(v, V, u, link, ttr):
            v.wait_ge(un_ps, 2 * u + 1)
            link(V.tensor_tensor(sW[:, 0:WIN], bank[0][:, :], sbias[u][:, PAST - WIN:PAST], ALU.add))
            link(V.tensor_tensor(sW[:, WIN:WIN + TS], bank[4][:, 32:64], nbias[:, u * TS:(u + 1) * TS], ALU.add))
            link(V.tensor_tensor(sW[:, 0:4], sW[:, 0:4], con[:, K_WIN:K_WIN + 4], ALU.add))
            link(ttr(sC[:, 0:NCS], bank[4][:, 64:64 + NCS], sbias[u][:, 31:31 + 16 * (NCS - 1) + 1:16], us[:, 0:1]))
            link(V.tensor_reduce(us[:, 1:2], sW[:, :], AX.X, ALU.max))
            V.tensor_scalar(us[:, 4:6], us[:, 0:2], -1.0, None, ALU.mult).then_inc(un_w, 1)

        def mid(v, V, u, link):
            v.wait_ge(un_e, 2 * u + 1)
            link(V.tensor_scalar(us[:, 12:14], us[:, 8:10], 1e-30, None, ALU.max))
            link(V.reciprocal(us[:, 12:14], us[:, 12:14]))
            V.tensor_scalar(sC[:, 0:NCS], sC[:, 0:NCS], us[:, 12:13], None, ALU.mult).then_inc(im_in, 1)
            v.wait_ge(im_in, u + 1)

        def late(v, V, u, link, ttr):
            if u < 2:
                v.wait_ge(im_ps, u + 1)
                link(V.memset(imp[:, :], 0.0))
                link(V.tensor_copy(imp[:, 1:1 + NCS], bank[7][:, 0:NCS]))
                at = [imp[:, k:k + 4 * (NSB - 1) + 1:4] for k in range(5)]
                t = imp[:, 136:136 + NSB]
                link(V.tensor_tensor(t, at[1], at[2], ALU.add))
                link(V.tensor_tensor(t, t, at[3], ALU.add))
                link(V.scalar_tensor_tensor(out=t, in0=t, scalar=2.0, in1=at[0], op0=ALU.mult, op1=ALU.add))
                link(V.tensor_tensor(t, t, at[4], ALU.add))
                link(V.tensor_tensor(t, t, con[:, K_FB:K_FB + NSB], ALU.max))
                for _ in range(TOPB // 8):
                    link(V.max(us[:, 24:32], t))
                    link(V.match_replace(t, us[:, 24:32], t, MARK))
                link(V.tensor_scalar(bmask[:, 0:NSB], t, MARK, NEG, ALU.not_equal, ALU.mult))
                link(V.tensor_scalar(sC[:, 0:NCS], sC[:, 0:NCS], gateS[:, u:u + 1], None, ALU.mult))
                link(V.tensor_scalar(sW[:, :], sW[:, :], us[:, 13:14], gateS[:, 4 + u:5 + u], ALU.mult, ALU.mult))
            v.wait_ge(un_ps, 2 * u + 2 if u < 2 else 5)
            for f in range(4):
                V.tensor_tensor(sS[:, 512 * f:512 * f + 512], bank[f][:, :], sbias[u][:, 512 * f:512 * f + 512], ALU.add)
            link(V.tensor_tensor(sS[:, PAST:LS], bank[4][:, 0:TS], nbias[:, u * TS:(u + 1) * TS], ALU.add))
            if u < 2:
                s3 = sS[:, 0:PAST].rearrange("p (n s) -> p n s", s=64)
                link(V.tensor_tensor(s3, s3, bc(bmask[:, 0:32], 64), ALU.add))
                link(V.tensor_reduce(us[:, 2:3], sS[:, :], AX.X, ALU.max))
            else:
                link(ttr(sS[:, :], sS[:, :], wrk[:, :], us[:, 2:3]))
            V.tensor_scalar(us[:, 6:7], us[:, 2:3], -1.0, None, ALU.mult).then_inc(un_s, 1)
            v.wait_ge(un_e, 2 * u + 2 if u < 2 else 5)
            link(V.tensor_scalar(us[:, 14:15], us[:, 10:11], 1e-30, None, ALU.max))
            link(V.reciprocal(us[:, 14:15], us[:, 14:15]))
            if u < 2:
                link(V.tensor_scalar(us[:, 14:15], us[:, 14:15], gateS[:, 2 + u:3 + u], None, ALU.mult))
            V.tensor_scalar(sS[:, :], sS[:, :], us[:, 14:15], None, ALU.mult).then_inc(un_p, 1)

        def pool_out(v, V, g):
            v.wait_ge(pl_y, g + 1)
            for f in range(2):
                m = mix3[:, 8 + g, f * HALF:(f + 1) * HALF]
                last = V.scalar_tensor_tensor(out=m, in0=bank[2 * (g % 2) + f][:, 0:HALF], scalar=vecT[:, V_BSC + g:V_BSC + g + 1], in1=m, op0=ALU.mult, op1=ALU.mult)
            last.then_inc(pl_y2, 1)

        @block.sync
        def _(sp):
            small = [(con[:, :], I["constants"]), (expd[:, :], I["expanders"]), (ohr[:, :], I["bucket_rows"]),
                     (vrow[V_BADA:V_BADA + 48, :], I["b_ada"].rearrange("a (n p) -> (a n) p", p=P)),
                     (vrow[V_G:V_G + 16, :], I["norm_g"].rearrange("a (n p) -> (a n) p", p=P)),
                     (vrow[V_BSC:V_BSC + 4, :], I["b_scale"].rearrange("a (n p) -> (a n) p", p=P)),
                     (vrow[V_B1:V_B1 + 4, :], I["a_cmp_b1"].rearrange("a c (n p) -> (a c n) p", p=P)),
                     (vrow[V_B2:V_B2 + 2, :], I["a_cmp_b2"].rearrange("a c p -> (a c) p")),
                     (vrow[V_AQ:V_AQ + 1, :], I["a_qnorm"]), (vrow[V_CQ:V_CQ + 1, :], I["c_qnorm"]),
                     (vrow[V_AK:V_AK + 3, :], I["a_knorm"].rearrange("a c p -> (a c) p")),
                     (vrow[V_CK:V_CK + 1, :], I["c_knorm"]),
                     (prow[:, :], I["a_cmp_pe"].rearrange("a c s p -> (a c s) p")),
                     (crow[0:1, :], I["c_prompt"]), (crow[1:9, :], I["c_sample"]),
                     (relb[0:NB_, :], I["rel_bias"]), (relb[NB_:NB_ + 1, :], I["constants"][0:1, K_ONE:K_ONE + 12]),
                     (ptab[:, :], I["page_table"].rearrange("(a b) n -> a (b n)", a=1)),
                     (bst[:, :], I["state_b_pool"].rearrange("a b t c -> (a b t) c")),
                     (v3(wpool, "p (g d) -> p g d", g=4), I["b_pool_w"][0].rearrange("g c d -> c g d"))]
            for n, (o, i) in enumerate(small):
                sp.dma_start(o, i).then_inc(s_con, 16)
            for n, src in enumerate((I["a_knorm"][0, 1:2, :], I["a_knorm"][0, 2:3, :], I["c_knorm"], I["a_cmp_b2"][0, 1:2, :])):
                sp.dma_start(gk[:, n * P:(n + 1) * P], bass.AP(src.tensor, src.offset, [[0, P], [1, P]])).then_inc(s_con, 16)
            xp = I["x_prompt"].rearrange("a (t p) d -> (a t) p d", p=P)
            for t in range(2):
                sp.dma_start(xrow[t][:, :], xp[t]).then_inc(s_x[t], 16)

            wada = I["w_ada"][0].rearrange("(k p) n -> p k n", p=P)
            win = I["w_in"][0].rearrange("(k p) n -> p k n", p=P)
            for n in range(NADA + len(chunks)):
                if 2 <= n < NADA + 2:
                    sp.wait_ge(w_free, n - 1)
                elif n >= 2:
                    sp.wait_ge(m_done, last_job[n - 2 - NADA] + 1)
                if n < NADA:
                    sp.dma_start(v3(wbuf[n % 2], "p (k n) -> p k n", n=CW), wada[:, :, n * CW:(n + 1) * CW]).then_inc(w_in_[n % 2], 16)
                    if n == 1:
                        for t in range(2, QT + 1):
                            sp.wait_ge(x_tr, 4 * (t - 1))
                            if t < QT:
                                sp.dma_start(xrow[t % 2][:, :], xp[t]).then_inc(s_x[t % 2], 16)
                            else:
                                sp.dma_start(xrow[t % 2][0:TS, :], I["x_sample"].rearrange("b t d -> (b t) d")).then_inc(s_x[t % 2], 16)
                else:
                    c = n - NADA
                    off = 0
                    for col, w in chunks[c]:
                        sp.dma_start(wchunk(n, cwidth[c])[:, :, off:off + w], win[:, :, col:col + w]).then_inc(w_in_[n % 2], 16)
                        off += w

            after(sp, 1)
            for kv in range(2):
                sp.dma_start(v3(w1P[kv], "p (s h) -> p s h", h=256), I["a_cmp_w1"][0, kv].rearrange("(s p) h -> p s h", p=P)).then_inc(w1_in, 16)
                sp.dma_start(w2P[:, kv * 256:kv * 256 + 256].rearrange("p (n d) -> p n d", n=2), I["a_cmp_w2"][0, kv].rearrange("(n p) d -> p n d", p=P)).then_inc(w1_in, 16)
            after(sp, 2)
            sp.wait_ge(b_dma, 32 + 64)
            sp.dma_start(v3(bias, "p (h j) -> p h j", h=12), bass.AP(d_rep.tensor, d_rep.offset + 127, [[12 * TXL - 1, P], [TXL, 12], [1, T]])).then_inc(at_in, 16)

            after(sp, 3)

            def page(n):
                return sp.value_load(ptab[0:1, n:n + 1], min_val=0, max_val=NPOOL - 1)

            cki = I["cache_c_kidx"].rearrange("l n p c -> (l n) p c")
            cc = I["cache_c_kv"].rearrange("l n p a c -> (l n) p a c")
            ca = I["cache_a_kv"].rearrange("l n p a h c -> (l n) p a h c")
            for n in range(32):
                if n >= 8:
                    sp.wait_ge(kb_tr, n - 7)
                for q in range(4):
                    r = page(4 * n + q)
                    sp.dma_start(ixn[n % 8][:, q * ID:(q + 1) * ID], cki[bass.ds(r, 1), :, :].rearrange("a p c -> (a p) c")).then_inc(kb_in[n % 8], 16)
            after(sp, 4)
            for kv in range(2):
                if kv == 0:
                    for n in range(2):
                        sp.dma_start(w2S[:, n * 256:n * 256 + 256].rearrange("p (n d) -> p n d", n=2), I["a_cmp_w2"][0, n].rearrange("(n p) d -> p n d", p=P)).then_inc(w1s_in, 16)
                        sp.dma_start(v3(w1S[n], "p (s h) -> p s h", h=256), I["a_cmp_w1"][0, n].rearrange("(s p) h -> p s h", p=P)).then_inc(w1s_in, 16)
                for b in range(DB):
                    for q in range(4):
                        n = (kv * DB + b) * 4 + q
                        if n >= 4:
                            sp.wait_ge(xn_tr, 2 * (n - 3))
                        for i in range(4):
                            r = page(b * NPG + 4 * q + i)
                            sp.dma_start(xnat[n % 4][:, i * 256:(i + 1) * 256].rearrange("p (h c) -> p h c", h=2), ca[bass.ds(r, 1), :, kv, :, :].rearrange("a p h c -> (a p) h c")).then_inc(xn_in[n % 4], 16)
            after(sp, 5)
            sp.wait_ge(b_dma, 32 + 64)
            for u in range(3):
                for b in range(DB):
                    sp.dma_start(sbias[u][16 * b:16 * b + 16, :], d_smp[u]).then_inc(sb_in, 16)
            sw = I["state_a_win"][0]
            n = 0
            vn = 0

            def vload(u, b):
                nonlocal vn
                if vn >= 4:
                    sp.wait_ge(pv_b, vn - 3)
                for i in range(NPG):
                    r = page(b * NPG + i)
                    if u < 2:
                        src = ca[bass.ds(r, 1), :, 3, u, :]
                    else:
                        src = cc[bass.ds(r, 1), :, 1, :]
                    sp.dma_start(vr[vn % 4][:, i * P:(i + 1) * P], src.rearrange("a p c -> (a p) c")).then_inc(vr_in[vn % 4], 16)
                vn += 1

            def wvload(k, half):
                nonlocal vn
                if vn >= 4:
                    sp.wait_ge(pv_b, vn - 3)
                for j in range(4):
                    b = 4 * half + j
                    sp.dma_start(vr[vn % 4][:, j * 512:(j + 1) * 512].rearrange("p (i c) -> p i c", c=P), sw[b, :, 1, k, :].rearrange("(i p) c -> p i c", p=P)).then_inc(vr_in[vn % 4], 16)
                vn += 1

            def kblock(src4, parts):
                nonlocal n
                m = 32 + n
                if n >= 8:
                    sp.wait_ge(kb_tr, kb_gt[m - 8] + 1)
                for (o, s) in src4:
                    sp.dma_start(o, s()).then_inc(kb_in[n % 8], 16)
                n += 1

            for u in range(3):
                if u < 2:
                    for b in range(DB):
                        kblock([(v3(kn[n % 8], "p (i c) -> p i c", c=P), lambda b=b, u=u: sw[b, :, 0, u, :].rearrange("(i p) c -> p i c", p=P))], 1)
                for b in range(DB):
                    for q in range(4):
                        def src(i, b=b, q=q, u=u):
                            r = page(b * NPG + 4 * q + i)
                            s = ca[bass.ds(r, 1), :, 2, u, :] if u < 2 else cc[bass.ds(r, 1), :, 0, :]
                            return s.rearrange("a p c -> (a p) c")
                        kblock([(kn[n % 8][:, i * P:(i + 1) * P], (lambda i=i, f=src: f(i))) for i in range(4)], 4)
                if u < 2:
                    for half in range(2):
                        wvload(u, half)
                for b in range(DB):
                    vload(u, b)
            after(sp, 6)
            sp.dma_start(v3(xres, "p (i d) -> p i d", i=5)[:, 0:QT, :], I["x_prompt"][0].rearrange("(i p) d -> p i d", p=P)).then_inc(xr_in, 16)
            sp.dma_start(v3(xres, "p (i d) -> p i d", i=5)[0:TS, QT, :], I["x_sample"].rearrange("b t d -> (b t) d")).then_inc(xr_in, 16)
            wout = I["w_out"][0].rearrange("(k p) n -> p k n", p=P)
            for c in range(D // CW):
                if c >= 3:
                    sp.wait_ge(y_ps, 2 * (c - 2))
                sp.dma_start(v3(wo[c % 3], "p (k n) -> p k n", n=CW), wout[:, :, c * CW:(c + 1) * CW]).then_inc(wo_in[c % 3], 16)

        @block.gpsimd
        def _(pool):
            outs = 0

            def out(o, i, s=None):
                nonlocal outs
                ins = pool.dma_start(o, i)
                if s is None:
                    ins.then_inc(d_out, 16)
                    outs += 1
                else:
                    ins.then_inc(s, 16)

            out(O["a_win_s"][0, :, 0:WIN - DT].rearrange("b n a h c -> b n (a h c)"), I["state_a_win"][0, :, DT:WIN].rearrange("b n a h c -> b n (a h c)"))
            out(O["b_pool_s"][0, :, 0:11, :], I["state_b_pool"][0, :, 4:15, :])
            pool.wait_ge(b_ev, 5)
            pool.dma_start(d_rows, btmp[:, :]).then_inc(b_dma, 16)
            pool.wait_ge(b_dma, 16)
            pool.dma_start(d_rep.rearrange("p (h x) -> p h x", h=12), bass.AP(d_rows.tensor, d_rows.offset + TX0, [[0, P], [XL, 12], [1, TXL]])).then_inc(b_dma, 16)
            for t in range(DT):
                pool.dma_start(d_smp.rearrange("u (t g) x -> t u g x", t=DT)[t], bass.AP(d_rows.tensor, d_rows.offset + 3 - t, [[4 * XL, 3], [XL, 4], [1, SX]])).then_inc(b_dma, 16)
            o_akp = O["a_kv_p"].rearrange("l b (i p) a h c -> (l b i) p a (h c)", p=P)
            o_aks = O["a_kv_s"].rearrange("l b t a h c -> (l b t) a (h c)")
            o_ckp = O["c_kv_p"].rearrange("l b (i p) a c -> (l b i) p (a c)", p=P)
            o_cks = O["c_kv_s"].rearrange("l b t a c -> (l b t) (a c)")
            o_kip = O["c_kidx_p"].rearrange("l b (i p) c -> (l b i) p c", p=P)
            o_kis = O["c_kidx_s"].rearrange("l b t c -> (l b t) c")
            o_wp = O["a_win_p"].rearrange("l b (i p) a h c -> (l b i) p a (h c)", p=P)
            comp = {"kcmp": 0, "vcmp": 1, "kslc": 2, "vslc": 3}
            for j, (kind, b, t, c) in enumerate(jobs):
                if kind not in ROW_KINDS:
                    continue
                w = width(t)
                if j == idx_of[("kcmp", 0, 0)]:
                    pool.dma_start(v3(iqh, "p (c t) -> p c t", c=2), iqT3[ID:2 * ID, :, T:TT]).then_inc(iqh_in, 16)
                if j in staged:
                    n = staged.index(j)
                    pool.wait_ge(m_free, j + 1)
                    s, si = stage[n % 4], st_out[n % 4]
                    if kind == "small":
                        out(o_kip[t] if t < QT else o_kis, s[0:w, 0:ID], si)
                    elif kind == "ckv":
                        out(o_ckp[t] if t < QT else o_cks, s[0:w, :], si)
                    elif kind in comp:
                        out(o_akp[t, :, comp[kind]] if t < QT else o_aks[:, comp[kind]], s[0:w, :], si)
                    elif t < QT:
                        out(o_wp[t, :, 0], s[:, :], si)
                    else:
                        for b in range(DB):
                            out(O["a_win_s"][0, b, WIN - DT:WIN, 0].rearrange("t h c -> t (h c)"), s[DT * b:DT * b + DT, :], si if b == 0 else None)
                else:
                    pool.wait_ge(m_free, j + 1)
                    v = 0 if kind == "vslc" else 1
                    src = vnat3[:, t, v * CW:(v + 1) * CW] if t < QT else vN[:, v * CW:(v + 1) * CW]
                    if kind == "vslc":
                        out(o_akp[t, :, 3] if t < QT else o_aks[:, 3], src)
                    elif t < QT:
                        out(o_wp[t, :, 1], src)
                    else:
                        for b in range(DB):
                            out(O["a_win_s"][0, b, WIN - DT:WIN, 1].rearrange("t h c -> t (h c)"), vN[DT * b:DT * b + DT, CW:2 * CW])
            pool.wait_ge(pl_c, 2)
            out(O["b_pool_p"][0, 0], prw[1:16, 0:512])
            for b in range(DB):
                out(O["b_pool_s"][0, b, 11:15, :], prw[DT * b:DT * b + DT, 512:1024])
            for i in range(4):
                pool.wait_ge(st_out[i], 16 * len(range(i, len(staged), 4)))
            pool.wait_ge(d_out, 16 * outs)
            pool.drain().then_inc(ph_pool, 1)
            oy = O["y_prompt"].rearrange("a (i p) d -> p (a i) d", p=P)
            oys = O["y_sample"].rearrange("b t d -> (b t) d")
            for c in range(D // CW):
                pool.wait_ge(y_fin, 4 * (c + 1))
                pool.dma_start(oy[:, :, c * CW:(c + 1) * CW], v3(yrow[c % 2], "p (i d) -> p i d", i=5)[:, 0:QT, :]).then_inc(y_out, 16)
                pool.dma_start(oys[:, c * CW:(c + 1) * CW], v3(yrow[c % 2], "p (i d) -> p i d", i=5)[0:TS, QT, :]).then_inc(y_out, 16)
                pool.wait_ge(y_out, 32 * (c + 1))

        @block.tensor
        def _(pe):
            mm, tr = nc.tensor.matmul, nc.tensor.transpose

            def end_phase():
                pe.drain().then_inc(ph_pe, 1)

            pe.wait_ge(s_con, 16 * NSMALL)
            tr(bank[7][:, 0:NV], vrow[:, :], con[0:NV, 0:NV])
            tr(bank[7][:, 128:192], prow[:, :], con[0:64, 0:64])
            for k in range(KD):
                last = tr(bank[7][:, 256 + 9 * k:265 + 9 * k], crow[:, k * P:(k + 1) * P], con[0:9, 0:9])
            last.then_inc(su_tr, 1)
            for n in range(5):
                w = min(512, XL - 512 * n)
                mm(bank[n][0:12, 0:w], relb[:, :], ohr[:, 512 * n:512 * n + w], start=True, stop=True).then_inc(b_ps, 1)
            for t in range(QT + 1):
                w = width(t)
                pe.wait_ge(x_n, t + 1)
                for q in range(4):
                    g = 4 * t + q
                    if g < 4:
                        pe.wait_ge(b_ev, g + 1)
                    else:
                        pe.wait_ge(x_ev, g - 3)
                    for i in range(4):
                        k = 4 * q + i
                        last = tr(bank[g % 4][:, i * w:(i + 1) * w], xrow[t % 2][0:w, k * P:(k + 1) * P], con[0:w, 0:w])
                    last.then_inc(x_tr, 1)

            for g in range(4):
                last = tr(bank[6][:, g * 120:(g + 1) * 120], bst[:, g * P:(g + 1) * P], con[0:120, 0:120])
            last.then_inc(pst_t, 1)

            pe.wait_ge(c_s, 1)
            for n in range(NADA):
                pe.wait_ge(w_in_[n % 2], need[n])
                wv = v3(wbuf[n % 2], "p (k n) -> p k n", n=CW)
                for j in range(2):
                    for k in range(KD):
                        last = mm(bank[5][:, (2 * n + j) * 9:(2 * n + j + 1) * 9], wv[:, k, j * P:(j + 1) * P],
                                  cT[:, 9 * k:9 * k + 9], start=(k == 0), stop=(k == KD - 1))
                last.then_inc(w_free, 1)

            aux = 0

            def hook(j):
                nonlocal aux
                if j >= 1:
                    i = j - 1
                    kind, b, t, c = jobs[i]
                    if i in turned_set:
                        w = width(t)
                        pe.wait_ge(m_free, i + 1)
                        s = stage[staged.index(i) % 4]
                        for x in range(turns(i)):
                            if aux >= 2:
                                pe.wait_ge(a_free, aux - 1)
                            if aux < 2:
                                pe.wait_ge(pst_ev, 1)
                            tr(bank[6 + aux % 2][:, 0:w], s[0:w, x * P:(x + 1) * P], con[0:w, 0:w]).then_inc(a_done, 1)
                            aux += 1
                    if kind in ("cq", "aq"):
                        n = normT.index(i)
                        pe.wait_ge(n_sq, n + 1)
                        if n >= 1:
                            pe.wait_ge(n_std, n)
                        else:
                            pe.wait_ge(ixp_r, 12)
                        for f in range(2):
                            last = mm(bank[4 + f][:, 0:HALF], ones, sq[:, f * HALF:(f + 1) * HALF], start=True, stop=True)
                        last.then_inc(n_sum, 1)
                if j in ix_slot:
                    s = ix_slot[j]
                    if s[0] == "dots":
                        _, i, h, n = s
                        if n == 0:
                            pe.wait_ge(h_copied, 1)
                        if n >= 2:
                            pe.wait_ge(ixp_r, n - 1)
                        r0 = 64 * (h % 2)
                        mm(bank[4 + n % 2][:, 0:P * (i + 1)], iqT3[r0:r0 + 64, h // 2, i * P:(i + 1) * P],
                           ikT[r0:r0 + 64, 0:P * (i + 1)], start=True, stop=True).then_inc(ixp_d, 1)

            pe.wait_ge(h_ready, HREADY)
            pe.wait_ge(x_ev, 20)
            for j, (kind, b, t, c) in enumerate(jobs):
                n = NADA + c
                wv = wchunk(n, cwidth[c])
                pe.wait_ge(w_in_[n % 2], need[n])
                if j >= 2:
                    pe.wait_ge(m_free, j - 1)
                if kind in ROW_KINDS:
                    w = width(t)
                    for k in range(KD):
                        if k == 8:
                            hook(j)
                        last = mm(bank[2 * (j % 2)][0:w, 0:cwidth[c]], hT3[:, k, t * P:t * P + w], wv[:, k, :],
                                  start=(k == 0), stop=(k == KD - 1))
                else:
                    for f in range(2):
                        if f == 1:
                            hook(j)
                        for k in range(KD):
                            last = mm(bank[2 * (j % 2) + f][:, 0:HALF], wv[:, k, t * P:(t + 1) * P],
                                      hT3[:, k, f * HALF:(f + 1) * HALF], start=(k == 0), stop=(k == KD - 1))
                last.then_inc(m_done, 1)
            for g in range(4):
                pe.wait_ge(pl_d, g + 1)
                if g < 2:
                    pe.wait_ge(m_free, njobs)
                else:
                    pe.wait_ge(pl_y2, g - 1)
                for f in range(2):
                    last = mm(bank[2 * (g % 2) + f][:, 0:HALF], wpool[:, g * P:(g + 1) * P],
                              (sq if g % 2 == 0 else rs)[:, f * HALF:(f + 1) * HALF], start=True, stop=True)
                last.then_inc(pl_y, 1)
            pe.wait_ge(a_free, aux)
            for g in range(4):
                tr(bank[6][0:16, g * P:(g + 1) * P], bT3[:, g, T:T + 16], ident)
                last = tr(bank[7][0:TS, g * P:(g + 1) * P], wk[:, g * TS:(g + 1) * TS], ident)
            last.then_inc(pl_t, 1)
            mm(bank[4][:, 0:24], expd[:, 0:P], gateS0[:, :], start=True, stop=True)
            mm(bank[5][:, 0:4], expd[:, P:2 * P], iwS[:, :], start=True, stop=True).then_inc(pl_t, 1)
            end_phase()

            after(pe, 1)
            pe.wait_ge(w1_in, 64)
            for kv in range(2):
                w1 = v3(w1P[kv], "p (s h) -> p s h", h=256)
                for hb in range(2):
                    bk = bank[2 * kv + hb]
                    for s in range(32):
                        mm(bk[:, 0:62], w1[:, s, hb * P:(hb + 1) * P],
                           cmp4[:, kv, :, s:s + 16 * 30 + 1:16], start=(s == 0), stop=(s == 31))
                    for s in range(32):
                        last = mm(bk[:, 64:65], w1[:, s, hb * P:(hb + 1) * P], peT[:, kv * 32 + s:kv * 32 + s + 1],
                                  start=(s == 0), stop=(s == 31))
                    last.then_inc(cp_ps, 1)
            pe.wait_ge(cp_ev, 4)
            for hb in range(2):
                last = mm(bank[4][:, 0:62], w2P[:, hb * P:(hb + 1) * P], hidP[:, hb * 64:hb * 64 + 62], start=(hb == 0), stop=(hb == 1))
            last.then_inc(cp_ps, 1)
            for h in range(KVH):
                for hb in range(2):
                    last = mm(bank[5][0:NCP, h * P:(h + 1) * P], hidP[:, (2 + hb) * 64 + NCP * h:(2 + hb) * 64 + NCP * h + NCP],
                              w2P[:, 256 + hb * P:256 + (hb + 1) * P], start=(hb == 0), stop=(hb == 1))
            last.then_inc(cp_ps, 1)
            pe.wait_ge(cp_ev, 5)
            mm(bank[6][:, 0:62], ones, cxP[:, 64:126], start=True, stop=True).then_inc(cp_ps, 1)
            end_phase()

            after(pe, 2)

            def qk(u):
                grp, i, h = units[u]
                nk = P * (i + 1)
                if u >= 1:
                    pe.wait_ge(q_s, u)
                if grp == "A":
                    q = aqT3[:, h, i * P:(i + 1) * P]
                    k = h // G
                    mm(bank[2][:, 0:8 * i + 7], q, kcP[:, 32 * k:32 * k + 8 * i + 7], start=True, stop=True)
                    mm(bank[0][:, 0:nk], q, kslcT[:, k * T:k * T + nk], start=True, stop=True)
                    mm(bank[1][:, 0:nk], q, kwinT[:, k * T:k * T + nk], start=True, stop=True).then_inc(q_ps, 1)
                else:
                    mm(bank[0][:, 0:nk], cqT3[:, h, i * P:(i + 1) * P], ckT[:, 0:nk], start=True, stop=True).then_inc(q_ps, 1)

            def turn_p(u):
                grp, i, h = units[u]
                pe.wait_ge(q_p, u + 1)
                if u >= 1:
                    pe.wait_ge(q_ta, u)
                    pe.wait_ge(q_td, min(u, NUA))
                s = SP_[u % 3]
                if grp == "A":
                    for x in range(i + 1):
                        tr(bank[4][:, x * P:(x + 1) * P], s[:, 512 + x * P:512 + (x + 1) * P], ident)
                    tr(bank[5][0:8 * i + 7, 0:P], s[:, 1024:1024 + 8 * i + 7], ident)
                for x in range(i + 1):
                    last = tr(bank[3][:, x * P:(x + 1) * P], s[:, x * P:(x + 1) * P], ident)
                last.then_inc(q_t, 1)

            def pv(u):
                grp, i, h = units[u]
                pe.wait_ge(q_ta, u + 1)
                pe.wait_ge(q_td, min(u + 1, NUA))
                if u >= 2:
                    pe.wait_ge(q_m, u - 1)
                o = bank[6 + u % 2][:, 0:P]
                s = PTP[u % 2]
                if grp == "A":
                    k = h // G
                    nc_ = 8 * i + 7
                    mm(o, vcP[0:nc_, k * P:(k + 1) * P], s[0:nc_, 1024:1024 + P], start=True, stop=False)
                    for x in range(i + 1):
                        mm(o, vnat3[:, x, CW + k * P:CW + (k + 1) * P], s[:, 512 + x * P:512 + (x + 1) * P], start=False, stop=False)
                    for x in range(i + 1):
                        last = mm(o, vnat3[:, x, k * P:(k + 1) * P], s[:, x * P:(x + 1) * P], start=False, stop=(x == i))
                else:
                    for x in range(i + 1):
                        last = mm(o, cvnat[:, x * P:(x + 1) * P], s[:, x * P:(x + 1) * P], start=(x == 0), stop=(x == i))
                last.then_inc(q_o, 1)

            for n in range(len(units) + 3):
                if n < len(units):
                    qk(n)
                if 0 <= n - 2 < len(units):
                    turn_p(n - 2)
                if 0 <= n - 3 < len(units):
                    pv(n - 3)
            end_phase()

            after(pe, 3)

            def kturn(g, rows_out):
                if g >= 2:
                    pe.wait_ge(kb_d if g % 2 else kb_a, (g - 2) // 2 + 1)

            def evacuated(g):
                pe.wait_ge(kb_d if g % 2 else kb_a, g // 2 + 1)

            def ix_mm(n):
                b, q = n // 4, n % 4
                evacuated(n)
                mm(bank[q][32 * (b // 2):32 * (b // 2) + 32, :], zi[:, b * 32:(b + 1) * 32], ixT[n % 4][:, :],
                   start=(b % 2 == 0), stop=(b % 2 == 1), tile_position=(0, 32 * (b // 2))).then_inc(kb_mm, 1)

            for n in range(32):
                pe.wait_ge(kb_in[n % 8], kneed[n])
                kturn(n, ID)
                for i in range(4):
                    last = tr(bank[5 + n % 2][0:ID, i * P:(i + 1) * P], ixn[n % 8][:, i * ID:(i + 1) * ID], ident)
                last.then_inc(kb_tr, 1)
                if n >= 1:
                    ix_mm(n - 1)
            ix_mm(31)
            mm(bank[4][:, 0:TS], qfi[:, :], kiN[0:ID, :], start=True, stop=True).then_inc(si_ps, 1)
            for f in range(5):
                pe.wait_ge(si_ev, f + 1)
                w = 512 if f < 4 else TS
                mm(bank[f][:, 0:w], wsel[:, :], ixr[:, 512 * f:512 * f + w], start=True, stop=True).then_inc(si_ps, 1)
            end_phase()

            after(pe, 4)

            def row_turn(x):
                n, q, h = x // 8, x % 8 // 2, x % 2
                m = 4 * n + q
                pe.wait_ge(xn_in[m % 4], 64 * (m // 4 + 1))
                if x >= 2:
                    pe.wait_ge(xt_d if x % 2 else xt_a, (x - 2) // 2 + 1)
                for i in range(4):
                    last = tr(bank[4 + x % 2][:, i * P:(i + 1) * P], xnat[m % 4][:, i * 256 + h * P:i * 256 + (h + 1) * P], ident)
                last.then_inc(xn_tr, 1)

            def w2_mm(n):
                kv = n // 8
                pe.wait_ge(hd_ev, 2 * (n + 1))
                if n >= 1:
                    pe.wait_ge(kc_ok, n)
                if kv == 0:
                    for hb in range(2):
                        last = mm(bank[6][:, 0:254], w2S[:, hb * P:(hb + 1) * P], hid[0][:, hb * 256:hb * 256 + 254], start=(hb == 0), stop=(hb == 1))
                else:
                    for h in range(KVH):
                        for hb in range(2):
                            last = mm(bank[6][0:NCS, h * P:(h + 1) * P], hid[0][:, hb * 256 + NCS * h:hb * 256 + NCS * (h + 1)],
                                      w2S[:, 256 + hb * P:256 + (hb + 1) * P], start=(hb == 0), stop=(hb == 1))
                last.then_inc(kc_ps, 1)

            for n in range(18):
                for i in range(8):
                    g = n - 1
                    if 0 <= g < 16:
                        kv = g // 8
                        if i == 0:
                            pe.wait_ge(w1s_in, 64)
                            pe.wait_ge(xt_a, 4 * (g + 1))
                            pe.wait_ge(xt_d, 4 * (g + 1))
                            if g >= 2:
                                pe.wait_ge(hd_ev, 2 * (g - 1))
                        w1 = v3(w1S[kv], "p (s h) -> p s h", h=256)
                        xv = v3(xt[g % 2], "p (h s c) -> p h s c", h=2, s=16)
                        for e in range(8):
                            hb, s = (8 * i + e) // 32, (8 * i + e) % 32
                            last = mm(bank[2 * (g % 2) + hb][:, 0:254], w1[:, s, hb * P:(hb + 1) * P],
                                      xv[:, :, s % 16, s // 16:s // 16 + NCS], start=(s == 0), stop=(s == 31))
                        if i == 7:
                            last.then_inc(hd_ps, 1)
                    if n < 16:
                        row_turn(8 * n + i)
                    if 0 <= n - 2 < 16 and i == 3:
                        w2_mm(n - 2)
                    if 0 <= n - 2 < 8 and i == 6:
                        pe.wait_ge(kc_x, n - 1)
                        mm(bank[7][:, 0:254], ones, cx[:, 256:510], start=True, stop=True).then_inc(kc_sum, 1)
            end_phase()

            after(pe, 5)
            gt = 32

            def kb(n, pend):
                nonlocal gt
                m = 32 + n
                pe.wait_ge(kb_in[m % 8], kneed[m])
                kturn(gt, HD)
                for i in range(4):
                    last = tr(bank[5 + gt % 2][:, i * P:(i + 1) * P], kn[n % 8][:, i * P:(i + 1) * P], ident)
                last.then_inc(kb_tr, 1)
                g = gt
                gt += 1
                return g

            def kmm(n, g):
                u, kind, b, q = sblocks[n]
                evacuated(g)
                mm(bank[q][32 * (b // 2):32 * (b // 2) + 32, :], zq4[:, u, b, :], kT[n % 4][:, :],
                   start=(b % 2 == 0), stop=(b % 2 == 1), tile_position=(0, 32 * (b // 2))).then_inc(kb_mm, 1)

            n = 0
            vn = 0
            for u in range(3):
                for kind, nb in ((("win", 8), ("slc", 32)) if u < 2 else (("slc", 32),)):
                    if kind == "slc" and u < 2:
                        pe.wait_ge(un_w, u + 1)
                    elif u >= 1:
                        pe.wait_ge(un_s, u)
                    held = None
                    for x in range(nb):
                        g = kb(n, held)
                        if held is not None:
                            kmm(*held)
                        held = (n, g)
                        n += 1
                        if kind == "slc" and u < 2 and x == 12:
                            pe.wait_ge(im_in, u + 1)
                            if u == 1:
                                pe.wait_ge(un_x, 1)
                            mm(bank[7][:, 0:NCS], con[:, K_GRP:K_GRP + P], sC[:, 0:NCS], start=True, stop=True).then_inc(im_ps, 1)
                    kmm(*held)
                    if kind == "win":
                        mm(bank[4][:, 32:64], qf3[:, u, :], ksN[:, (2 + u) * TS:(3 + u) * TS], start=True, stop=True)
                        for b in range(DB):
                            last = mm(bank[4][32 * (b // 2):32 * (b // 2) + 32, 64:64 + NCS], zq4[:, u, b, :], kc[:, (b * KVH + u) * P:(b * KVH + u) * P + NCS],
                                      start=(b % 2 == 0), stop=(b % 2 == 1), tile_position=(0, 32 * (b // 2)), skip_group_check=True)
                        last.then_inc(un_ps, 1)
                    else:
                        mm(bank[4][:, 0:TS], qf3[:, u, :], ksN[:, (u if u < 2 else 4) * TS:(u if u < 2 else 4) * TS + TS], start=True, stop=True).then_inc(un_ps, 1)
                pe.wait_ge(un_p, u + 1)
                for src in pgroups(u):
                    kturn(gt, HD)
                    for i, (s, rows) in enumerate(src):
                        last = tr(bank[5 + gt % 2][0:rows, i * P:(i + 1) * P], s, ident)
                    last.then_inc(kb_tr, 1)
                    gt += 1
                evacuated(gt - 1)
                evacuated(gt - 2)
                if u >= 1:
                    pe.wait_ge(un_x, u)
                o = bank[7]
                k = u
                if u < 2:
                    mm(o[:, 0:P], vN[:, k * P:(k + 1) * P], pT[0:TS, 16 * P:17 * P], start=True, stop=False)
                    for b in range(DB):
                        mm(o[:, 16 * b:16 * b + 16], vc[0:NCS, (b * KVH + k) * P:(b * KVH + k + 1) * P], pT[0:NCS, 22 * P + 16 * b:22 * P + 16 * b + 16],
                           start=False, stop=False, skip_group_check=True)
                    for half in range(2):
                        pe.wait_ge(vr_in[vn % 4], vneed[vn])
                        for j in range(4):
                            b = 4 * half + j
                            for i in range(4):
                                last = mm(o[:, 16 * b:16 * b + 16], vr[vn % 4][:, (4 * j + i) * P:(4 * j + i + 1) * P],
                                          pT[:, (17 + i) * P + 16 * b:(17 + i) * P + 16 * b + 16], start=False, stop=False, skip_group_check=True)
                        last.then_inc(pv_b, 1)
                        vn += 1
                for b in range(DB):
                    pe.wait_ge(vr_in[vn % 4], vneed[vn])
                    if u == 2:
                        mm(o[:, 16 * b:16 * b + 16], cvN[:, :], pT[0:TS, 16 * P + 16 * b:16 * P + 16 * b + 16], start=True, stop=False)
                    for i in range(NPG):
                        last = mm(o[:, 16 * b:16 * b + 16], vr[vn % 4][:, i * P:(i + 1) * P],
                                  pT[:, i * P + 16 * b:i * P + 16 * b + 16], start=False, stop=(u == 2 and i == NPG - 1), skip_group_check=(u < 2))
                    if u < 2 and b == DB - 1:
                        last = mm(o[:, 0:P], vN[:, CW + k * P:CW + (k + 1) * P], pT[0:TS, 21 * P:22 * P], start=False, stop=True)
                    last.then_inc(pv_b, 1)
                    vn += 1
            end_phase()

            after(pe, 6)

            def y_turn(nb):
                pe.wait_ge(y_ev, nb + 1)
                if nb >= 2:
                    pe.wait_ge(y_fin, 2 * (nb - 1))
                s = yT[nb % 4]
                for i in range(QT):
                    tr(bank[4 + nb % 2][:, i * P:(i + 1) * P], s[:, i * P:(i + 1) * P], ident)
                tr(bank[6 + nb % 2][0:TS, 0:P], s[:, T:TT], ident).then_inc(y_tr, 1)

            for nb in range(KD):
                c = nb // 2
                pe.wait_ge(wo_in[c % 3], 16 * (c // 3 + 1))
                if nb >= 2:
                    pe.wait_ge(y_ev, nb - 1)
                wv = v3(wo[c % 3], "p (k n) -> p k n", n=CW)
                for f in range(2):
                    for k in range(KD):
                        last = mm(bank[2 * (nb % 2) + f][:, 0:HALF], wv[:, k, (nb % 2) * P:(nb % 2 + 1) * P],
                                  mix3[:, k, f * HALF:(f + 1) * HALF], start=(k == 0), stop=(k == KD - 1))
                    if f == 0 and nb >= 1:
                        y_turn(nb - 1)
                last.then_inc(y_ps, 1)
            y_turn(KD - 1)

        @block.scalar
        def _(act):
            A = nc.scalar.activation
            mine = Count(act, act_)
            eps = con[:, K_EPS:K_EPS + 1]

            def end_phase():
                act.drain().then_inc(ph_act, 1)

            for n in range(5):
                w = min(512, XL - 512 * n)
                act.wait_ge(b_ps, n + 1)
                A(btmp[:, 512 * n:512 * n + w], bank[n][0:12, 0:w], ACT.Copy).then_inc(b_ev, 1)
            act.wait_ge(su_ev, 1)
            A(cT[:, 144:288], bank[7][:, 256:400], ACT.Exp, scale=-1.0).then_inc(c_e, 1)
            for t in range(QT + 1):
                w = width(t)
                act.wait_ge(s_x[t % 2], 16 * (t // 2 + 1))
                if t >= 1:
                    evac_x(act, A, t - 1)
                mine.link(A(mix[0:w, 0:D], xrow[t % 2][0:w, :], ACT.Square, accum_out=st[0:w, t:t + 1]))
                A(st[0:w, 8 + t:9 + t], st[0:w, t:t + 1], ACT.Sqrt, scale=1.0 / D, bias=con[0:w, K_EPS:K_EPS + 1]).then_inc(x_std, 1)
            evac_x(act, A, QT)
            act.wait_ge(pst_t, 1)
            for g in range(4):
                last = act.copy(bS4[:, g, :, 0:15], bank[6][:, g * 120:(g + 1) * 120].rearrange("p (b t) -> p b t", t=15))
            last.then_inc(pst_ev, 1)

            aux = 0
            nr = 0

            def hook(j):
                nonlocal aux
                if j >= 1:
                    i = j - 1
                    kind, b, t, c = jobs[i]
                    if i in turned_set:
                        w = width(t)
                        for x in range(turns(i)):
                            act.wait_ge(a_done, aux + 1)
                            act.copy(turned_to(kind, t, x), bank[6 + aux % 2][:, 0:w]).then_inc(a_free, 1)
                            aux += 1
                    if kind in ("cq", "aq"):
                        n = normT.index(i)
                        act.wait_ge(n_sum, n + 1)
                        if n >= 1:
                            act.wait_ge(m_free, normT[n - 1] + 1)
                        for f in range(2):
                            last = A(rs[:, f * HALF:(f + 1) * HALF], bank[4 + f][:, 0:HALF], ACT.Sqrt, scale=1.0 / HD, bias=eps)
                        last.then_inc(n_std, 1)
                if j in ix_slot and ix_slot[j][0] == "dots":
                    _, i, h, n = ix_slot[j]
                    act.wait_ge(ixp_d, n + 1)
                    if n >= 1:
                        act.wait_ge(ixp_a, n)
                    A(rs[:, 0:P * (i + 1)], bank[4 + n % 2][:, 0:P * (i + 1)], ACT.Relu).then_inc(ixp_r, 1)

            for j, (kind, b, t, c) in enumerate(jobs):
                hook(j)
                if j in rownorm:
                    w = width(t)
                    act.wait_ge(m_done, j + 1)
                    nh = 1 if kind == "ckv" else 2
                    o = 24 + 4 * (nr % 2)
                    if nr >= 2:
                        act.wait_ge(m_free, rownorm[nr - 2] + 1)
                    for h in range(nh):
                        mine(A(sq[0:w, 0:P], bank[2 * (j % 2)][0:w, h * P:(h + 1) * P], ACT.Square, accum_out=st[0:w, o + h:o + h + 1]))
                        mine.wait()
                    A(st[0:w, o + 2:o + 2 + nh], st[0:w, o:o + nh], ACT.Sqrt, scale=1.0 / HD, bias=con[0:w, K_EPS:K_EPS + 1]).then_inc(r_std, 1)
                    nr += 1
                elif kind in ("cq", "aq"):
                    n = normT.index(j)
                    act.wait_ge(m_done, j + 1)
                    if n >= 1:
                        act.wait_ge(n_sum, n)
                    for f in range(2):
                        last = A(sq[:, f * HALF:(f + 1) * HALF], bank[2 * (j % 2) + f][:, 0:HALF], ACT.Square)
                    last.then_inc(n_sq, 1)
                elif kind in SIL_AT:
                    n = silj.index(j)
                    act.wait_ge(m_done, j + 1)
                    if n >= 2:
                        act.wait_ge(m_free, silj[n - 2] + 1)
                    elif n == 0:
                        act.wait_ge(n_sum, len(normT))
                        act.wait_ge(m_free, normT[-1] + 1)
                    for f in range(2):
                        last = A((sq, rs)[n % 2][:, f * HALF:(f + 1) * HALF], bank[2 * (j % 2) + f][:, 0:HALF], ACT.Exp, scale=-1.0)
                    last.then_inc(sil_e, 1)
            hook(njobs)
            A(gateP[:, :], gateP[:, :], ACT.Exp, scale=-1.0).then_inc(g_e, 1)
            act.wait_ge(gs_in, 1)
            A(gateS[:, :], gateS[:, :], ACT.Exp, scale=-1.0).then_inc(g_e, 1)
            end_phase()

            after(act, 1)
            for kv in range(2):
                for hb in range(2):
                    n = 2 * kv + hb
                    act.wait_ge(cp_ps, n + 1)
                    mine.link(A(b1e[:, n:n + 1], bank[n][:, 64:65], ACT.Identity, bias=vecT[:, V_B1 + n:V_B1 + n + 1]))
                    A(hidP[:, n * 64:n * 64 + 62], bank[n][:, 0:62], ACT.Gelu_apprx_tanh, bias=b1e[:, n:n + 1]).then_inc(cp_ev, 1)
            act.wait_ge(cp_ps, 5)
            mine(A(cxP[:, 0:62], bank[4][:, 0:62], ACT.Identity, bias=vecT[:, V_B2:V_B2 + 1]))
            A(cxP[:, 64:126], bank[4][:, 0:62], ACT.Square, bias=vecT[:, V_B2:V_B2 + 1]).then_inc(cp_ev, 1)
            act.wait_ge(cp_ps, 7)
            A(cxP[:, 128:190], bank[6][:, 0:62], ACT.Sqrt, scale=1.0 / HD, bias=eps).then_inc(cp_ev, 1)
            end_phase()

            after(act, 2)

            def exps(u):
                grp, i, h = units[u]
                nk = P * (i + 1)
                s, a = SP_[u % 3], 16 * (u % 4)
                act.wait_ge(q_s, u + 1)
                parts = ((1024, 8 * i + 7, 0), (0, nk, 1), (512, nk, 2)) if grp == "A" else ((0, nk, 1),)
                for off, n, r in parts:
                    last = A(s[:, off:off + n], s[:, off:off + n], ACT.Exp, bias=as_[:, a + 3 + r:a + 4 + r], accum_out=as_[:, a + 6 + r:a + 7 + r])
                last.then_inc(q_e, 1)

            def take_slc(u):
                grp, i, h = units[u]
                act.wait_ge(q_t, u + 1)
                if u >= 2:
                    act.wait_ge(q_o, u - 1)
                act.copy(PTP[u % 2][:, 0:P * (i + 1)], bank[3][:, 0:P * (i + 1)]).then_inc(q_ta, 1)

            for n in range(len(units) + 2):
                if n < len(units):
                    exps(n)
                if 0 <= n - 2 < len(units):
                    take_slc(n - 2)
            end_phase()

            after(act, 3)
            for n in range(0, 32, 2):
                act.wait_ge(kb_tr, n + 1)
                if n >= 4:
                    act.wait_ge(kb_mm, n - 3)
                act.copy(ixT[n % 4][:, :], bank[5][0:ID, :]).then_inc(kb_a, 1)
            act.wait_ge(kb_mm, 32)
            act.wait_ge(si_ps, 1)
            for f in range(5):
                w = 512 if f < 4 else TS
                A(ixr[:, 512 * f:512 * f + w], bank[f][:, 0:w], ACT.Relu).then_inc(si_ev, 1)
            end_phase()

            after(act, 4)

            def hidden(g):
                act.wait_ge(hd_ps, g + 1)
                if g >= 1:
                    act.wait_ge(kc_ps, g)
                for hb in range(2):
                    A(hid[0][:, hb * 256:hb * 256 + 254], bank[2 * (g % 2) + hb][:, 0:254], ACT.Gelu_apprx_tanh,
                      bias=b1e[:, 2 * (g // 8) + hb:2 * (g // 8) + hb + 1]).then_inc(hd_ev, 1)

            for n in range(18):
                if 0 <= n - 2 < 16:
                    hidden(n - 2)
                for i in range(0, 8, 2):
                    if n < 16:
                        x = 8 * n + i
                        take_rows(act, act.copy, x, xt_a)
                    if 0 <= n - 2 < 8 and i == 4:
                        g = n - 2
                        act.wait_ge(kc_ps, g + 1)
                        if g >= 1:
                            act.wait_ge(kc_ok, g)
                        mine(A(cx[:, 0:254], bank[6][:, 0:254], ACT.Identity, bias=vecT[:, V_B2:V_B2 + 1]))
                        A(cx[:, 256:510], bank[6][:, 0:254], ACT.Square, bias=vecT[:, V_B2:V_B2 + 1]).then_inc(kc_x, 1)
                if 0 <= n - 2 < 8:
                    act.wait_ge(kc_sum, n - 1)
                    A(cx[:, 256:510], bank[7][:, 0:254], ACT.Sqrt, scale=1.0 / HD, bias=eps).then_inc(kc_std, 1)
            end_phase()

            after(act, 5)
            gt = 32
            n = 0
            for u in range(3):
                nb = 40 if u < 2 else 32
                for x in range(nb):
                    if u < 2 and x == 8:
                        unit_exps(act, A, u, "early")
                    if gt % 2 == 0:
                        act.wait_ge(kb_tr, gt + 1)
                        if n >= 4:
                            act.wait_ge(kb_mm, 32 + n - 3)
                        act.copy(kT[n % 4][:, :], bank[5][:, :]).then_inc(kb_a, 1)
                    gt += 1
                    n += 1
                unit_exps(act, A, u, "late")
                for gi, src in enumerate(pgroups(u)):
                    if gt % 2 == 0:
                        act.wait_ge(kb_tr, gt + 1)
                        take_p(act, act.copy, u, gi, src, kb_a)
                    gt += 1
            end_phase()

        @block.vector
        def _(v):
            V = nc.vector
            mine = Count(v, dve)
            link = mine.link

            def end_phase():
                v.drain().then_inc(ph_dve, 1)

            def ttr(out, a, b, acc):
                return V.tensor_tensor_reduce(out=out, in0=a, in1=b, scale=1.0, scalar=FLOOR, op0=ALU.add, op1=ALU.max, accum_out=acc)

            v.wait_ge(su_tr, 1)
            link(V.tensor_copy(vecT[:, :], bank[7][:, 0:NV]))
            V.tensor_copy(peT[:, :], bank[7][:, 128:192]).then_inc(su_ev, 1)
            v.wait_ge(c_e, 1)
            link(V.tensor_scalar(cT[:, 144:288], cT[:, 144:288], 1.0, None, ALU.add))
            link(V.reciprocal(cT[:, 144:288], cT[:, 144:288]))
            V.tensor_tensor(cT[:, 0:144], bank[7][:, 256:400], cT[:, 144:288], ALU.mult).then_inc(c_s, 1)
            link(V.tensor_scalar(vecT[:, V_AQ:V_CQ + 1], vecT[:, V_AQ:V_CQ + 1], SCALE, None, ALU.mult))
            for t in range(QT + 1):
                w = width(t)
                v.wait_ge(x_std, t + 1)
                link(V.reciprocal(st[0:w, 16 + t:17 + t], st[0:w, 8 + t:9 + t]))
                V.tensor_scalar(xrow[t % 2][0:w, :], xrow[t % 2][0:w, :], st[0:w, 16 + t:17 + t], None, ALU.mult).then_inc(x_n, 1)
            link(V.memset(zq[:, :], 0.0))
            link(V.memset(zi[:, :], 0.0))
            link(V.memset(bT[:, :], 0.0))
            v.wait_ge(w_free, NADA)
            link(V.tensor_tensor(mod3, bank[5][:, 0:432].rearrange("p (n b) -> p n b", b=9), bc(vecT[:, 0:48], 9), ALU.add))
            V.tensor_scalar(ascale[:, :], modT[:, 144:288], 1.0, None, ALU.add).then_inc(h_copied, 1)
            v.wait_ge(h_copied, 1)
            link(V.tensor_tensor(asc3, asc3, bc(vecT[:, V_G:V_G + 16], 9), ALU.mult))
            v.wait_ge(x_ev, 20)
            for k in range(KD):
                V.tensor_scalar(hT3[:, k, 0:T], hT3[:, k, 0:T], asc3[:, k, 0:1], mod3[:, k, 0:1], ALU.mult, ALU.add).then_inc(h_ready, 1)
            for k in range(KD):
                hs = hT3[:, k, T:TT].rearrange("p (b t) -> p b t", t=DT)
                link(V.tensor_tensor(hs, hs, bc(asc3[:, k, 1:9], DT), ALU.mult))
                V.tensor_tensor(hs, hs, bc(mod3[:, k, 1:9], DT), ALU.add).then_inc(h_ready, 1)

            nr = 0

            def topk(w, out8, times):
                for _ in range(times):
                    link(V.max(out8, w))
                    link(V.match_replace(w, out8, w, MARK))

            for j, (kind, b, t, c) in enumerate(jobs):
                bk = bank[2 * (j % 2)]
                if j in ix_slot:
                    s = ix_slot[j]
                    i = s[1]
                    nk = P * (i + 1)
                    if s[0] == "dots":
                        _, i, h, n = s
                        v.wait_ge(ixp_r, n + 1)
                        wi = iwP[:, 4 * i + h:4 * i + h + 1]
                        if h == 0:
                            link(V.tensor_scalar(wk[:, 0:nk], rs[:, 0:nk], wi, None, ALU.mult))
                            V.tensor_tensor(wk[:, P * i:nk], wk[:, P * i:nk], con[:, K_DIAG:K_DIAG + P], ALU.add).then_inc(ixp_a, 1)
                        else:
                            V.scalar_tensor_tensor(out=wk[:, 0:nk], in0=rs[:, 0:nk], scalar=wi, in1=wk[:, 0:nk], op0=ALU.mult, op1=ALU.add).then_inc(ixp_a, 1)
                        v.wait_ge(ixp_a, n + 1)
                    else:
                        topk(wk[:, 0:nk], st[:, 48:56], 4)
                        if s[2] == 3:
                            link(V.tensor_scalar(maskC[:, MOFF[i]:MOFF[i] + nk], wk[:, 0:nk], MARK, NEG, ALU.not_equal, ALU.mult))
                v.wait_ge(m_done, j + 1)
                w = width(t)
                if j in staged_set:
                    n = staged.index(j)
                    if n >= 4:
                        v.wait_ge(st_out[n % 4], 16 * (n // 4))
                        i = staged[n - 4]
                        if i in turned_set:
                            v.wait_ge(a_done, sum(turns(x) for x in turned if x <= i))
                    s = stage[n % 4]
                if kind == "small":
                    V.tensor_copy(s[0:w, 0:ID], bk[0:w, 24:24 + ID])
                    V.tensor_copy(s[0:w, ID:2 * ID], bk[0:w, 24:24 + ID])
                    V.tensor_copy(gateP[:, 24 * t:24 * t + 24] if t < QT else gateS0[:, :], bk[0:w, 0:24])
                    V.tensor_copy(iwP[:, 4 * t:4 * t + 4] if t < QT else iwS[:, :], bk[0:w, 24 + ID:24 + ID + 4]).then_inc(m_free, 1)
                elif j in rownorm:
                    nh = 1 if kind == "ckv" else 2
                    o = 24 + 4 * (nr % 2)
                    nr += 1
                    v.wait_ge(r_std, nr)
                    link(V.reciprocal(st[0:w, o + 2:o + 2 + nh], st[0:w, o + 2:o + 2 + nh]))
                    gr = {"kslc": 0, "kwin": 1, "ckv": 2}[kind]
                    if kind == "ckv":
                        V.tensor_copy(s[0:w, P:2 * P], bk[0:w, P:2 * P])
                        V.tensor_copy(cvnat[:, t * P:(t + 1) * P] if t < QT else cvN[:, :], bk[0:w, P:2 * P])
                    for h in range(nh):
                        last = V.scalar_tensor_tensor(out=s[0:w, h * P:(h + 1) * P], in0=bk[0:w, h * P:(h + 1) * P], scalar=st[0:w, o + 2 + h:o + 3 + h],
                                                      in1=gk[0:w, gr * P:(gr + 1) * P], op0=ALU.mult, op1=ALU.mult)
                    last.then_inc(m_free, 1)
                elif kind in ("kcmp", "vcmp"):
                    V.tensor_copy(s[0:w, :], bk[0:w, 0:CW]).then_inc(m_free, 1)
                elif kind in ("vslc", "vwin"):
                    x = 0 if kind == "vslc" else CW
                    V.tensor_copy(vnat3[:, t, x:x + CW] if t < QT else vN[:, x:x + CW], bk[0:w, 0:CW]).then_inc(m_free, 1)
                else:
                    b2 = bank[2 * (j % 2) + 1]
                    if kind == "iq":
                        V.tensor_copy(iqT3[:, b, 0:HALF], bk[:, 0:HALF])
                        V.tensor_copy(iqT3[:, b, HALF:TT], b2[:, 0:HALF]).then_inc(m_free, 1)
                    elif kind in ("cq", "aq"):
                        n = normT.index(j)
                        v.wait_ge(n_std, n + 1)
                        link(V.reciprocal(rs[:, :], rs[:, :]))
                        dst = aqT3 if kind == "aq" else cqT3
                        col = vecT[:, V_AQ:V_AQ + 1] if kind == "aq" else vecT[:, V_CQ:V_CQ + 1]
                        u, g = (b // G, b % G) if kind == "aq" else (2, b)
                        for o, i, r in ((dst[:, b, 0:HALF], bk[:, 0:HALF], rs[:, 0:HALF]),
                                        (dst[:, b, HALF:T], b2[:, 0:T - HALF], rs[:, HALF:T]),
                                        (qf3[:, u, g:P:4], b2[:, T - HALF:HALF], rs[:, T:TT])):
                            last = V.scalar_tensor_tensor(out=o, in0=i, scalar=col, in1=r, op0=ALU.mult, op1=ALU.mult)
                        last.then_inc(m_free, 1)
                    elif kind == "bin":
                        V.tensor_copy(bT3[:, b, 16:16 + HALF], bk[:, 0:HALF])
                        V.tensor_copy(bT3[:, b, 16 + HALF:16 + T], b2[:, 0:T - HALF])
                        V.tensor_copy(wk[:, b * TS:(b + 1) * TS], b2[:, T - HALF:HALF])
                        V.tensor_copy(bS4[:, b, :, 15:19], b2[:, T - HALF:HALF].rearrange("p (b t) -> p b t", t=DT)).then_inc(m_free, 1)
                    else:
                        n = silj.index(j)
                        e = (sq, rs)[n % 2]
                        blk = SIL_AT[kind] + b
                        v.wait_ge(sil_e, n + 1)
                        link(V.tensor_scalar(e[:, :], e[:, :], 1.0, None, ALU.add))
                        link(V.reciprocal(e[:, :], e[:, :]))
                        V.tensor_tensor(mix3[:, blk, 0:HALF], bk[:, 0:HALF], e[:, 0:HALF], ALU.mult)
                        V.tensor_tensor(mix3[:, blk, HALF:TT], b2[:, 0:HALF], e[:, HALF:TT], ALU.mult).then_inc(m_free, 1)
            v.wait_ge(m_free, njobs)
            v.wait_ge(iqh_in, 16)
            for h in range(IH):
                src = (iqT3[0:ID, h // 2, T:TT] if h % 2 == 0 else iqh[:, (h // 2) * TS:(h // 2 + 1) * TS]).rearrange("p (b t) -> p b t", t=DT)
                last = V.tensor_copy(qfi[:, :].rearrange("p (b h t) -> p b h t", h=IH, t=DT)[:, :, h, :], src)
            link(last)
            for par in range(2):
                V.tensor_copy(v3(zi, "p (c e r) -> p c e r", e=2, r=32)[:, :, par, 16 * par:16 * par + 16], v3(qfi, "p (c e r) -> p c e r", e=2, r=16)[:, :, par, :])
                V.tensor_copy(v3(zq, "p (c e r) -> p c e r", e=2, r=32)[:, :, par, 16 * par:16 * par + 16], v3(qf, "p (c e r) -> p c e r", e=2, r=16)[:, :, par, :])
            v.wait_ge(pst_ev, 1)
            for g in range(4):
                o = (sq, rs)[g % 2]
                if g >= 2:
                    v.wait_ge(pl_y, g - 1)
                win_w = 2 << g
                cur = bT3[:, g, :]
                lo = 16
                step = 1
                src_p, src_s = cur, bS4[:, g, :, :]
                pa, pb_ = pls[:, 0:528], pls[:, 528:1056]
                sa, sb_ = pls[:, 1056:1056 + 160], pls[:, 1216:1216 + 160]
                flip = 0
                while step < win_w:
                    dp = (pa, pb_)[flip]
                    ds_ = (sa, sb_)[flip].rearrange("p (b t) -> p b t", t=20)
                    link(V.tensor_tensor(dp[:, 2 * step - 1:528], src_p[:, 2 * step - 1:528], src_p[:, step - 1:528 - step], ALU.add))
                    link(V.tensor_tensor(ds_[:, :, 2 * step - 1:19], src_s[:, :, 2 * step - 1:19], src_s[:, :, step - 1:19 - step], ALU.add))
                    src_p, src_s = dp, ds_
                    flip ^= 1
                    step *= 2
                V.scalar_tensor_tensor(out=o[:, 0:T], in0=src_p[:, 16:528], scalar=1.0 / win_w, in1=cur[:, 16:528], op0=ALU.mult, op1=ALU.subtract)
                link(V.scalar_tensor_tensor(out=o[:, T:TT].rearrange("p (b t) -> p b t", t=DT), in0=src_s[:, :, 15:19], scalar=1.0 / win_w,
                                            in1=bS4[:, g, :, 15:19], op0=ALU.mult, op1=ALU.subtract))
                link(V.tensor_tensor(pls[:, 1376:1392], src_p[:, 16:32], con[:, K_RC + 16 * g:K_RC + 16 * g + 16], ALU.mult))
                V.tensor_tensor(o[:, 0:16], pls[:, 1376:1392], cur[:, 16:32], ALU.subtract).then_inc(pl_d, 1)
                if g >= 1:
                    pool_out(v, V, g - 1)
            pool_out(v, V, 3)
            v.wait_ge(pl_t, 1)
            v.wait_ge(pl_y, 4)
            V.tensor_copy(prw[0:16, 0:512], bank[6][0:16, :]).then_inc(pl_c, 1)
            V.tensor_copy(prw[0:TS, 512:1024], bank[7][0:TS, :]).then_inc(pl_c, 1)
            v.wait_ge(pl_t, 2)
            link(V.tensor_copy(gateS1[:, :], bank[4][:, 0:24]))
            for r in range(3):
                for k in range(2):
                    link(V.tensor_tensor_reduce(out=st[:, 56:60], in0=gateS1[:, 8 * r + 4 * k:8 * r + 4 * k + 4], in1=con[:, K_M3:K_M3 + 4], scale=1.0, scalar=0.0,
                                                op0=ALU.mult, op1=ALU.add, accum_out=gateS[:, 2 * r + k:2 * r + k + 1]))
            V.tensor_tensor_reduce(out=st[:, 60:64], in0=bank[5][:, 0:4], in1=con[:, K_M2:K_M2 + 4], scale=1.0, scalar=0.0,
                                   op0=ALU.mult, op1=ALU.add, accum_out=wiS[:, 0:1]).then_inc(gs_in, 1)
            v.wait_ge(gs_in, 1)
            link(V.tensor_scalar(wsel[:, :], con[:, K_WM:K_WM + P], wiS[:, 0:1], None, ALU.mult))
            v.wait_ge(g_e, 2)
            for gt_ in (gateP, gateS):
                link(V.tensor_scalar(gt_[:, :], gt_[:, :], 1.0, None, ALU.add))
                link(V.reciprocal(gt_[:, :], gt_[:, :]))
            end_phase()

            after(v, 1)
            v.wait_ge(cp_ps, 6)
            V.tensor_tensor(vcP[0:NCP, :].rearrange("p (h c) -> p h c", h=2), bank[5][0:NCP, 0:256].rearrange("p (h c) -> p h c", h=2),
                            gk[0:NCP, 3 * P:4 * P].unsqueeze(1).broadcast_to([NCP, 2, P]), ALU.add)
            v.wait_ge(cp_ev, 6)
            link(V.reciprocal(cxP[:, 128:190], cxP[:, 128:190]))
            for h in range(2):
                V.scalar_tensor_tensor(out=kcP[:, 32 * h:32 * h + NCP], in0=cxP[:, NCP * h:NCP * (h + 1)], scalar=vecT[:, V_AK:V_AK + 1],
                                       in1=cxP[:, 128 + NCP * h:128 + NCP * (h + 1)], op0=ALU.mult, op1=ALU.mult)
            end_phase()

            after(v, 2)
            v.wait_ge(at_in, 16)
            b3 = v3(bias, "p (h j) -> p h j", h=12)

            def scores(u):
                grp, i, h = units[u]
                nk = P * (i + 1)
                s, a = SP_[u % 3], 16 * (u % 4)
                off = 384 - P * i
                v.wait_ge(q_ps, u + 1)
                if u >= 3:
                    v.wait_ge(q_t, u - 2)
                if grp == "A":
                    n = 8 * i + 7
                    ttr(s[:, 1024:1024 + n], bank[2][:, 0:n], b3[:, h, off + 31:off + 31 + 16 * (n - 1) + 1:16], as_[:, a:a + 1])
                    ttr(s[:, 0:nk], bank[0][:, 0:nk], b3[:, h, off:off + nk], as_[:, a + 1:a + 2])
                    link(ttr(s[:, 512:512 + nk], bank[1][:, 0:nk], b3[:, h, off:off + nk], as_[:, a + 2:a + 3]))
                    V.tensor_scalar(as_[:, a + 3:a + 6], as_[:, a:a + 3], -1.0, None, ALU.mult).then_inc(q_s, 1)
                else:
                    if i == 0:
                        link(ttr(s[:, 0:nk], bank[0][:, 0:nk], b3[:, 8 + h, off:off + nk], as_[:, a + 1:a + 2]))
                    else:
                        link(V.tensor_tensor(s[:, 0:nk], bank[0][:, 0:nk], b3[:, 8 + h, off:off + nk], ALU.add))
                        link(ttr(s[:, 0:nk], s[:, 0:nk], maskC[:, MOFF[i]:MOFF[i] + nk], as_[:, a + 1:a + 2]))
                    V.tensor_scalar(as_[:, a + 4:a + 5], as_[:, a + 1:a + 2], -1.0, None, ALU.mult).then_inc(q_s, 1)

            def norm(u):
                grp, i, h = units[u]
                nk = P * (i + 1)
                s, a = SP_[u % 3], 16 * (u % 4)
                v.wait_ge(q_e, u + 1)
                r0, r1 = (0, 3) if grp == "A" else (1, 2)
                link(V.tensor_scalar(as_[:, a + 6 + r0:a + 6 + r1], as_[:, a + 6 + r0:a + 6 + r1], 1e-30, None, ALU.max))
                link(V.reciprocal(as_[:, a + 9 + r0:a + 9 + r1], as_[:, a + 6 + r0:a + 6 + r1]))
                if grp == "A":
                    link(V.tensor_tensor(as_[:, a + 9:a + 12], as_[:, a + 9:a + 12], gateP[:, 24 * i + h:24 * i + h + 17:8], ALU.mult))
                parts = ((1024, 8 * i + 7, 0), (512, nk, 2), (0, nk, 1)) if grp == "A" else ((0, nk, 1),)
                for off, n, r in parts:
                    last = V.tensor_scalar(s[:, off:off + n], s[:, off:off + n], as_[:, a + 9 + r:a + 10 + r], None, ALU.mult)
                last.then_inc(q_p, 1)

            def take_win(u):
                grp, i, h = units[u]
                if grp != "A":
                    return
                v.wait_ge(q_t, u + 1)
                if u >= 2:
                    v.wait_ge(q_o, u - 1)
                n = 8 * i + 7
                V.tensor_copy(PTP[u % 2][0:n, 1024:1024 + P], bank[5][0:n, 0:P])
                V.tensor_copy(PTP[u % 2][:, 512:512 + P * (i + 1)], bank[4][:, 0:P * (i + 1)]).then_inc(q_td, 1)

            def gated(u):
                grp, i, h = units[u]
                v.wait_ge(q_o, u + 1)
                m = mix3[:, h if grp == "A" else 12 + h, P * i:P * (i + 1)]
                V.tensor_tensor(m, bank[6 + u % 2][:, 0:P], m, ALU.mult).then_inc(q_m, 1)

            NU = len(units)
            for n in range(NU + 3):
                if n < NU:
                    scores(n)
                if 0 <= n - 1 < NU:
                    norm(n - 1)
                if 0 <= n - 2 < NU:
                    take_win(n - 2)
                if 0 <= n - 3 < NU:
                    gated(n - 3)
            end_phase()

            after(v, 3)
            for n in range(1, 32, 2):
                v.wait_ge(kb_tr, n + 1)
                if n >= 4:
                    v.wait_ge(kb_mm, n - 3)
                V.tensor_copy(ixT[n % 4][:, :], bank[6][0:ID, :]).then_inc(kb_d, 1)
            for f in range(5):
                v.wait_ge(si_ps, f + 2)
                if f < 4:
                    link(V.tensor_copy(wrk[:, 512 * f:512 * f + 512], bank[f][:, :]))
                else:
                    link(V.tensor_tensor(wrk[:, PAST:LS], bank[4][:, 0:TS], con[:, K_BM:K_BM + TS], ALU.add))
            end_phase()

            after(v, 4)
            for n in range(18):
                for i in range(1, 8, 2):
                    if n < 16:
                        take_rows(v, V.tensor_copy, 8 * n + i, xt_d)
                if 0 <= n - 2 < 16:
                    g = n - 2
                    kv, b = g // 8, g % 8
                    if kv == 0:
                        v.wait_ge(kc_std, g + 1)
                        link(V.reciprocal(cx[:, 256:510], cx[:, 256:510]))
                        V.scalar_tensor_tensor(out=v3(kc, "p (b h c) -> p b h c", b=DB, h=2)[:, b, :, 0:NCS], in0=cx[:, 0:254].rearrange("p (h c) -> p h c", h=2),
                                               scalar=vecT[:, V_AK:V_AK + 1], in1=cx[:, 256:510].rearrange("p (h c) -> p h c", h=2), op0=ALU.mult, op1=ALU.mult).then_inc(kc_ok, 1)
                    else:
                        v.wait_ge(kc_ps, g + 1)
                        V.tensor_tensor(v3(vc, "p (b h c) -> p b h c", b=DB, h=2)[0:NCS, b], bank[6][0:NCS, 0:256].rearrange("p (h c) -> p h c", h=2),
                                        gk[0:NCS, 3 * P:4 * P].unsqueeze(1).broadcast_to([NCS, 2, P]), ALU.add).then_inc(kc_ok, 1)
                if n < 16:
                    topk(wrk[:, :], st[:, 48:56], 2)
            V.tensor_scalar(wrk[:, :], wrk[:, :], MARK, NEG, ALU.not_equal, ALU.mult)
            end_phase()

            after(v, 5)
            v.wait_ge(sb_in, 16 * 24)
            for u in range(3):
                link(V.tensor_tensor(nbias[:, u * TS:(u + 1) * TS].rearrange("p (b t) -> p b t", t=DT),
                                     sbias[u][:, PAST:PAST + DT].unsqueeze(1).broadcast_to([P, DB, DT]),
                                     con[:, K_BM:K_BM + TS].rearrange("p (b t) -> p b t", t=DT), ALU.add))
            gt = 32
            n = 0
            for u in range(3):
                nb = 40 if u < 2 else 32
                for x in range(nb):
                    if u < 2 and x == 8:
                        early(v, V, u, link, ttr)
                    if u < 2 and x == 16:
                        mid(v, V, u, link)
                    if gt % 2 == 1:
                        v.wait_ge(kb_tr, gt + 1)
                        if n >= 4:
                            v.wait_ge(kb_mm, 32 + n - 3)
                        V.tensor_copy(kT[n % 4][:, :], bank[6][:, :]).then_inc(kb_d, 1)
                    gt += 1
                    n += 1
                late(v, V, u, link, ttr)
                for gi, src in enumerate(pgroups(u)):
                    if gt % 2 == 1:
                        v.wait_ge(kb_tr, gt + 1)
                        take_p(v, V.tensor_copy, u, gi, src, kb_d)
                    gt += 1
                v.wait_ge(pv_b, (10, 20, 28)[u])
                for g in range(4):
                    m = mix3[:, 4 * u + g if u < 2 else 12 + g, T:TT]
                    last = V.tensor_tensor(m, bank[7][:, g:P:4], m, ALU.mult)
                last.then_inc(un_x, 1)
            end_phase()

            after(v, 6)
            v.wait_ge(xr_in, 32)

            def y_rows(nb):
                c, j = nb // 2, nb % 2
                v.wait_ge(y_tr, nb + 1)
                if c >= 2 and j == 0:
                    v.wait_ge(y_out, 32 * (c - 1))
                y5 = v3(yrow[c % 2], "p (i d) -> p i d", i=5)
                x5 = v3(xres, "p (i d) -> p i d", i=5)
                V.tensor_tensor(y5[:, 0:QT, j * P:(j + 1) * P], bank[4 + nb % 2][:, :].rearrange("p (i d) -> p i d", i=4), x5[:, 0:QT, nb * P:(nb + 1) * P], ALU.add).then_inc(y_fin, 1)
                V.tensor_tensor(y5[0:TS, QT, j * P:(j + 1) * P], bank[6 + nb % 2][0:TS, 0:P], x5[0:TS, QT, nb * P:(nb + 1) * P], ALU.add).then_inc(y_fin, 1)

            for nb in range(KD):
                v.wait_ge(y_ps, nb + 1)
                if nb >= 4:
                    v.wait_ge(y_tr, nb - 3)
                s = yT[nb % 4]
                gate = mod3[:, 32 + nb, 0:1]
                V.tensor_scalar(s[:, 0:HALF], bank[2 * (nb % 2)][:, 0:HALF], gate, None, ALU.mult)
                V.tensor_scalar(s[:, HALF:T], bank[2 * (nb % 2) + 1][:, 0:T - HALF], gate, None, ALU.mult)
                V.tensor_tensor(s[:, T:TT].rearrange("p (b t) -> p b t", t=DT), bank[2 * (nb % 2) + 1][:, T - HALF:HALF].rearrange("p (b t) -> p b t", t=DT),
                                bc(mod3[:, 32 + nb, 1:9], DT), ALU.mult).then_inc(y_ev, 1)
                if nb >= 1:
                    y_rows(nb - 1)
            y_rows(KD - 1)


_INS = ["x_prompt", "x_sample", "cache_a_kv", "cache_c_kv", "cache_c_kidx", "state_a_win", "state_b_pool", "page_table",
        "c_prompt", "c_sample", "rel_bias", "norm_g", "w_ada", "b_ada", "w_in", "w_out", "a_qnorm", "a_knorm",
        "a_cmp_pe", "a_cmp_w1", "a_cmp_b1", "a_cmp_w2", "a_cmp_b2", "b_pool_w", "b_scale", "c_qnorm", "c_knorm"]
_OUTS = [("y_prompt", (1, T, D)), ("y_sample", (DB, DT, D)),
         ("a_kv_p", (1, 1, T, 4, KVH, HD)), ("a_kv_s", (1, DB, DT, 4, KVH, HD)),
         ("c_kv_p", (1, 1, T, 2, HD)), ("c_kv_s", (1, DB, DT, 2, HD)),
         ("c_kidx_p", (1, 1, T, ID)), ("c_kidx_s", (1, DB, DT, ID)),
         ("a_win_p", (1, 1, T, 2, KVH, HD)), ("a_win_s", (1, DB, WIN, 2, KVH, HD)),
         ("b_pool_p", (1, 1, 15, 512)), ("b_pool_s", (1, DB, 15, 512))]


def kernel(**inputs):
    import concourse.bacc as bacc
    from concourse.bass_utils import run_bass_kernel_spmd as run

    nc = bacc.Bacc("TRN2", target_bir_lowering=False, num_devices=1)
    arrays, ins, outs = {}, {}, {}
    for name in _INS:
        arrays[f"in_{name}_dram"] = np.ascontiguousarray(inputs[name])
    for name, a in shape_constants().items():
        arrays[f"in_{name}_dram"] = a
    for name, a in arrays.items():
        ins[name[3:-5]] = nc.dram_tensor(name, a.shape, mybir.dt.from_np(a.dtype), kind="ExternalInput").ap()
    for i, (name, shape) in enumerate(_OUTS):
        outs[name] = nc.dram_tensor(f"out_{i}_dram", shape, F32, kind="ExternalOutput").ap()
    build(nc, ins, outs)
    r = run(nc, [arrays], core_ids=[0])
    return tuple(r.results[0][f"out_{i}_dram"] for i in range(len(_OUTS)))
```

```python
from contextlib import ExitStack
import math

import numpy as np

import concourse.bass as bass
from concourse import mybir

F32 = mybir.dt.float32
I32 = mybir.dt.int32
ACT = mybir.ActivationFunctionType
ALU = mybir.AluOpType
AX = mybir.AxisListType

P = 128
D = 2048
KD = D // P
T = 512
QT = T // P
DB, DT = 8, 4
TS = DB * DT
TT = T + TS
HALF = TT // 2
PAST, PAGE = 2048, 128
NPG = PAST // PAGE
NPOOL = 5 * DB * NPG // 4
HD = 128
AH, KVH, G = 8, 2, 4
CH = 4
IH, ID = 4, 64
WIN = 512
NB_, MAXD = 32, 128
LS = PAST + TS
NCS = (PAST + DT) // 16 - 1
NCP = T // 16 - 1
NSB = 33
TOPB = 16
NKR, NVR = 4, 4
KEEP_P, KEEP_S = 128, 256
EPS = 1e-6
NEG = -1e30
FLOOR = -1e29
MARK = -3e38
FORCE = 1e6
SCALE = HD ** -0.5
XOFF = PAST + DT - 1
XL = 2184
TX0 = XOFF - 384 - 127
TXL = 640
SX = 2052

C_AQ, C_AKV, C_GATE, C_ASIL, C_BIN, C_BSIL = 0, 1024, 2560, 2584, 3608, 4120
C_CQ, C_CKV, C_IQ, C_IK, C_IW, C_CSIL = 4632, 5144, 5400, 5656, 5720, 5724
CW = 256

V_BADA, V_G, V_BSC, V_B1, V_B2, V_AQ, V_CQ, V_AK, V_CK = 0, 48, 64, 68, 72, 74, 75, 76, 79
NV = 80
K_ID, K_ONE, K_GRP, K_WM, K_BM, K_WIN, K_DIAG, K_RC, K_M2, K_M3, K_FB = 0, 128, 256, 384, 512, 608, 612, 740, 804, 808, 816
K_EPS = K_FB + 33
NK = K_EPS + 1
NSMALL = 24
HREADY = 2 * KD


def bucket(rel):
    rel = np.maximum(rel, 0)
    exact = NB_ // 2
    relf = np.maximum(rel, exact).astype(np.float32)
    lb = exact + (np.log(relf / np.float32(exact)) / np.float32(math.log(MAXD / exact)) * np.float32(NB_ - exact)).astype(np.int32)
    return np.where(rel < exact, rel, np.minimum(lb, NB_ - 1))


def shape_constants():
    c = np.zeros((P, NK), np.float32)
    p = np.arange(P)
    c[:, K_ID:K_ID + P] = np.eye(P)
    c[:, K_ONE:K_ONE + P] = 1.0
    c[:, K_GRP:K_GRP + P] = p[:, None] // 4 == p[None] // 4
    pb, pi, pt = p // 16, p // 4 % 4, p % 4
    qb, qt, qg = p // 16, p // 4 % 4, p % 4
    c[:, K_WM:K_WM + P] = (pb[:, None] == qb[None]) & (pt[:, None] == qt[None])
    k = np.arange(TS)
    rows_b = (p // 32, 4 + p // 32, qb)
    for u in range(3):
        c[:, K_BM + TS * u:K_BM + TS * (u + 1)] = np.where((k[None] // DT == rows_b[u][:, None]) & (k[None] % DT <= qt[:, None]), 0.0, NEG)
    c[:, K_WIN:K_WIN + 4] = np.where(np.arange(4)[None] < qt[:, None], NEG, 0.0)
    c[:, K_DIAG:K_DIAG + P] = np.where(p[None] <= p[:, None], 0.0, NEG)
    for g in range(4):
        c[:, K_RC + 16 * g:K_RC + 16 * g + 16] = 1.0 / np.minimum(np.arange(16) + 1, 2 << g)
    c[:, K_M2:K_M2 + 4] = np.arange(4)[None] == pi[:, None]
    c[:, K_M3:K_M3 + 8] = np.arange(8)[None] == (4 * (p // 16 % 2) + qg)[:, None]
    c[:, K_EPS] = EPS
    c[:, [K_FB, K_FB + 31, K_FB + 32]] = FORCE
    e = np.zeros((TS, 3 * P), np.float32)
    kb, kt = k // DT, k % DT
    for u in range(2):
        e[:, P * u:P * (u + 1)] = (kb[:, None] == rows_b[u][None]) & (kt[:, None] == qt[None])
    e[:, 2 * P:] = (kb[:, None] == pb[None]) & (kt[:, None] == pt[None])
    rel = XOFF - np.arange(XL)
    oh = np.zeros((NB_ + 1, XL), np.float32)
    oh[bucket(rel), np.arange(XL)] = (rel >= 0)
    oh[NB_] = np.where(rel < 0, NEG, 0.0)
    return {"constants": c, "expanders": e, "bucket_rows": oh}


def plan_projection():
    chunks, jobs = [], []

    def rows(kind, parts):
        chunks.append(parts)
        jobs.extend((kind, 0, t, len(chunks) - 1) for t in range(QT + 1))

    def cols(kind, first, blocks):
        for b in range(0, blocks, 2):
            chunks.append([(first + b * P, CW)])
            jobs.extend((kind, b + j, j, len(chunks) - 1) for j in range(2))

    rows("small", [(C_GATE, 24), (C_IK, ID + IH)])
    cols("iq", C_IQ, 2)
    rows("ckv", [(C_CKV, CW)])
    for n, kind in enumerate(("kcmp", "vcmp", "kslc", "vslc", "kwin", "vwin")):
        rows(kind, [(C_AKV + n * CW, CW)])
    cols("cq", C_CQ, CH)
    cols("aq", C_AQ, AH)
    cols("bin", C_BIN, 4)
    cols("bsil", C_BSIL, 4)
    cols("asil", C_ASIL, AH)
    cols("csil", C_CSIL, 4)
    return chunks, jobs


ROW_KINDS = ("small", "ckv", "kcmp", "vcmp", "kslc", "vslc", "kwin", "vwin")
SIL_AT = {"asil": 0, "bsil": 8, "csil": 12}


class Count:

    def __init__(self, eng, sem):
        self.eng, self.sem, self.n = eng, sem, 0

    def __call__(self, ins):
        ins.then_inc(self.sem, 1)
        self.n += 1
        return self.n

    def wait(self):
        self.eng.wait_ge(self.sem, self.n)

    def link(self, ins):
        self(ins)
        self.wait()


def build(nc, I, O, debug=None):
    chunks, jobs = plan_projection()
    njobs = len(jobs)
    with ExitStack() as ctx:
        sems = {}

        def sem(name):
            sems[name] = ctx.enter_context(nc.semaphore(name))
            return sems[name]

        top = [16512]
        hi = [top[0]]

        def sb(name, rows, words, dt=F32, at=None):
            where = top[0] if at is None else at
            words_r = -(-words // 8) * 8
            t = nc.alloc_sbuf_tensor_at(name, [rows, words], dt, offset=where)
            if at is None:
                top[0] += 4 * words_r
                assert top[0] <= 229344, (name, top[0])
            return t

        def region(start):
            pos = [start]

            def place(name, rows, words, dt=F32):
                t = sb(name, rows, words, dt, at=pos[0])
                pos[0] += 4 * (-(-words // 8) * 8)
                assert pos[0] <= 229344, (name, pos[0])
                return t
            return place, pos

        con = sb("con", P, NK)
        expd = sb("expd", TS, 3 * P)
        vecT = sb("vecT", P, NV)
        peT = sb("peT", P, 64)
        modT = sb("modT", P, 48 * 9)
        ascale = sb("ascale", P, KD * 9)
        gk = sb("gk", P, 4 * P)
        relb = sb("relb", NB_ + 1, 12)
        gateP = sb("gateP", P, QT * 24)
        gateS0 = sb("gateS0", TS, 24)
        gateS = sb("gateS", P, 6)
        gateS1 = sb("gateS1", P, 48)
        iwP = sb("iwP", P, QT * 4)
        iwS = sb("iwS", TS, 4)
        wiS = sb("wiS", P, 4)
        zq = sb("zq", P, 3 * 256)
        qf = sb("qf", P, P)
        zi = sb("zi", ID, DB * 32)
        qfi = sb("qfi", ID, P)
        ksN = sb("ksN", P, 5 * TS)
        kiN = sb("kiN", P, TS)
        vN = sb("vN", TS, 2 * CW)
        cvN = sb("cvN", TS, P)
        wsel = sb("wsel", P, P)
        maskC = sb("maskC", P, 256 + 384 + 512)
        wpool = sb("wpool", P, 4 * P)
        ptab = sb("ptab", 1, DB * NPG, I32)
        st = sb("st", P, 64)
        b1e = sb("b1e", P, 4)
        mix = sb("mix", P, KD * TT)
        base_free = top[0]

        data, dpos = region(base_free)
        aqT = data("aqT", P, AH * T)
        cqT = data("cqT", P, CH * T)
        kslcT = data("kslcT", P, KVH * T)
        kwinT = data("kwinT", P, KVH * T)
        ckT = data("ckT", P, T)
        vnat = data("vnat", P, QT * 2 * CW)
        cvnat = data("cvnat", P, QT * P)
        kcP = data("kcP", P, KVH * 32)
        vcP = data("vcP", 32, KVH * P)
        cmpT = data("cmpT", P, 2 * KVH * T)
        xrow = [sb(f"xrow{i}", P, D, at=base_free + i * 4 * D) for i in range(2)]
        crow = sb("crow", 9, D, at=base_free + 2 * 4 * D)
        vrow = sb("vrow", NV, P, at=base_free + 3 * 4 * D)
        prow = sb("prow", 64, P, at=base_free + 3 * 4 * D + 4 * P)
        cT = sb("cT", P, KD * 9 * 2, at=base_free + 3 * 4 * D + 8 * P)
        btmp = sb("btmp", 12, XL, at=base_free + 3 * 4 * D + 8 * P + 1280)
        ohr = sb("ohr", NB_ + 1, XL, at=base_free + 3 * 4 * D + 8 * P + 1280 + 4 * XL)
        bst = sb("bst", DB * 15, 512, at=base_free + 3 * 4 * D + 8 * P + 1280 + 8 * XL)
        assert 2048 + 3 * 4 * D + 8 * P + 1280 + 8 * XL <= dpos[0] - base_free

        big0 = dpos[0]
        big, bpos = region(big0)
        hT = big("hT", P, KD * TT)
        wbuf = [big(f"wbuf{i}", P, KD * CW) for i in range(2)]
        big_end = bpos[0]
        ext, epos = region(big_end)
        iqh = ext("iqh", ID, 2 * TS)
        iqT = ext("iqT", P, 2 * TT)
        ikT = ext("ikT", P, T)
        bT = ext("bT", P, 4 * (16 + T))
        bS = ext("bS", P, 4 * DB * 20)
        stage = [ext(f"stage{i}", P, CW) for i in range(4)]
        sq = ext("sq", P, TT)
        rs = ext("rs", P, TT)
        wk = ext("wk", P, T)
        w1p, _ = region(big0)
        w1P = [w1p(f"w1P{i}", P, 32 * 256) for i in range(2)]
        w2p, _ = region(big_end)
        w2P = w2p("w2P", P, 2 * 2 * P)
        hidP = w2p("hidP", P, 4 * 64)
        cxP = w2p("cxP", P, 3 * 64)
        att, apos = region(big0)
        bias = att("bias", P, 12 * T)
        SP_ = [att(f"SP{i}", P, 1056) for i in range(3)]
        PTP = [att(f"PTP{i}", P, 1152) for i in range(2)]
        as_ = att("as_", P, 64)
        smp, spos = region(base_free)
        kc = smp("kc", P, DB * KVH * P)
        vc = smp("vc", P, DB * KVH * P)
        wrk = smp("wrk", P, LS)
        s2 = spos[0]
        cm, _ = region(s2)
        w1S = [cm(f"w1S{i}", P, 32 * 256) for i in range(2)]
        xt = [cm(f"xt{i}", P, 2 * PAST) for i in range(2)]
        xnat = [cm(f"xnat{i}", P, 4 * 256) for i in range(4)]
        hid = [cm(f"hid{i}", P, 2 * 256) for i in range(1)]
        w2S = cm("w2S", P, 2 * 2 * P)
        cx = cm("cx", P, 2 * 256)
        ix, _ = region(s2)
        ixn = [ix(f"ixn{i}", P, 4 * ID) for i in range(8)]
        ixT = [ix(f"ixT{i}", ID, 512) for i in range(4)]
        ixr = ix("ixr", P, LS)
        at_, tpos = region(s2)
        sbias = [at_(f"sbias{i}", P, SX) for i in range(2)]
        sbias = [sbias[0], sbias[0], sbias[1]]
        nbias = at_("nbias", P, 3 * TS)
        kn = [at_(f"kn{i}", P, 1024) for i in range(NKR)]
        kT = [at_(f"kT{i}", P, 512) for i in range(4)]
        vr = [at_(f"vr{i}", P, NPG * P) for i in range(NVR)]
        win_v = at_("win_v", P, 4 * 1024)
        sS = at_("sS", P, LS)
        sW = at_("sW", P, WIN + TS)
        sC = at_("sC", P, P)
        pT = at_("pT", P, 23 * P)
        imp = at_("imp", P, 5 * 40)
        bmask = at_("bmask", P, 2 * NSB)
        us = at_("us", P, 64)
        ou, _ = region(base_free)
        wo = [ou(f"wo{i}", P, KD * CW) for i in range(3)]
        yT = [ou(f"yT{i}", P, TT) for i in range(4)]
        xres = ou("xres", P, 5 * D)
        yrow = [ou(f"yrow{i}", P, 5 * CW) for i in range(2)]
        tmp, _ = region(big0)
        pls = tmp("pls", P, 1400)
        prw = tmp("prw", TS, 1024)

        ident = con[:, K_ID:K_ID + P]
        ones = con[:, K_ONE:K_ONE + P]

        bank = [ctx.enter_context(nc.psum_tensor(f"bank{i}", [P, 512], F32)) for i in range(8)]

        d_rows = nc.dram_tensor("bias_rows", (12, XL), F32).ap()
        d_rep = nc.dram_tensor("bias_repeated", (P, 12 * TXL), F32).ap()
        d_smp = nc.dram_tensor("bias_sample", (3, 16, SX), F32).ap()

        s_con = sem("s_con")
        s_x = [sem(f"s_x{i}") for i in range(2)]
        x_free = sem("x_free")
        dve = sem("dve")
        act_ = sem("act_")
        ph_pe, ph_act, ph_dve, ph_pool = (sem(n) for n in ("ph_pe", "ph_act", "ph_dve", "ph_pool"))
        ixp_d, ixp_r, ixp_a, r_std, g_e, gs_in, iqh_in, pl_y2, pst_t, pst_ev, un_w, h_copied = (
            sem(n) for n in ("ixp_d", "ixp_r", "ixp_a", "r_std", "g_e", "gs_in", "iqh_in", "pl_y2", "pst_t", "pst_ev", "un_w", "h_copied"))
        su_tr = sem("su_tr")
        su_ev = sem("su_ev")
        c_T = sem("c_T")
        c_e = sem("c_e")
        c_s = sem("c_s")
        b_ps = sem("b_ps")
        b_ev = sem("b_ev")
        b_dma = sem("b_dma")
        x_ss = sem("x_ss")
        x_std = sem("x_std")
        x_n = sem("x_n")
        x_tr = sem("x_tr")
        x_ev = sem("x_ev")
        w_in_ = [sem(f"w_in{i}") for i in range(2)]
        w_free = sem("w_free")
        ada_ps = sem("ada_ps")
        h_ready = sem("h_ready")
        m_done = sem("m_done")
        m_free = sem("m_free")
        n_sq = sem("n_sq")
        n_sum = sem("n_sum")
        n_std = sem("n_std")
        st_rdy = sem("st_rdy")
        a_done = sem("a_done")
        a_free = sem("a_free")
        st_out = [sem(f"st_out{i}") for i in range(4)]
        sil_e = sem("sil_e")
        d_out = sem("d_out")
        o_rdy = sem("o_rdy")
        ix_ps = sem("ix_ps")
        ix_rl = sem("ix_rl")
        ix_us = sem("ix_us")
        pl_d = sem("pl_d")
        pl_y = sem("pl_y")
        pl_t = sem("pl_t")
        pl_c = sem("pl_c")
        w1_in = sem("w1_in")
        cp_ps = sem("cp_ps")
        cp_ev = sem("cp_ev")
        at_in = sem("at_in")
        q_ps = sem("q_ps")
        q_s = sem("q_s")
        q_e = sem("q_e")
        q_p = sem("q_p")
        q_t = sem("q_t")
        q_ta = sem("q_ta")
        q_td = sem("q_td")
        q_o = sem("q_o")
        q_m = sem("q_m")
        si_ps = sem("si_ps")
        si_ev = sem("si_ev")
        kb_in = [sem(f"kb_in{i}") for i in range(8)]
        kb_tr = sem("kb_tr")
        kb_a = sem("kb_a")
        kb_d = sem("kb_d")
        kb_mm = sem("kb_mm")
        xn_in = [sem(f"xn_in{i}") for i in range(4)]
        xn_tr = sem("xn_tr")
        xt_a = sem("xt_a")
        xt_d = sem("xt_d")
        hd_ps = sem("hd_ps")
        hd_ev = sem("hd_ev")
        kc_ps = sem("kc_ps")
        kc_x = sem("kc_x")
        kc_sum = sem("kc_sum")
        kc_std = sem("kc_std")
        kc_ok = sem("kc_ok")
        w1s_in = sem("w1s_in")
        sb_in = sem("sb_in")
        vr_in = [sem(f"vr_in{i}") for i in range(NVR)]
        kk_in = [sem(f"kk_in{i}") for i in range(NKR)]
        wv_in = sem("wv_in")
        pv_b = sem("pv_b")
        un_ps = sem("un_ps")
        un_s = sem("un_s")
        un_m = sem("un_m")
        un_e = sem("un_e")
        un_p = sem("un_p")
        un_t = sem("un_t")
        un_te = sem("un_te")
        un_o = sem("un_o")
        un_x = sem("un_x")
        im_ps = sem("im_ps")
        im_in = sem("im_in")
        im_bc = sem("im_bc")
        wo_in = [sem(f"wo_in{i}") for i in range(3)]
        xr_in = sem("xr_in")
        y_ps = sem("y_ps")
        y_ev = sem("y_ev")
        y_tr = sem("y_tr")
        y_fin = sem("y_fin")
        y_out = sem("y_out")
        block = ctx.enter_context(nc.Block())

        def v3(tensor, pattern, /, **k):
            return tensor[:, :].rearrange(pattern, **k)

        hT3 = v3(hT, "p (k t) -> p k t", t=TT)
        mix3 = v3(mix, "p (k t) -> p k t", t=TT)
        mod3 = v3(modT, "p (n b) -> p n b", b=9)
        asc3 = v3(ascale, "p (n b) -> p n b", b=9)
        aqT3 = v3(aqT, "p (h t) -> p h t", t=T)
        cqT3 = v3(cqT, "p (h t) -> p h t", t=T)
        iqT3 = v3(iqT, "p (h t) -> p h t", t=TT)
        bT3 = v3(bT, "p (g t) -> p g t", t=16 + T)
        bS4 = v3(bS, "p (g b t) -> p g b t", g=4, t=20)
        cmp4 = v3(cmpT, "p (c h t) -> p c h t", c=2, h=KVH)
        vnat3 = v3(vnat, "p (i c) -> p i c", c=2 * CW)
        MOFF = (0, 0, 256, 640)

        idx_of = {}
        for j, (kind, b, t, c) in enumerate(jobs):
            idx_of[(kind, b, t)] = j
        normT = [j for j, (k, b, t, c) in enumerate(jobs) if k in ("cq", "aq")]
        staged = [j for j, (k, b, t, c) in enumerate(jobs) if k in ("small", "ckv", "kcmp", "vcmp", "kslc", "kwin")]
        turned = [j for j in staged if not (jobs[j][0] in ("kcmp", "vcmp") and jobs[j][2] == QT)]
        silj = [j for j, (k, b, t, c) in enumerate(jobs) if k in SIL_AT]
        rownorm = [j for j, (k, b, t, c) in enumerate(jobs) if k in ("ckv", "kslc", "kwin")]

        def turns(j):
            return 2 if jobs[j][0] in ("kcmp", "vcmp", "kslc", "kwin") else 1

        def width(t):
            return P if t < QT else TS

        def wchunk(c, w):
            return wbuf[c % 2][:, 0:KD * w].rearrange("p (k n) -> p k n", n=w)

        cwidth = [sum(w for _, w in parts) for parts in chunks]
        cparts = [len(parts) for parts in chunks]
        NADA = 3 * D // CW
        need, count = {}, [0, 0]
        for n in range(NADA + len(chunks)):
            parts = 1 if n < NADA else cparts[n - NADA]
            count[n % 2] += 16 * parts
            need[n] = count[n % 2]

        def w_of(n):
            return need[NADA + n] if n >= 0 else None


        turned_set, staged_set = set(turned), set(staged)
        last_job = {c: j for j, (_, _, _, c) in enumerate(jobs)}
        ix_slot, n_ = {}, 0
        for i in range(1, QT):
            for x in range(4):
                ix_slot[idx_of[("kcmp", 0, 0)] + 8 * (i - 1) + x] = ("dots", i, x, n_)
                ix_slot[idx_of[("kcmp", 0, 0)] + 8 * (i - 1) + 4 + x] = ("topk", i, x)
                n_ += 1
        units = [("A", i, h) for i in range(QT) for h in range(AH)] + [("C", i, h) for i in range(QT) for h in range(CH)]
        NUA = QT * AH
        sblocks, kloads = [], []
        for u in range(2):
            for kind, nq in (("win", 1), ("slc", 4)):
                for b in range(4 * u, 4 * u + 4):
                    for q in range(nq):
                        for k in range(KVH):
                            sblocks.append((u, kind, b, q, k, len(kloads)))
                        kloads.append((1 if kind == "win" else 4, len(sblocks) - 1, (u, kind, b, q)))
        for b in range(DB):
            for q in range(4):
                sblocks.append((2, "c", b, q, 0, len(kloads)))
                kloads.append((4, len(sblocks) - 1, (2, "c", b, q)))
        kneed, kc_ = [], [0] * 8
        for m in range(32):
            kc_[m % 8] += 64
            kneed.append(kc_[m % 8])
        kkneed, kc_ = [], [0] * NKR
        for m, (k_, _, _) in enumerate(kloads):
            kc_[m % NKR] += 16 * k_
            kkneed.append(kc_[m % NKR])
        vneed, vc_ = [], [0] * NVR
        for m in range(24):
            vc_[m % NVR] += 16 * (8 if m < 16 else 16)
            vneed.append(vc_[m % NVR])
        NBLK = (40, 40, 32)
        FIRSTB = (0, 40, 80)
        STEPS = (("head", 0), ("body", 0), ("head", 1), ("turn", 0), ("body", 1), ("head", 2), ("turn", 1), ("body", 2), ("turn", 2))

        def blocks_of(step, u):
            f = FIRSTB[u]
            return range(f, f + 8) if step == "head" else range(f + 8, f + NBLK[u])

        def pgroups(u):
            t = [(sS[:, i * P:(i + 1) * P], P) for i in range(16)] + [(sS[:, PAST:LS], TS)]
            if u < 2:
                t += [(sW[:, i * P:(i + 1) * P], P) for i in range(4)] + [(sW[:, WIN:WIN + TS], TS), (sC[:, 0:NCS], NCS)]
            return [t[i:i + 4] for i in range(0, len(t), 4)]

        kb_gt, g_ = {}, 32
        for step, u in STEPS:
            if step == "turn":
                g_ += len(pgroups(u))
            else:
                for n in blocks_of(step, u):
                    kb_gt[n] = g_
                    g_ += 1

        def bc(ap, n):
            return ap.unsqueeze(2).broadcast_to([ap.shape[0], ap.shape[1], n])

        def after(eng, n):
            eng.wait_ge(ph_pe, n)
            eng.wait_ge(ph_act, n)
            eng.wait_ge(ph_dve, n)
            if n == 1:
                eng.wait_ge(ph_pool, 1)

        def turned_to(kind, t, x):
            a, w = t * P, width(t)
            if kind == "small":
                return ikT[:, a:a + P] if t < QT else kiN[:, :]
            if kind == "ckv":
                return ckT[:, a:a + P] if t < QT else ksN[:, 4 * TS:5 * TS]
            if kind in ("kcmp", "vcmp"):
                return cmp4[:, 0 if kind == "kcmp" else 1, x, a:a + P]
            o = 0 if kind == "kslc" else 2
            return (kslcT, kwinT)[o // 2][:, x * T + a:x * T + a + P] if t < QT else ksN[:, (o + x) * TS:(o + x + 1) * TS]

        def evac_x(eng, A, t):
            w = width(t)
            for q in range(4):
                g = 4 * t + q
                eng.wait_ge(x_tr, g + 1)
                eng.copy(hT3[:, 4 * q:4 * q + 4, t * P:t * P + w], bank[g % 4][:, 0:4 * w].rearrange("p (k t) -> p k t", k=4)).then_inc(x_ev, 1)

        def take_rows(eng, copy, x, s):
            n, q, h = x // 8, x % 8 // 2, x % 2
            eng.wait_ge(xn_tr, x + 1)
            if n >= 2:
                eng.wait_ge(hd_ps, n - 1)
            o = v3(xt[n % 2], "p (h s c) -> p h c s", h=2, s=16)[:, h, 32 * q:32 * q + 32, :]
            copy(o, bank[4 + x % 2][:, :].rearrange("p (c s) -> p c s", s=16)).then_inc(s, 1)

        def take_p(eng, copy, u, gi, src, s):
            if u >= 1:
                eng.wait_ge(pv_b, 8 * u)
            b, i = bank[5 + (s is kb_d)], 0
            while i < len(src):
                j = i
                while j < len(src) and src[j][1] == src[i][1]:
                    j += 1
                r = src[i][1]
                last = copy(pT[0:r, (4 * gi + i) * P:(4 * gi + j) * P], b[0:r, i * P:j * P])
                i = j
            last.then_inc(s, 1)

        def take_k(eng, copy, n, gt, s):
            eng.wait_ge(kb_tr, gt + 1)
            if n >= 4:
                eng.wait_ge(kb_mm, 32 + n - 3)
            copy(kT[n % 4][:, :], bank[5 + gt % 2][:, :]).then_inc(s, 1)

        def unit_exps(eng, A, u, when):
            if when == "early":
                eng.wait_ge(un_w, u + 1)
                A(sC[:, 0:NCS], sC[:, 0:NCS], ACT.Exp, bias=us[:, 4:5], accum_out=us[:, 8:9])
                A(sW[:, :], sW[:, :], ACT.Exp, bias=us[:, 5:6], accum_out=us[:, 9:10]).then_inc(un_e, 1)
            else:
                eng.wait_ge(un_s, u + 1)
                A(sS[:, :], sS[:, :], ACT.Exp, bias=us[:, 6:7], accum_out=us[:, 10:11]).then_inc(un_e, 1)

        def early(v, V, u, link, ttr):
            v.wait_ge(un_ps, 2 * u + 1)
            link(V.tensor_tensor(sW[:, 0:WIN], bank[0][:, :], sbias[u][:, PAST - WIN:PAST], ALU.add))
            link(V.tensor_tensor(sW[:, WIN:WIN + TS], bank[4][:, 32:64], nbias[:, u * TS:(u + 1) * TS], ALU.add))
            link(V.tensor_tensor(sW[:, 0:4], sW[:, 0:4], con[:, K_WIN:K_WIN + 4], ALU.add))
            link(ttr(sC[:, 0:NCS], bank[4][:, 64:64 + NCS], sbias[u][:, 31:31 + 16 * (NCS - 1) + 1:16], us[:, 0:1]))
            link(V.tensor_reduce(us[:, 1:2], sW[:, :], AX.X, ALU.max))
            V.tensor_scalar(us[:, 4:6], us[:, 0:2], -1.0, None, ALU.mult).then_inc(un_w, 1)

        def mid(v, V, u, link):
            v.wait_ge(un_e, 2 * u + 1)
            link(V.tensor_scalar(us[:, 12:14], us[:, 8:10], 1e-30, None, ALU.max))
            link(V.reciprocal(us[:, 12:14], us[:, 12:14]))
            V.tensor_scalar(sC[:, 0:NCS], sC[:, 0:NCS], us[:, 12:13], None, ALU.mult).then_inc(im_in, 1)
            v.wait_ge(im_in, u + 1)

        def late(v, V, u, link, ttr):
            if u < 2:
                v.wait_ge(im_ps, u + 1)
                link(V.memset(imp[:, :], 0.0))
                link(V.tensor_copy(imp[:, 1:1 + NCS], bank[7][:, 0:NCS]))
                at = [imp[:, k:k + 4 * (NSB - 1) + 1:4] for k in range(5)]
                t = imp[:, 136:136 + NSB]
                link(V.tensor_tensor(t, at[1], at[2], ALU.add))
                link(V.tensor_tensor(t, t, at[3], ALU.add))
                link(V.scalar_tensor_tensor(out=t, in0=t, scalar=2.0, in1=at[0], op0=ALU.mult, op1=ALU.add))
                link(V.tensor_tensor(t, t, at[4], ALU.add))
                link(V.tensor_tensor(t, t, con[:, K_FB:K_FB + NSB], ALU.max))
                for _ in range(TOPB // 8):
                    link(V.max(us[:, 24:32], t))
                    link(V.match_replace(t, us[:, 24:32], t, MARK))
                link(V.tensor_scalar(bmask[:, 0:NSB], t, MARK, NEG, ALU.not_equal, ALU.mult))
                link(V.tensor_scalar(sC[:, 0:NCS], sC[:, 0:NCS], gateS[:, u:u + 1], None, ALU.mult))
                link(V.tensor_scalar(sW[:, :], sW[:, :], us[:, 13:14], gateS[:, 4 + u:5 + u], ALU.mult, ALU.mult))
            v.wait_ge(un_ps, 2 * u + 2 if u < 2 else 5)
            for f in range(4):
                V.tensor_tensor(sS[:, 512 * f:512 * f + 512], bank[f][:, :], sbias[u][:, 512 * f:512 * f + 512], ALU.add)
            link(V.tensor_tensor(sS[:, PAST:LS], bank[4][:, 0:TS], nbias[:, u * TS:(u + 1) * TS], ALU.add))
            if u < 2:
                s3 = sS[:, 0:PAST].rearrange("p (n s) -> p n s", s=64)
                link(V.tensor_tensor(s3, s3, bc(bmask[:, 0:32], 64), ALU.add))
                link(V.tensor_reduce(us[:, 2:3], sS[:, :], AX.X, ALU.max))
            else:
                link(ttr(sS[:, :], sS[:, :], wrk[:, :], us[:, 2:3]))
            V.tensor_scalar(us[:, 6:7], us[:, 2:3], -1.0, None, ALU.mult).then_inc(un_s, 1)
            v.wait_ge(un_e, 2 * u + 2 if u < 2 else 5)
            link(V.tensor_scalar(us[:, 14:15], us[:, 10:11], 1e-30, None, ALU.max))
            link(V.reciprocal(us[:, 14:15], us[:, 14:15]))
            if u < 2:
                link(V.tensor_scalar(us[:, 14:15], us[:, 14:15], gateS[:, 2 + u:3 + u], None, ALU.mult))
            V.tensor_scalar(sS[:, :], sS[:, :], us[:, 14:15], None, ALU.mult).then_inc(un_p, 1)

        def pool_out(v, V, g):
            v.wait_ge(pl_y, g + 1)
            for f in range(2):
                m = mix3[:, 8 + g, f * HALF:(f + 1) * HALF]
                last = V.scalar_tensor_tensor(out=m, in0=bank[2 * (g % 2) + f][:, 0:HALF], scalar=vecT[:, V_BSC + g:V_BSC + g + 1], in1=m, op0=ALU.mult, op1=ALU.mult)
            last.then_inc(pl_y2, 1)

        @block.sync
        def _(sp):
            small = [(con[:, :], I["constants"]), (expd[:, :], I["expanders"]), (ohr[:, :], I["bucket_rows"]),
                     (vrow[V_BADA:V_BADA + 48, :], I["b_ada"].rearrange("a (n p) -> (a n) p", p=P)),
                     (vrow[V_G:V_G + 16, :], I["norm_g"].rearrange("a (n p) -> (a n) p", p=P)),
                     (vrow[V_BSC:V_BSC + 4, :], I["b_scale"].rearrange("a (n p) -> (a n) p", p=P)),
                     (vrow[V_B1:V_B1 + 4, :], I["a_cmp_b1"].rearrange("a c (n p) -> (a c n) p", p=P)),
                     (vrow[V_B2:V_B2 + 2, :], I["a_cmp_b2"].rearrange("a c p -> (a c) p")),
                     (vrow[V_AQ:V_AQ + 1, :], I["a_qnorm"]), (vrow[V_CQ:V_CQ + 1, :], I["c_qnorm"]),
                     (vrow[V_AK:V_AK + 3, :], I["a_knorm"].rearrange("a c p -> (a c) p")),
                     (vrow[V_CK:V_CK + 1, :], I["c_knorm"]),
                     (prow[:, :], I["a_cmp_pe"].rearrange("a c s p -> (a c s) p")),
                     (crow[0:1, :], I["c_prompt"]), (crow[1:9, :], I["c_sample"]),
                     (relb[0:NB_, :], I["rel_bias"]), (relb[NB_:NB_ + 1, :], I["constants"][0:1, K_ONE:K_ONE + 12]),
                     (ptab[:, :], I["page_table"].rearrange("(a b) n -> a (b n)", a=1)),
                     (bst[:, :], I["state_b_pool"].rearrange("a b t c -> (a b t) c")),
                     (v3(wpool, "p (g d) -> p g d", g=4), I["b_pool_w"][0].rearrange("g c d -> c g d"))]
            for n, (o, i) in enumerate(small):
                sp.dma_start(o, i).then_inc(s_con, 16)
            for n, src in enumerate((I["a_knorm"][0, 1:2, :], I["a_knorm"][0, 2:3, :], I["c_knorm"], I["a_cmp_b2"][0, 1:2, :])):
                sp.dma_start(gk[:, n * P:(n + 1) * P], bass.AP(src.tensor, src.offset, [[0, P], [1, P]])).then_inc(s_con, 16)
            xp = I["x_prompt"].rearrange("a (t p) d -> (a t) p d", p=P)
            for t in range(2):
                sp.dma_start(xrow[t][:, :], xp[t]).then_inc(s_x[t], 16)

            wada = I["w_ada"][0].rearrange("(k p) n -> p k n", p=P)
            win = I["w_in"][0].rearrange("(k p) n -> p k n", p=P)
            for n in range(NADA + len(chunks)):
                if 2 <= n < NADA + 2:
                    sp.wait_ge(w_free, n - 1)
                elif n >= 2:
                    sp.wait_ge(m_done, last_job[n - 2 - NADA] + 1)
                if n < NADA:
                    sp.dma_start(v3(wbuf[n % 2], "p (k n) -> p k n", n=CW), wada[:, :, n * CW:(n + 1) * CW]).then_inc(w_in_[n % 2], 16)
                    if n == 1:
                        for t in range(2, QT + 1):
                            sp.wait_ge(x_tr, 4 * (t - 1))
                            if t < QT:
                                sp.dma_start(xrow[t % 2][:, :], xp[t]).then_inc(s_x[t % 2], 16)
                            else:
                                sp.dma_start(xrow[t % 2][0:TS, :], I["x_sample"].rearrange("b t d -> (b t) d")).then_inc(s_x[t % 2], 16)
                else:
                    c = n - NADA
                    off = 0
                    for col, w in chunks[c]:
                        sp.dma_start(wchunk(n, cwidth[c])[:, :, off:off + w], win[:, :, col:col + w]).then_inc(w_in_[n % 2], 16)
                        off += w

            after(sp, 1)
            for kv in range(2):
                sp.dma_start(v3(w1P[kv], "p (s h) -> p s h", h=256), I["a_cmp_w1"][0, kv].rearrange("(s p) h -> p s h", p=P)).then_inc(w1_in, 16)
                sp.dma_start(w2P[:, kv * 256:kv * 256 + 256].rearrange("p (n d) -> p n d", n=2), I["a_cmp_w2"][0, kv].rearrange("(n p) d -> p n d", p=P)).then_inc(w1_in, 16)
            after(sp, 2)
            sp.wait_ge(b_dma, 32 + 64)
            sp.dma_start(v3(bias, "p (h j) -> p h j", h=12), bass.AP(d_rep.tensor, d_rep.offset + 127, [[12 * TXL - 1, P], [TXL, 12], [1, T]])).then_inc(at_in, 16)

            after(sp, 3)

            regs = [sp.alloc_register(f"page{i}") for i in range(NPG)]

            cki = I["cache_c_kidx"].rearrange("l n p c -> (l n) p c")
            cc = I["cache_c_kv"].rearrange("l n p a c -> (l n) p a c")
            ca = I["cache_a_kv"].rearrange("l n p a h c -> (l n) p a h c")
            for n in range(32):
                if n >= 8:
                    sp.wait_ge(kb_tr, n - 7)
                if n % 4 == 0:
                    sp.load(regs, ptab[0:1, n * 4:n * 4 + NPG])
                for q in range(4):
                    r = sp.snap(regs[4 * (n % 4) + q], min_val=0, max_val=NPOOL - 1)
                    sp.dma_start(ixn[n % 8][:, q * ID:(q + 1) * ID], cki[bass.ds(r, 1), :, :].rearrange("a p c -> (a p) c")).then_inc(kb_in[n % 8], 16)
            after(sp, 4)
            for kv in range(2):
                if kv == 0:
                    for n in range(2):
                        sp.dma_start(w2S[:, n * 256:n * 256 + 256].rearrange("p (n d) -> p n d", n=2), I["a_cmp_w2"][0, n].rearrange("(n p) d -> p n d", p=P)).then_inc(w1s_in, 16)
                        sp.dma_start(v3(w1S[n], "p (s h) -> p s h", h=256), I["a_cmp_w1"][0, n].rearrange("(s p) h -> p s h", p=P)).then_inc(w1s_in, 16)
                for b in range(DB):
                    sp.load(regs, ptab[0:1, b * NPG:(b + 1) * NPG])
                    for q in range(4):
                        n = (kv * DB + b) * 4 + q
                        if n >= 4:
                            sp.wait_ge(xn_tr, 2 * (n - 3))
                        for i in range(4):
                            r = sp.snap(regs[4 * q + i], min_val=0, max_val=NPOOL - 1)
                            sp.dma_start(xnat[n % 4][:, i * 256:(i + 1) * 256].rearrange("p (h c) -> p h c", h=2), ca[bass.ds(r, 1), :, kv, :, :].rearrange("a p h c -> (a p) h c")).then_inc(xn_in[n % 4], 16)
            after(sp, 5)
            sp.wait_ge(b_dma, 32 + 64)
            for b in range(4):
                sp.dma_start(sbias[0][32 * b:32 * b + 32, :], d_smp[0:2].rearrange("u r x -> (u r) x")).then_inc(sb_in, 16)
            for b in range(DB):
                sp.dma_start(sbias[2][16 * b:16 * b + 16, :], d_smp[2]).then_inc(sb_in, 16)
            sw = I["state_a_win"][0]
            loaded = [None]

            def page(b, i):
                if loaded[0] != b:
                    sp.load(regs, ptab[0:1, b * NPG:(b + 1) * NPG])
                    loaded[0] = b
                return sp.snap(regs[i], min_val=0, max_val=NPOOL - 1)

            def keys(step, u):
                for m, (_, last, (lu, kind, b, q)) in enumerate(kloads):
                    if last not in blocks_of(step, u):
                        continue
                    if m >= NKR:
                        sp.wait_ge(kb_tr, kb_gt[kloads[m - NKR][1]] + 1)
                    slot, s = kn[m % NKR], kk_in[m % NKR]
                    if kind == "win":
                        sp.dma_start(v3(slot, "p (i c) -> p i c", c=256), sw[b, :, 0, :, :].rearrange("(i p) h c -> p i (h c)", p=P)).then_inc(s, 16)
                    for i in range(4 if kind != "win" else 0):
                        r = page(b, 4 * q + i)
                        if kind == "slc":
                            sp.dma_start(slot[:, i * 256:(i + 1) * 256], ca[bass.ds(r, 1), :, 2, :, :].rearrange("a p h c -> (a p) (h c)")).then_inc(s, 16)
                        else:
                            sp.dma_start(slot[:, i * P:(i + 1) * P], cc[bass.ds(r, 1), :, 0, :].rearrange("a p c -> (a p) c")).then_inc(s, 16)

            def values(u, first, last):
                for x in range(first, last):
                    m = 8 * u + x
                    if m >= NVR:
                        sp.wait_ge(pv_b, m - NVR + 1)
                    slot, s = vr[m % NVR], vr_in[m % NVR]
                    if u < 2:
                        for i in range(8):
                            r = page(4 * u + x // 2, 8 * (x % 2) + i)
                            sp.dma_start(slot[:, i * 256:(i + 1) * 256], ca[bass.ds(r, 1), :, 3, :, :].rearrange("a p h c -> (a p) (h c)")).then_inc(s, 16)
                    else:
                        for i in range(NPG):
                            r = page(x, i)
                            sp.dma_start(slot[:, i * P:(i + 1) * P], cc[bass.ds(r, 1), :, 1, :].rearrange("a p c -> (a p) c")).then_inc(s, 16)

            for step, u in STEPS:
                if step == "turn":
                    values(u, NVR, 8)
                    continue
                keys(step, u)
                if step == "body":
                    if u < 2:
                        if u == 1:
                            sp.wait_ge(pv_b, 8)
                        for b in range(4):
                            sp.dma_start(win_v[:, b * 1024:(b + 1) * 1024].rearrange("p (i c) -> p i c", c=256), sw[4 * u + b, :, 1, :, :].rearrange("(i p) h c -> p i (h c)", p=P)).then_inc(wv_in, 16)
                    values(u, 0, NVR)
            after(sp, 6)
            sp.dma_start(v3(xres, "p (i d) -> p i d", i=5)[:, 0:QT, :], I["x_prompt"][0].rearrange("(i p) d -> p i d", p=P)).then_inc(xr_in, 16)
            sp.dma_start(v3(xres, "p (i d) -> p i d", i=5)[0:TS, QT, :], I["x_sample"].rearrange("b t d -> (b t) d")).then_inc(xr_in, 16)
            wout = I["w_out"][0].rearrange("(k p) n -> p k n", p=P)
            for c in range(D // CW):
                if c >= 3:
                    sp.wait_ge(y_ps, 2 * (c - 2))
                sp.dma_start(v3(wo[c % 3], "p (k n) -> p k n", n=CW), wout[:, :, c * CW:(c + 1) * CW]).then_inc(wo_in[c % 3], 16)

        @block.gpsimd
        def _(pool):
            outs = 0

            def out(o, i, s=None):
                nonlocal outs
                ins = pool.dma_start(o, i)
                if s is None:
                    ins.then_inc(d_out, 16)
                    outs += 1
                else:
                    ins.then_inc(s, 16)

            out(O["a_win_s"][0, :, 0:WIN - DT].rearrange("b n a h c -> b n (a h c)"), I["state_a_win"][0, :, DT:WIN].rearrange("b n a h c -> b n (a h c)"))
            out(O["b_pool_s"][0, :, 0:11, :], I["state_b_pool"][0, :, 4:15, :])
            pool.wait_ge(b_ev, 5)
            pool.dma_start(d_rows, btmp[:, :]).then_inc(b_dma, 16)
            pool.wait_ge(b_dma, 16)
            pool.dma_start(d_rep.rearrange("p (h x) -> p h x", h=12), bass.AP(d_rows.tensor, d_rows.offset + TX0, [[0, P], [XL, 12], [1, TXL]])).then_inc(b_dma, 16)
            for t in range(DT):
                pool.dma_start(d_smp.rearrange("u (t g) x -> t u g x", t=DT)[t], bass.AP(d_rows.tensor, d_rows.offset + 3 - t, [[4 * XL, 3], [XL, 4], [1, SX]])).then_inc(b_dma, 16)
            o_akp = O["a_kv_p"].rearrange("l b (i p) a h c -> (l b i) p a (h c)", p=P)
            o_aks = O["a_kv_s"].rearrange("l b t a h c -> (l b t) a (h c)")
            o_ckp = O["c_kv_p"].rearrange("l b (i p) a c -> (l b i) p (a c)", p=P)
            o_cks = O["c_kv_s"].rearrange("l b t a c -> (l b t) (a c)")
            o_kip = O["c_kidx_p"].rearrange("l b (i p) c -> (l b i) p c", p=P)
            o_kis = O["c_kidx_s"].rearrange("l b t c -> (l b t) c")
            o_wp = O["a_win_p"].rearrange("l b (i p) a h c -> (l b i) p a (h c)", p=P)
            comp = {"kcmp": 0, "vcmp": 1, "kslc": 2, "vslc": 3}
            for j, (kind, b, t, c) in enumerate(jobs):
                if kind not in ROW_KINDS:
                    continue
                w = width(t)
                if j == idx_of[("kcmp", 0, 0)]:
                    pool.dma_start(v3(iqh, "p (c t) -> p c t", c=2), iqT3[ID:2 * ID, :, T:TT]).then_inc(iqh_in, 16)
                if j in staged:
                    n = staged.index(j)
                    pool.wait_ge(m_free, j + 1)
                    s, si = stage[n % 4], st_out[n % 4]
                    if kind == "small":
                        out(o_kip[t] if t < QT else o_kis, s[0:w, 0:ID], si)
                    elif kind == "ckv":
                        out(o_ckp[t] if t < QT else o_cks, s[0:w, :], si)
                    elif kind in comp:
                        out(o_akp[t, :, comp[kind]] if t < QT else o_aks[:, comp[kind]], s[0:w, :], si)
                    elif t < QT:
                        out(o_wp[t, :, 0], s[:, :], si)
                    else:
                        for b in range(DB):
                            out(O["a_win_s"][0, b, WIN - DT:WIN, 0].rearrange("t h c -> t (h c)"), s[DT * b:DT * b + DT, :], si if b == 0 else None)
                else:
                    pool.wait_ge(m_free, j + 1)
                    v = 0 if kind == "vslc" else 1
                    src = vnat3[:, t, v * CW:(v + 1) * CW] if t < QT else vN[:, v * CW:(v + 1) * CW]
                    if kind == "vslc":
                        out(o_akp[t, :, 3] if t < QT else o_aks[:, 3], src)
                    elif t < QT:
                        out(o_wp[t, :, 1], src)
                    else:
                        for b in range(DB):
                            out(O["a_win_s"][0, b, WIN - DT:WIN, 1].rearrange("t h c -> t (h c)"), vN[DT * b:DT * b + DT, CW:2 * CW])
            pool.wait_ge(pl_c, 2)
            out(O["b_pool_p"][0, 0], prw[1:16, 0:512])
            for b in range(DB):
                out(O["b_pool_s"][0, b, 11:15, :], prw[DT * b:DT * b + DT, 512:1024])
            for i in range(4):
                pool.wait_ge(st_out[i], 16 * len(range(i, len(staged), 4)))
            pool.wait_ge(d_out, 16 * outs)
            pool.drain().then_inc(ph_pool, 1)
            oy = O["y_prompt"].rearrange("a (i p) d -> p (a i) d", p=P)
            oys = O["y_sample"].rearrange("b t d -> (b t) d")
            for c in range(D // CW):
                pool.wait_ge(y_fin, 4 * (c + 1))
                pool.dma_start(oy[:, :, c * CW:(c + 1) * CW], v3(yrow[c % 2], "p (i d) -> p i d", i=5)[:, 0:QT, :]).then_inc(y_out, 16)
                pool.dma_start(oys[:, c * CW:(c + 1) * CW], v3(yrow[c % 2], "p (i d) -> p i d", i=5)[0:TS, QT, :]).then_inc(y_out, 16)
                pool.wait_ge(y_out, 32 * (c + 1))

        @block.tensor
        def _(pe):
            mm, tr = nc.tensor.matmul, nc.tensor.transpose

            def end_phase():
                pe.drain().then_inc(ph_pe, 1)

            pe.wait_ge(s_con, 16 * NSMALL)
            tr(bank[7][:, 0:NV], vrow[:, :], con[0:NV, 0:NV])
            tr(bank[7][:, 128:192], prow[:, :], con[0:64, 0:64])
            for k in range(KD):
                last = tr(bank[7][:, 256 + 9 * k:265 + 9 * k], crow[:, k * P:(k + 1) * P], con[0:9, 0:9])
            last.then_inc(su_tr, 1)
            for n in range(5):
                w = min(512, XL - 512 * n)
                mm(bank[n][0:12, 0:w], relb[:, :], ohr[:, 512 * n:512 * n + w], start=True, stop=True).then_inc(b_ps, 1)
            for t in range(QT + 1):
                w = width(t)
                pe.wait_ge(x_n, t + 1)
                for q in range(4):
                    g = 4 * t + q
                    if g < 4:
                        pe.wait_ge(b_ev, g + 1)
                    else:
                        pe.wait_ge(x_ev, g - 3)
                    for i in range(4):
                        k = 4 * q + i
                        last = tr(bank[g % 4][:, i * w:(i + 1) * w], xrow[t % 2][0:w, k * P:(k + 1) * P], con[0:w, 0:w])
                    last.then_inc(x_tr, 1)

            for g in range(4):
                last = tr(bank[6][:, g * 120:(g + 1) * 120], bst[:, g * P:(g + 1) * P], con[0:120, 0:120])
            last.then_inc(pst_t, 1)

            pe.wait_ge(c_s, 1)
            for n in range(NADA):
                pe.wait_ge(w_in_[n % 2], need[n])
                wv = v3(wbuf[n % 2], "p (k n) -> p k n", n=CW)
                for j in range(2):
                    for k in range(KD):
                        last = mm(bank[5][:, (2 * n + j) * 9:(2 * n + j + 1) * 9], wv[:, k, j * P:(j + 1) * P],
                                  cT[:, 9 * k:9 * k + 9], start=(k == 0), stop=(k == KD - 1))
                last.then_inc(w_free, 1)

            aux = 0

            def hook(j):
                nonlocal aux
                if j >= 1:
                    i = j - 1
                    kind, b, t, c = jobs[i]
                    if i in turned_set:
                        w = width(t)
                        pe.wait_ge(m_free, i + 1)
                        s = stage[staged.index(i) % 4]
                        for x in range(turns(i)):
                            if aux >= 2:
                                pe.wait_ge(a_free, aux - 1)
                            if aux < 2:
                                pe.wait_ge(pst_ev, 1)
                            tr(bank[6 + aux % 2][:, 0:w], s[0:w, x * P:(x + 1) * P], con[0:w, 0:w]).then_inc(a_done, 1)
                            aux += 1
                    if kind in ("cq", "aq"):
                        n = normT.index(i)
                        pe.wait_ge(n_sq, n + 1)
                        if n >= 1:
                            pe.wait_ge(n_std, n)
                        else:
                            pe.wait_ge(ixp_r, 12)
                        for f in range(2):
                            last = mm(bank[4 + f][:, 0:HALF], ones, sq[:, f * HALF:(f + 1) * HALF], start=True, stop=True)
                        last.then_inc(n_sum, 1)
                if j in ix_slot:
                    s = ix_slot[j]
                    if s[0] == "dots":
                        _, i, h, n = s
                        if n == 0:
                            pe.wait_ge(h_copied, 1)
                        if n >= 2:
                            pe.wait_ge(ixp_r, n - 1)
                        r0 = 64 * (h % 2)
                        mm(bank[4 + n % 2][:, 0:P * (i + 1)], iqT3[r0:r0 + 64, h // 2, i * P:(i + 1) * P],
                           ikT[r0:r0 + 64, 0:P * (i + 1)], start=True, stop=True).then_inc(ixp_d, 1)

            pe.wait_ge(h_ready, HREADY)
            pe.wait_ge(x_ev, 20)
            for j, (kind, b, t, c) in enumerate(jobs):
                n = NADA + c
                wv = wchunk(n, cwidth[c])
                pe.wait_ge(w_in_[n % 2], need[n])
                if j >= 2:
                    pe.wait_ge(m_free, j - 1)
                if kind in ROW_KINDS:
                    w = width(t)
                    for k in range(KD):
                        if k == 8:
                            hook(j)
                        last = mm(bank[2 * (j % 2)][0:w, 0:cwidth[c]], hT3[:, k, t * P:t * P + w], wv[:, k, :],
                                  start=(k == 0), stop=(k == KD - 1))
                else:
                    for f in range(2):
                        if f == 1:
                            hook(j)
                        for k in range(KD):
                            last = mm(bank[2 * (j % 2) + f][:, 0:HALF], wv[:, k, t * P:(t + 1) * P],
                                      hT3[:, k, f * HALF:(f + 1) * HALF], start=(k == 0), stop=(k == KD - 1))
                last.then_inc(m_done, 1)
            for g in range(4):
                pe.wait_ge(pl_d, g + 1)
                if g < 2:
                    pe.wait_ge(m_free, njobs)
                else:
                    pe.wait_ge(pl_y2, g - 1)
                for f in range(2):
                    last = mm(bank[2 * (g % 2) + f][:, 0:HALF], wpool[:, g * P:(g + 1) * P],
                              (sq if g % 2 == 0 else rs)[:, f * HALF:(f + 1) * HALF], start=True, stop=True)
                last.then_inc(pl_y, 1)
            pe.wait_ge(a_free, aux)
            for g in range(4):
                tr(bank[6][0:16, g * P:(g + 1) * P], bT3[:, g, T:T + 16], ident)
                last = tr(bank[7][0:TS, g * P:(g + 1) * P], wk[:, g * TS:(g + 1) * TS], ident)
            last.then_inc(pl_t, 1)
            for u in range(2):
                mm(bank[4][:, 24 * u:24 * u + 24], expd[:, u * P:(u + 1) * P], gateS0[:, :], start=True, stop=True)
            mm(bank[5][:, 0:4], expd[:, 2 * P:3 * P], iwS[:, :], start=True, stop=True).then_inc(pl_t, 1)
            end_phase()

            after(pe, 1)
            pe.wait_ge(w1_in, 64)
            for kv in range(2):
                w1 = v3(w1P[kv], "p (s h) -> p s h", h=256)
                for hb in range(2):
                    bk = bank[2 * kv + hb]
                    for s in range(32):
                        mm(bk[:, 0:62], w1[:, s, hb * P:(hb + 1) * P],
                           cmp4[:, kv, :, s:s + 16 * 30 + 1:16], start=(s == 0), stop=(s == 31))
                    for s in range(32):
                        last = mm(bk[:, 64:65], w1[:, s, hb * P:(hb + 1) * P], peT[:, kv * 32 + s:kv * 32 + s + 1],
                                  start=(s == 0), stop=(s == 31))
                    last.then_inc(cp_ps, 1)
            pe.wait_ge(cp_ev, 4)
            for hb in range(2):
                last = mm(bank[4][:, 0:62], w2P[:, hb * P:(hb + 1) * P], hidP[:, hb * 64:hb * 64 + 62], start=(hb == 0), stop=(hb == 1))
            last.then_inc(cp_ps, 1)
            for h in range(KVH):
                for hb in range(2):
                    last = mm(bank[5][0:NCP, h * P:(h + 1) * P], hidP[:, (2 + hb) * 64 + NCP * h:(2 + hb) * 64 + NCP * h + NCP],
                              w2P[:, 256 + hb * P:256 + (hb + 1) * P], start=(hb == 0), stop=(hb == 1))
            last.then_inc(cp_ps, 1)
            pe.wait_ge(cp_ev, 5)
            mm(bank[6][:, 0:62], ones, cxP[:, 64:126], start=True, stop=True).then_inc(cp_ps, 1)
            end_phase()

            after(pe, 2)

            def qk(u):
                grp, i, h = units[u]
                nk = P * (i + 1)
                if u >= 1:
                    pe.wait_ge(q_s, u)
                if grp == "A":
                    q = aqT3[:, h, i * P:(i + 1) * P]
                    k = h // G
                    mm(bank[2][:, 0:8 * i + 7], q, kcP[:, 32 * k:32 * k + 8 * i + 7], start=True, stop=True)
                    mm(bank[0][:, 0:nk], q, kslcT[:, k * T:k * T + nk], start=True, stop=True)
                    mm(bank[1][:, 0:nk], q, kwinT[:, k * T:k * T + nk], start=True, stop=True).then_inc(q_ps, 1)
                else:
                    mm(bank[0][:, 0:nk], cqT3[:, h, i * P:(i + 1) * P], ckT[:, 0:nk], start=True, stop=True).then_inc(q_ps, 1)

            def turn_p(u):
                grp, i, h = units[u]
                pe.wait_ge(q_p, u + 1)
                if u >= 1:
                    pe.wait_ge(q_ta, u)
                    pe.wait_ge(q_td, min(u, NUA))
                s = SP_[u % 3]
                if grp == "A":
                    for x in range(i + 1):
                        tr(bank[4][:, x * P:(x + 1) * P], s[:, 512 + x * P:512 + (x + 1) * P], ident)
                    tr(bank[5][0:8 * i + 7, 0:P], s[:, 1024:1024 + 8 * i + 7], ident)
                for x in range(i + 1):
                    last = tr(bank[3][:, x * P:(x + 1) * P], s[:, x * P:(x + 1) * P], ident)
                last.then_inc(q_t, 1)

            def pv(u):
                grp, i, h = units[u]
                pe.wait_ge(q_ta, u + 1)
                pe.wait_ge(q_td, min(u + 1, NUA))
                if u >= 2:
                    pe.wait_ge(q_m, u - 1)
                o = bank[6 + u % 2][:, 0:P]
                s = PTP[u % 2]
                if grp == "A":
                    k = h // G
                    nc_ = 8 * i + 7
                    mm(o, vcP[0:nc_, k * P:(k + 1) * P], s[0:nc_, 1024:1024 + P], start=True, stop=False)
                    for x in range(i + 1):
                        mm(o, vnat3[:, x, CW + k * P:CW + (k + 1) * P], s[:, 512 + x * P:512 + (x + 1) * P], start=False, stop=False)
                    for x in range(i + 1):
                        last = mm(o, vnat3[:, x, k * P:(k + 1) * P], s[:, x * P:(x + 1) * P], start=False, stop=(x == i))
                else:
                    for x in range(i + 1):
                        last = mm(o, cvnat[:, x * P:(x + 1) * P], s[:, x * P:(x + 1) * P], start=(x == 0), stop=(x == i))
                last.then_inc(q_o, 1)

            for n in range(len(units) + 3):
                if n < len(units):
                    qk(n)
                if 0 <= n - 2 < len(units):
                    turn_p(n - 2)
                if 0 <= n - 3 < len(units):
                    pv(n - 3)
            end_phase()

            after(pe, 3)

            def kturn(g, rows_out):
                if g >= 2:
                    pe.wait_ge(kb_d if g % 2 else kb_a, (g - 2) // 2 + 1)

            def evacuated(g):
                pe.wait_ge(kb_d if g % 2 else kb_a, g // 2 + 1)

            def ix_mm(n):
                b, q = n // 4, n % 4
                evacuated(n)
                mm(bank[q][32 * (b // 2):32 * (b // 2) + 32, :], zi[:, b * 32:(b + 1) * 32], ixT[n % 4][:, :],
                   start=(b % 2 == 0), stop=(b % 2 == 1), tile_position=(0, 32 * (b // 2))).then_inc(kb_mm, 1)

            for n in range(32):
                pe.wait_ge(kb_in[n % 8], kneed[n])
                kturn(n, ID)
                for i in range(4):
                    last = tr(bank[5 + n % 2][0:ID, i * P:(i + 1) * P], ixn[n % 8][:, i * ID:(i + 1) * ID], ident)
                last.then_inc(kb_tr, 1)
                if n >= 1:
                    ix_mm(n - 1)
            ix_mm(31)
            mm(bank[4][:, 0:TS], qfi[:, :], kiN[0:ID, :], start=True, stop=True).then_inc(si_ps, 1)
            for f in range(5):
                pe.wait_ge(si_ev, f + 1)
                w = 512 if f < 4 else TS
                mm(bank[f][:, 0:w], wsel[:, :], ixr[:, 512 * f:512 * f + w], start=True, stop=True).then_inc(si_ps, 1)
            end_phase()

            after(pe, 4)

            def row_turn(x):
                n, q, h = x // 8, x % 8 // 2, x % 2
                m = 4 * n + q
                pe.wait_ge(xn_in[m % 4], 64 * (m // 4 + 1))
                if x >= 2:
                    pe.wait_ge(xt_d if x % 2 else xt_a, (x - 2) // 2 + 1)
                for i in range(4):
                    last = tr(bank[4 + x % 2][:, i * P:(i + 1) * P], xnat[m % 4][:, i * 256 + h * P:i * 256 + (h + 1) * P], ident)
                last.then_inc(xn_tr, 1)

            def w2_mm(n):
                kv = n // 8
                pe.wait_ge(hd_ev, 2 * (n + 1))
                if n >= 1:
                    pe.wait_ge(kc_ok, n)
                if kv == 0:
                    for hb in range(2):
                        last = mm(bank[6][:, 0:254], w2S[:, hb * P:(hb + 1) * P], hid[0][:, hb * 256:hb * 256 + 254], start=(hb == 0), stop=(hb == 1))
                else:
                    for h in range(KVH):
                        for hb in range(2):
                            last = mm(bank[6][0:NCS, h * P:(h + 1) * P], hid[0][:, hb * 256 + NCS * h:hb * 256 + NCS * (h + 1)],
                                      w2S[:, 256 + hb * P:256 + (hb + 1) * P], start=(hb == 0), stop=(hb == 1))
                last.then_inc(kc_ps, 1)

            for n in range(18):
                for i in range(8):
                    g = n - 1
                    if 0 <= g < 16:
                        kv = g // 8
                        if i == 0:
                            pe.wait_ge(w1s_in, 64)
                            pe.wait_ge(xt_a, 4 * (g + 1))
                            pe.wait_ge(xt_d, 4 * (g + 1))
                            if g >= 2:
                                pe.wait_ge(hd_ev, 2 * (g - 1))
                        w1 = v3(w1S[kv], "p (s h) -> p s h", h=256)
                        xv = v3(xt[g % 2], "p (h s c) -> p h s c", h=2, s=16)
                        for e in range(8):
                            hb, s = (8 * i + e) // 32, (8 * i + e) % 32
                            last = mm(bank[2 * (g % 2) + hb][:, 0:254], w1[:, s, hb * P:(hb + 1) * P],
                                      xv[:, :, s % 16, s // 16:s // 16 + NCS], start=(s == 0), stop=(s == 31))
                        if i == 7:
                            last.then_inc(hd_ps, 1)
                    if n < 16:
                        row_turn(8 * n + i)
                    if 0 <= n - 2 < 16 and i == 3:
                        w2_mm(n - 2)
                    if 0 <= n - 2 < 8 and i == 6:
                        pe.wait_ge(kc_x, n - 1)
                        mm(bank[7][:, 0:254], ones, cx[:, 256:510], start=True, stop=True).then_inc(kc_sum, 1)
            end_phase()

            after(pe, 5)
            gt = 32

            def kb(n):
                nonlocal gt
                u, kind, b, q, k, m = sblocks[n]
                pe.wait_ge(kk_in[m % NKR], kkneed[m])
                kturn(gt, HD)
                w = 256 if u < 2 else P
                for i in range(4):
                    last = tr(bank[5 + gt % 2][:, i * P:(i + 1) * P], kn[m % NKR][:, i * w + k * P:i * w + (k + 1) * P], ident)
                last.then_inc(kb_tr, 1)
                gt += 1

            def kmm(n):
                u, kind, b, q, k, m = sblocks[n]
                evacuated(kb_gt[n])
                if u < 2:
                    r = 32 * (b % 4)
                    lhs, st_, sp_ = zq[:, u * 256 + k * P + r:u * 256 + k * P + r + 32], k == 0, k == 1
                else:
                    r = 32 * (b // 2)
                    lhs, st_, sp_ = zq[:, 512 + 32 * b:512 + 32 * b + 32], b % 2 == 0, b % 2 == 1
                mm(bank[q][r:r + 32, :], lhs, kT[n % 4][:, :], start=st_, stop=sp_, tile_position=(0, r)).then_inc(kb_mm, 1)

            for step, u in STEPS:
                o = bank[7]
                if step != "turn":
                    if step == "head" and u >= 1:
                        pe.wait_ge(un_s, u)
                    if step == "body" and u < 2:
                        pe.wait_ge(un_w, u + 1)
                    ns = blocks_of(step, u)
                    for n in ns:
                        kb(n)
                        if n > ns[0]:
                            kmm(n - 1)
                        if step == "body" and u < 2 and n == ns[0] + 12:
                            pe.wait_ge(im_in, u + 1)
                            mm(o[:, 0:NCS], con[:, K_GRP:K_GRP + P], sC[:, 0:NCS], start=True, stop=True).then_inc(im_ps, 1)
                    kmm(ns[-1])
                    if u < 2:
                        col, kind = (32, 2) if step == "head" else (0, 0)
                        for k in range(KVH):
                            last = mm(bank[4][:, col:col + TS], zq[:, u * 256 + k * P:u * 256 + (k + 1) * P], ksN[:, (kind + k) * TS:(kind + k + 1) * TS],
                                      start=(k == 0), stop=(k == 1))
                        if step == "head":
                            for b in range(4):
                                for k in range(KVH):
                                    c0 = ((4 * u + b) * KVH + k) * P
                                    last = mm(bank[4][32 * b:32 * b + 32, 64:64 + NCS], zq[:, u * 256 + k * P + 32 * b:u * 256 + k * P + 32 * b + 32],
                                              kc[:, c0:c0 + NCS], start=(k == 0), stop=(k == 1), tile_position=(0, 32 * b))
                        last.then_inc(un_ps, 1)
                    elif step == "body":
                        mm(bank[4][:, 0:TS], qf[:, :], ksN[:, 4 * TS:5 * TS], start=True, stop=True).then_inc(un_ps, 1)
                    continue
                pe.wait_ge(un_p, u + 1)
                for src in pgroups(u):
                    kturn(gt, HD)
                    for i, (s, rows) in enumerate(src):
                        last = tr(bank[5 + gt % 2][0:rows, i * P:(i + 1) * P], s, ident)
                    last.then_inc(kb_tr, 1)
                    gt += 1
                evacuated(gt - 1)
                evacuated(gt - 2)
                if u < 2:
                    pe.wait_ge(im_ps, u + 1)
                    pe.wait_ge(wv_in, 64 * (u + 1))
                    for b in range(4):
                        for k in range(KVH):
                            cs = slice(32 * b + 16 * k, 32 * b + 16 * k + 16)

                            def p_of(tile, rows):
                                return pT[0:rows, tile * P + cs.start:tile * P + cs.stop]
                            mm(o[:, cs], vN[:, k * P:(k + 1) * P], p_of(16, TS), start=True, stop=False)
                            mm(o[:, cs], vN[:, CW + k * P:CW + (k + 1) * P], p_of(21, TS), start=False, stop=False)
                            c0 = ((4 * u + b) * KVH + k) * P
                            mm(o[:, cs], vc[0:NCS, c0:c0 + P], p_of(22, NCS), start=False, stop=False)
                            for i in range(4):
                                mm(o[:, cs], win_v[:, b * 1024 + i * 256 + k * P:b * 1024 + i * 256 + (k + 1) * P], p_of(17 + i, P), start=False, stop=False)
                            for i in range(NPG):
                                m = 8 * u + 2 * b + i // 8
                                if k == 0 and i % 8 == 0:
                                    pe.wait_ge(vr_in[m % NVR], vneed[m])
                                last = mm(o[:, cs], vr[m % NVR][:, i % 8 * 256 + k * P:i % 8 * 256 + (k + 1) * P], p_of(i, P), start=False, stop=(i == NPG - 1))
                                if k == 1 and i % 8 == 7:
                                    last.then_inc(pv_b, 1)
                else:
                    for b in range(DB):
                        m = 16 + b
                        pe.wait_ge(vr_in[m % NVR], vneed[m])
                        cs = slice(16 * b, 16 * b + 16)
                        mm(o[:, cs], cvN[:, :], pT[0:TS, 16 * P + 16 * b:16 * P + 16 * b + 16], start=True, stop=False)
                        for i in range(NPG):
                            last = mm(o[:, cs], vr[m % NVR][:, i * P:(i + 1) * P], pT[:, i * P + 16 * b:i * P + 16 * b + 16], start=False, stop=(i == NPG - 1))
                        last.then_inc(pv_b, 1)
            end_phase()

            after(pe, 6)

            def y_turn(nb):
                pe.wait_ge(y_ev, nb + 1)
                if nb >= 2:
                    pe.wait_ge(y_fin, 2 * (nb - 1))
                s = yT[nb % 4]
                for i in range(QT):
                    tr(bank[4 + nb % 2][:, i * P:(i + 1) * P], s[:, i * P:(i + 1) * P], ident)
                tr(bank[6 + nb % 2][0:TS, 0:P], s[:, T:TT], ident).then_inc(y_tr, 1)

            for nb in range(KD):
                c = nb // 2
                pe.wait_ge(wo_in[c % 3], 16 * (c // 3 + 1))
                if nb >= 2:
                    pe.wait_ge(y_ev, nb - 1)
                wv = v3(wo[c % 3], "p (k n) -> p k n", n=CW)
                for f in range(2):
                    for k in range(KD):
                        last = mm(bank[2 * (nb % 2) + f][:, 0:HALF], wv[:, k, (nb % 2) * P:(nb % 2 + 1) * P],
                                  mix3[:, k, f * HALF:(f + 1) * HALF], start=(k == 0), stop=(k == KD - 1))
                    if f == 0 and nb >= 1:
                        y_turn(nb - 1)
                last.then_inc(y_ps, 1)
            y_turn(KD - 1)

        @block.scalar
        def _(act):
            A = nc.scalar.activation
            mine = Count(act, act_)
            eps = con[:, K_EPS:K_EPS + 1]

            def end_phase():
                act.drain().then_inc(ph_act, 1)

            for n in range(5):
                w = min(512, XL - 512 * n)
                act.wait_ge(b_ps, n + 1)
                A(btmp[:, 512 * n:512 * n + w], bank[n][0:12, 0:w], ACT.Copy).then_inc(b_ev, 1)
            act.wait_ge(su_ev, 1)
            A(cT[:, 144:288], bank[7][:, 256:400], ACT.Exp, scale=-1.0).then_inc(c_e, 1)
            for t in range(QT + 1):
                w = width(t)
                act.wait_ge(s_x[t % 2], 16 * (t // 2 + 1))
                if t >= 1:
                    evac_x(act, A, t - 1)
                mine.link(A(mix[0:w, 0:D], xrow[t % 2][0:w, :], ACT.Square, accum_out=st[0:w, t:t + 1]))
                A(st[0:w, 8 + t:9 + t], st[0:w, t:t + 1], ACT.Sqrt, scale=1.0 / D, bias=con[0:w, K_EPS:K_EPS + 1]).then_inc(x_std, 1)
            evac_x(act, A, QT)
            act.wait_ge(pst_t, 1)
            for g in range(4):
                last = act.copy(bS4[:, g, :, 0:15], bank[6][:, g * 120:(g + 1) * 120].rearrange("p (b t) -> p b t", t=15))
            last.then_inc(pst_ev, 1)

            aux = 0
            nr = 0

            def hook(j):
                nonlocal aux
                if j >= 1:
                    i = j - 1
                    kind, b, t, c = jobs[i]
                    if i in turned_set:
                        w = width(t)
                        for x in range(turns(i)):
                            act.wait_ge(a_done, aux + 1)
                            act.copy(turned_to(kind, t, x), bank[6 + aux % 2][:, 0:w]).then_inc(a_free, 1)
                            aux += 1
                    if kind in ("cq", "aq"):
                        n = normT.index(i)
                        act.wait_ge(n_sum, n + 1)
                        if n >= 1:
                            act.wait_ge(m_free, normT[n - 1] + 1)
                        for f in range(2):
                            last = A(rs[:, f * HALF:(f + 1) * HALF], bank[4 + f][:, 0:HALF], ACT.Sqrt, scale=1.0 / HD, bias=eps)
                        last.then_inc(n_std, 1)
                if j in ix_slot and ix_slot[j][0] == "dots":
                    _, i, h, n = ix_slot[j]
                    act.wait_ge(ixp_d, n + 1)
                    if n >= 1:
                        act.wait_ge(ixp_a, n)
                    A(rs[:, 0:P * (i + 1)], bank[4 + n % 2][:, 0:P * (i + 1)], ACT.Relu).then_inc(ixp_r, 1)

            for j, (kind, b, t, c) in enumerate(jobs):
                hook(j)
                if j in rownorm:
                    w = width(t)
                    act.wait_ge(m_done, j + 1)
                    nh = 1 if kind == "ckv" else 2
                    o = 24 + 4 * (nr % 2)
                    if nr >= 2:
                        act.wait_ge(m_free, rownorm[nr - 2] + 1)
                    for h in range(nh):
                        mine(A(sq[0:w, 0:P], bank[2 * (j % 2)][0:w, h * P:(h + 1) * P], ACT.Square, accum_out=st[0:w, o + h:o + h + 1]))
                        mine.wait()
                    A(st[0:w, o + 2:o + 2 + nh], st[0:w, o:o + nh], ACT.Sqrt, scale=1.0 / HD, bias=con[0:w, K_EPS:K_EPS + 1]).then_inc(r_std, 1)
                    nr += 1
                elif kind in ("cq", "aq"):
                    n = normT.index(j)
                    act.wait_ge(m_done, j + 1)
                    if n >= 1:
                        act.wait_ge(n_sum, n)
                    for f in range(2):
                        last = A(sq[:, f * HALF:(f + 1) * HALF], bank[2 * (j % 2) + f][:, 0:HALF], ACT.Square)
                    last.then_inc(n_sq, 1)
                elif kind in SIL_AT:
                    n = silj.index(j)
                    act.wait_ge(m_done, j + 1)
                    if n >= 2:
                        act.wait_ge(m_free, silj[n - 2] + 1)
                    elif n == 0:
                        act.wait_ge(n_sum, len(normT))
                        act.wait_ge(m_free, normT[-1] + 1)
                    for f in range(2):
                        last = A((sq, rs)[n % 2][:, f * HALF:(f + 1) * HALF], bank[2 * (j % 2) + f][:, 0:HALF], ACT.Exp, scale=-1.0)
                    last.then_inc(sil_e, 1)
            hook(njobs)
            A(gateP[:, :], gateP[:, :], ACT.Exp, scale=-1.0).then_inc(g_e, 1)
            act.wait_ge(gs_in, 1)
            A(gateS[:, :], gateS[:, :], ACT.Exp, scale=-1.0).then_inc(g_e, 1)
            end_phase()

            after(act, 1)
            for kv in range(2):
                for hb in range(2):
                    n = 2 * kv + hb
                    act.wait_ge(cp_ps, n + 1)
                    mine.link(A(b1e[:, n:n + 1], bank[n][:, 64:65], ACT.Identity, bias=vecT[:, V_B1 + n:V_B1 + n + 1]))
                    A(hidP[:, n * 64:n * 64 + 62], bank[n][:, 0:62], ACT.Gelu_apprx_tanh, bias=b1e[:, n:n + 1]).then_inc(cp_ev, 1)
            act.wait_ge(cp_ps, 5)
            mine(A(cxP[:, 0:62], bank[4][:, 0:62], ACT.Identity, bias=vecT[:, V_B2:V_B2 + 1]))
            A(cxP[:, 64:126], bank[4][:, 0:62], ACT.Square, bias=vecT[:, V_B2:V_B2 + 1]).then_inc(cp_ev, 1)
            act.wait_ge(cp_ps, 7)
            A(cxP[:, 128:190], bank[6][:, 0:62], ACT.Sqrt, scale=1.0 / HD, bias=eps).then_inc(cp_ev, 1)
            end_phase()

            after(act, 2)

            def exps(u):
                grp, i, h = units[u]
                nk = P * (i + 1)
                s, a = SP_[u % 3], 16 * (u % 4)
                act.wait_ge(q_s, u + 1)
                parts = ((1024, 8 * i + 7, 0), (0, nk, 1), (512, nk, 2)) if grp == "A" else ((0, nk, 1),)
                for off, n, r in parts:
                    last = A(s[:, off:off + n], s[:, off:off + n], ACT.Exp, bias=as_[:, a + 3 + r:a + 4 + r], accum_out=as_[:, a + 6 + r:a + 7 + r])
                last.then_inc(q_e, 1)

            def take_slc(u):
                grp, i, h = units[u]
                act.wait_ge(q_t, u + 1)
                if u >= 2:
                    act.wait_ge(q_o, u - 1)
                act.copy(PTP[u % 2][:, 0:P * (i + 1)], bank[3][:, 0:P * (i + 1)]).then_inc(q_ta, 1)

            for n in range(len(units) + 2):
                if n < len(units):
                    exps(n)
                if 0 <= n - 2 < len(units):
                    take_slc(n - 2)
            end_phase()

            after(act, 3)
            for n in range(0, 32, 2):
                act.wait_ge(kb_tr, n + 1)
                if n >= 4:
                    act.wait_ge(kb_mm, n - 3)
                act.copy(ixT[n % 4][:, :], bank[5][0:ID, :]).then_inc(kb_a, 1)
            act.wait_ge(kb_mm, 32)
            act.wait_ge(si_ps, 1)
            for f in range(5):
                w = 512 if f < 4 else TS
                A(ixr[:, 512 * f:512 * f + w], bank[f][:, 0:w], ACT.Relu).then_inc(si_ev, 1)
            end_phase()

            after(act, 4)

            def hidden(g):
                act.wait_ge(hd_ps, g + 1)
                if g >= 1:
                    act.wait_ge(kc_ps, g)
                for hb in range(2):
                    A(hid[0][:, hb * 256:hb * 256 + 254], bank[2 * (g % 2) + hb][:, 0:254], ACT.Gelu_apprx_tanh,
                      bias=b1e[:, 2 * (g // 8) + hb:2 * (g // 8) + hb + 1]).then_inc(hd_ev, 1)

            for n in range(18):
                if 0 <= n - 2 < 16:
                    hidden(n - 2)
                for i in range(0, 8, 2):
                    if n < 16:
                        x = 8 * n + i
                        take_rows(act, act.copy, x, xt_a)
                    if 0 <= n - 2 < 8 and i == 4:
                        g = n - 2
                        act.wait_ge(kc_ps, g + 1)
                        if g >= 1:
                            act.wait_ge(kc_ok, g)
                        mine(A(cx[:, 0:254], bank[6][:, 0:254], ACT.Identity, bias=vecT[:, V_B2:V_B2 + 1]))
                        A(cx[:, 256:510], bank[6][:, 0:254], ACT.Square, bias=vecT[:, V_B2:V_B2 + 1]).then_inc(kc_x, 1)
                if 0 <= n - 2 < 8:
                    act.wait_ge(kc_sum, n - 1)
                    A(cx[:, 256:510], bank[7][:, 0:254], ACT.Sqrt, scale=1.0 / HD, bias=eps).then_inc(kc_std, 1)
            end_phase()

            after(act, 5)
            gt = 32
            for step, u in STEPS:
                if step == "turn":
                    for gi, src in enumerate(pgroups(u)):
                        if gt % 2 == 0:
                            act.wait_ge(kb_tr, gt + 1)
                            take_p(act, act.copy, u, gi, src, kb_a)
                        gt += 1
                    continue
                if step == "body" and u < 2:
                    unit_exps(act, A, u, "early")
                for n in blocks_of(step, u):
                    if gt % 2 == 0:
                        take_k(act, act.copy, n, gt, kb_a)
                    gt += 1
                if step == "body":
                    unit_exps(act, A, u, "late")
            end_phase()

        @block.vector
        def _(v):
            V = nc.vector
            mine = Count(v, dve)
            link = mine.link

            def end_phase():
                v.drain().then_inc(ph_dve, 1)

            def ttr(out, a, b, acc):
                return V.tensor_tensor_reduce(out=out, in0=a, in1=b, scale=1.0, scalar=FLOOR, op0=ALU.add, op1=ALU.max, accum_out=acc)

            v.wait_ge(su_tr, 1)
            link(V.tensor_copy(vecT[:, :], bank[7][:, 0:NV]))
            V.tensor_copy(peT[:, :], bank[7][:, 128:192]).then_inc(su_ev, 1)
            v.wait_ge(c_e, 1)
            link(V.tensor_scalar(cT[:, 144:288], cT[:, 144:288], 1.0, None, ALU.add))
            link(V.reciprocal(cT[:, 144:288], cT[:, 144:288]))
            V.tensor_tensor(cT[:, 0:144], bank[7][:, 256:400], cT[:, 144:288], ALU.mult).then_inc(c_s, 1)
            link(V.tensor_scalar(vecT[:, V_AQ:V_CQ + 1], vecT[:, V_AQ:V_CQ + 1], SCALE, None, ALU.mult))
            for t in range(QT + 1):
                w = width(t)
                v.wait_ge(x_std, t + 1)
                link(V.reciprocal(st[0:w, 16 + t:17 + t], st[0:w, 8 + t:9 + t]))
                V.tensor_scalar(xrow[t % 2][0:w, :], xrow[t % 2][0:w, :], st[0:w, 16 + t:17 + t], None, ALU.mult).then_inc(x_n, 1)
            link(V.memset(zq[:, :], 0.0))
            link(V.memset(zi[:, :], 0.0))
            link(V.memset(bT[:, :], 0.0))
            v.wait_ge(w_free, NADA)
            link(V.tensor_tensor(mod3, bank[5][:, 0:432].rearrange("p (n b) -> p n b", b=9), bc(vecT[:, 0:48], 9), ALU.add))
            V.tensor_scalar(ascale[:, :], modT[:, 144:288], 1.0, None, ALU.add).then_inc(h_copied, 1)
            v.wait_ge(h_copied, 1)
            link(V.tensor_tensor(asc3, asc3, bc(vecT[:, V_G:V_G + 16], 9), ALU.mult))
            v.wait_ge(x_ev, 20)
            for k in range(KD):
                V.tensor_scalar(hT3[:, k, 0:T], hT3[:, k, 0:T], asc3[:, k, 0:1], mod3[:, k, 0:1], ALU.mult, ALU.add).then_inc(h_ready, 1)
            for k in range(KD):
                hs = hT3[:, k, T:TT].rearrange("p (b t) -> p b t", t=DT)
                link(V.tensor_tensor(hs, hs, bc(asc3[:, k, 1:9], DT), ALU.mult))
                V.tensor_tensor(hs, hs, bc(mod3[:, k, 1:9], DT), ALU.add).then_inc(h_ready, 1)

            nr = 0

            def topk(w, out8, times):
                for _ in range(times):
                    link(V.max(out8, w))
                    link(V.match_replace(w, out8, w, MARK))

            for j, (kind, b, t, c) in enumerate(jobs):
                bk = bank[2 * (j % 2)]
                if j in ix_slot:
                    s = ix_slot[j]
                    i = s[1]
                    nk = P * (i + 1)
                    if s[0] == "dots":
                        _, i, h, n = s
                        v.wait_ge(ixp_r, n + 1)
                        wi = iwP[:, 4 * i + h:4 * i + h + 1]
                        if h == 0:
                            link(V.tensor_scalar(wk[:, 0:nk], rs[:, 0:nk], wi, None, ALU.mult))
                            V.tensor_tensor(wk[:, P * i:nk], wk[:, P * i:nk], con[:, K_DIAG:K_DIAG + P], ALU.add).then_inc(ixp_a, 1)
                        else:
                            V.scalar_tensor_tensor(out=wk[:, 0:nk], in0=rs[:, 0:nk], scalar=wi, in1=wk[:, 0:nk], op0=ALU.mult, op1=ALU.add).then_inc(ixp_a, 1)
                        v.wait_ge(ixp_a, n + 1)
                    else:
                        topk(wk[:, 0:nk], st[:, 48:56], 4)
                        if s[2] == 3:
                            link(V.tensor_scalar(maskC[:, MOFF[i]:MOFF[i] + nk], wk[:, 0:nk], MARK, NEG, ALU.not_equal, ALU.mult))
                v.wait_ge(m_done, j + 1)
                w = width(t)
                if j in staged_set:
                    n = staged.index(j)
                    if n >= 4:
                        v.wait_ge(st_out[n % 4], 16 * (n // 4))
                        i = staged[n - 4]
                        if i in turned_set:
                            v.wait_ge(a_done, sum(turns(x) for x in turned if x <= i))
                    s = stage[n % 4]
                if kind == "small":
                    V.tensor_copy(s[0:w, 0:ID], bk[0:w, 24:24 + ID])
                    V.tensor_copy(s[0:w, ID:2 * ID], bk[0:w, 24:24 + ID])
                    V.tensor_copy(gateP[:, 24 * t:24 * t + 24] if t < QT else gateS0[:, :], bk[0:w, 0:24])
                    V.tensor_copy(iwP[:, 4 * t:4 * t + 4] if t < QT else iwS[:, :], bk[0:w, 24 + ID:24 + ID + 4]).then_inc(m_free, 1)
                elif j in rownorm:
                    nh = 1 if kind == "ckv" else 2
                    o = 24 + 4 * (nr % 2)
                    nr += 1
                    v.wait_ge(r_std, nr)
                    link(V.reciprocal(st[0:w, o + 2:o + 2 + nh], st[0:w, o + 2:o + 2 + nh]))
                    gr = {"kslc": 0, "kwin": 1, "ckv": 2}[kind]
                    if kind == "ckv":
                        V.tensor_copy(s[0:w, P:2 * P], bk[0:w, P:2 * P])
                        V.tensor_copy(cvnat[:, t * P:(t + 1) * P] if t < QT else cvN[:, :], bk[0:w, P:2 * P])
                    for h in range(nh):
                        last = V.scalar_tensor_tensor(out=s[0:w, h * P:(h + 1) * P], in0=bk[0:w, h * P:(h + 1) * P], scalar=st[0:w, o + 2 + h:o + 3 + h],
                                                      in1=gk[0:w, gr * P:(gr + 1) * P], op0=ALU.mult, op1=ALU.mult)
                    last.then_inc(m_free, 1)
                elif kind in ("kcmp", "vcmp"):
                    V.tensor_copy(s[0:w, :], bk[0:w, 0:CW]).then_inc(m_free, 1)
                elif kind in ("vslc", "vwin"):
                    x = 0 if kind == "vslc" else CW
                    V.tensor_copy(vnat3[:, t, x:x + CW] if t < QT else vN[:, x:x + CW], bk[0:w, 0:CW]).then_inc(m_free, 1)
                else:
                    b2 = bank[2 * (j % 2) + 1]
                    if kind == "iq":
                        V.tensor_copy(iqT3[:, b, 0:HALF], bk[:, 0:HALF])
                        V.tensor_copy(iqT3[:, b, HALF:TT], b2[:, 0:HALF]).then_inc(m_free, 1)
                    elif kind in ("cq", "aq"):
                        n = normT.index(j)
                        v.wait_ge(n_std, n + 1)
                        link(V.reciprocal(rs[:, :], rs[:, :]))
                        dst = aqT3 if kind == "aq" else cqT3
                        col = vecT[:, V_AQ:V_AQ + 1] if kind == "aq" else vecT[:, V_CQ:V_CQ + 1]
                        parts = [(dst[:, b, 0:HALF], bk[:, 0:HALF], rs[:, 0:HALF]), (dst[:, b, HALF:T], b2[:, 0:T - HALF], rs[:, HALF:T])]
                        if kind == "cq":
                            parts.append((qf[:, b:P:4], b2[:, T - HALF:HALF], rs[:, T:TT]))
                        else:
                            k, g = b // G, b % G
                            z5 = v3(zq, "p (u k b x t g) -> p u k b x t g", u=3, k=2, b=4, x=2, t=DT)
                            for u in range(2):
                                a, e = T - HALF + 16 * u, T + 16 * u
                                parts.append((z5[:, u, k, :, k, :, g], b2[:, a:a + 16].rearrange("p (b t) -> p b t", t=DT), rs[:, e:e + 16].rearrange("p (b t) -> p b t", t=DT)))
                        for o, i, r in parts:
                            last = V.scalar_tensor_tensor(out=o, in0=i, scalar=col, in1=r, op0=ALU.mult, op1=ALU.mult)
                        last.then_inc(m_free, 1)
                    elif kind == "bin":
                        V.tensor_copy(bT3[:, b, 16:16 + HALF], bk[:, 0:HALF])
                        V.tensor_copy(bT3[:, b, 16 + HALF:16 + T], b2[:, 0:T - HALF])
                        V.tensor_copy(wk[:, b * TS:(b + 1) * TS], b2[:, T - HALF:HALF])
                        V.tensor_copy(bS4[:, b, :, 15:19], b2[:, T - HALF:HALF].rearrange("p (b t) -> p b t", t=DT)).then_inc(m_free, 1)
                    else:
                        n = silj.index(j)
                        e = (sq, rs)[n % 2]
                        blk = SIL_AT[kind] + b
                        v.wait_ge(sil_e, n + 1)
                        link(V.tensor_scalar(e[:, :], e[:, :], 1.0, None, ALU.add))
                        link(V.reciprocal(e[:, :], e[:, :]))
                        V.tensor_tensor(mix3[:, blk, 0:HALF], bk[:, 0:HALF], e[:, 0:HALF], ALU.mult)
                        V.tensor_tensor(mix3[:, blk, HALF:TT], b2[:, 0:HALF], e[:, HALF:TT], ALU.mult).then_inc(m_free, 1)
            v.wait_ge(m_free, njobs)
            v.wait_ge(iqh_in, 16)
            for h in range(IH):
                src = (iqT3[0:ID, h // 2, T:TT] if h % 2 == 0 else iqh[:, (h // 2) * TS:(h // 2 + 1) * TS]).rearrange("p (b t) -> p b t", t=DT)
                last = V.tensor_copy(qfi[:, :].rearrange("p (b h t) -> p b h t", h=IH, t=DT)[:, :, h, :], src)
            link(last)
            for par in range(2):
                V.tensor_copy(v3(zi, "p (c e r) -> p c e r", e=2, r=32)[:, :, par, 16 * par:16 * par + 16], v3(qfi, "p (c e r) -> p c e r", e=2, r=16)[:, :, par, :])
                V.tensor_copy(zq[:, 512:768].rearrange("p (c e r) -> p c e r", e=2, r=32)[:, :, par, 16 * par:16 * par + 16], v3(qf, "p (c e r) -> p c e r", e=2, r=16)[:, :, par, :])
            v.wait_ge(pst_ev, 1)
            for g in range(4):
                o = (sq, rs)[g % 2]
                if g >= 2:
                    v.wait_ge(pl_y, g - 1)
                win_w = 2 << g
                cur = bT3[:, g, :]
                lo = 16
                step = 1
                src_p, src_s = cur, bS4[:, g, :, :]
                pa, pb_ = pls[:, 0:528], pls[:, 528:1056]
                sa, sb_ = pls[:, 1056:1056 + 160], pls[:, 1216:1216 + 160]
                flip = 0
                while step < win_w:
                    dp = (pa, pb_)[flip]
                    ds_ = (sa, sb_)[flip].rearrange("p (b t) -> p b t", t=20)
                    link(V.tensor_tensor(dp[:, 2 * step - 1:528], src_p[:, 2 * step - 1:528], src_p[:, step - 1:528 - step], ALU.add))
                    link(V.tensor_tensor(ds_[:, :, 2 * step - 1:19], src_s[:, :, 2 * step - 1:19], src_s[:, :, step - 1:19 - step], ALU.add))
                    src_p, src_s = dp, ds_
                    flip ^= 1
                    step *= 2
                V.scalar_tensor_tensor(out=o[:, 0:T], in0=src_p[:, 16:528], scalar=1.0 / win_w, in1=cur[:, 16:528], op0=ALU.mult, op1=ALU.subtract)
                link(V.scalar_tensor_tensor(out=o[:, T:TT].rearrange("p (b t) -> p b t", t=DT), in0=src_s[:, :, 15:19], scalar=1.0 / win_w,
                                            in1=bS4[:, g, :, 15:19], op0=ALU.mult, op1=ALU.subtract))
                link(V.tensor_tensor(pls[:, 1376:1392], src_p[:, 16:32], con[:, K_RC + 16 * g:K_RC + 16 * g + 16], ALU.mult))
                V.tensor_tensor(o[:, 0:16], pls[:, 1376:1392], cur[:, 16:32], ALU.subtract).then_inc(pl_d, 1)
                if g >= 1:
                    pool_out(v, V, g - 1)
            pool_out(v, V, 3)
            v.wait_ge(pl_t, 1)
            v.wait_ge(pl_y, 4)
            V.tensor_copy(prw[0:16, 0:512], bank[6][0:16, :]).then_inc(pl_c, 1)
            V.tensor_copy(prw[0:TS, 512:1024], bank[7][0:TS, :]).then_inc(pl_c, 1)
            v.wait_ge(pl_t, 2)
            link(V.tensor_copy(gateS1[:, :], bank[4][:, 0:48]))
            for r in range(3):
                for k in range(2):
                    link(V.tensor_tensor_reduce(out=st[:, 32:40], in0=gateS1[:, 24 * k + 8 * r:24 * k + 8 * r + 8], in1=con[:, K_M3:K_M3 + 8], scale=1.0, scalar=0.0,
                                                op0=ALU.mult, op1=ALU.add, accum_out=gateS[:, 2 * r + k:2 * r + k + 1]))
            V.tensor_tensor_reduce(out=st[:, 60:64], in0=bank[5][:, 0:4], in1=con[:, K_M2:K_M2 + 4], scale=1.0, scalar=0.0,
                                   op0=ALU.mult, op1=ALU.add, accum_out=wiS[:, 0:1]).then_inc(gs_in, 1)
            v.wait_ge(gs_in, 1)
            link(V.tensor_scalar(wsel[:, :], con[:, K_WM:K_WM + P], wiS[:, 0:1], None, ALU.mult))
            v.wait_ge(g_e, 2)
            for gt_ in (gateP, gateS):
                link(V.tensor_scalar(gt_[:, :], gt_[:, :], 1.0, None, ALU.add))
                link(V.reciprocal(gt_[:, :], gt_[:, :]))
            end_phase()

            after(v, 1)
            v.wait_ge(cp_ps, 6)
            V.tensor_tensor(vcP[0:NCP, :].rearrange("p (h c) -> p h c", h=2), bank[5][0:NCP, 0:256].rearrange("p (h c) -> p h c", h=2),
                            gk[0:NCP, 3 * P:4 * P].unsqueeze(1).broadcast_to([NCP, 2, P]), ALU.add)
            v.wait_ge(cp_ev, 6)
            link(V.reciprocal(cxP[:, 128:190], cxP[:, 128:190]))
            for h in range(2):
                V.scalar_tensor_tensor(out=kcP[:, 32 * h:32 * h + NCP], in0=cxP[:, NCP * h:NCP * (h + 1)], scalar=vecT[:, V_AK:V_AK + 1],
                                       in1=cxP[:, 128 + NCP * h:128 + NCP * (h + 1)], op0=ALU.mult, op1=ALU.mult)
            end_phase()

            after(v, 2)
            v.wait_ge(at_in, 16)
            b3 = v3(bias, "p (h j) -> p h j", h=12)

            def scores(u):
                grp, i, h = units[u]
                nk = P * (i + 1)
                s, a = SP_[u % 3], 16 * (u % 4)
                off = 384 - P * i
                v.wait_ge(q_ps, u + 1)
                if u >= 3:
                    v.wait_ge(q_t, u - 2)
                if grp == "A":
                    n = 8 * i + 7
                    ttr(s[:, 1024:1024 + n], bank[2][:, 0:n], b3[:, h, off + 31:off + 31 + 16 * (n - 1) + 1:16], as_[:, a:a + 1])
                    ttr(s[:, 0:nk], bank[0][:, 0:nk], b3[:, h, off:off + nk], as_[:, a + 1:a + 2])
                    link(ttr(s[:, 512:512 + nk], bank[1][:, 0:nk], b3[:, h, off:off + nk], as_[:, a + 2:a + 3]))
                    V.tensor_scalar(as_[:, a + 3:a + 6], as_[:, a:a + 3], -1.0, None, ALU.mult).then_inc(q_s, 1)
                else:
                    if i == 0:
                        link(ttr(s[:, 0:nk], bank[0][:, 0:nk], b3[:, 8 + h, off:off + nk], as_[:, a + 1:a + 2]))
                    else:
                        link(V.tensor_tensor(s[:, 0:nk], bank[0][:, 0:nk], b3[:, 8 + h, off:off + nk], ALU.add))
                        link(ttr(s[:, 0:nk], s[:, 0:nk], maskC[:, MOFF[i]:MOFF[i] + nk], as_[:, a + 1:a + 2]))
                    V.tensor_scalar(as_[:, a + 4:a + 5], as_[:, a + 1:a + 2], -1.0, None, ALU.mult).then_inc(q_s, 1)

            def norm(u):
                grp, i, h = units[u]
                nk = P * (i + 1)
                s, a = SP_[u % 3], 16 * (u % 4)
                v.wait_ge(q_e, u + 1)
                r0, r1 = (0, 3) if grp == "A" else (1, 2)
                link(V.tensor_scalar(as_[:, a + 6 + r0:a + 6 + r1], as_[:, a + 6 + r0:a + 6 + r1], 1e-30, None, ALU.max))
                link(V.reciprocal(as_[:, a + 9 + r0:a + 9 + r1], as_[:, a + 6 + r0:a + 6 + r1]))
                if grp == "A":
                    link(V.tensor_tensor(as_[:, a + 9:a + 12], as_[:, a + 9:a + 12], gateP[:, 24 * i + h:24 * i + h + 17:8], ALU.mult))
                parts = ((1024, 8 * i + 7, 0), (512, nk, 2), (0, nk, 1)) if grp == "A" else ((0, nk, 1),)
                for off, n, r in parts:
                    last = V.tensor_scalar(s[:, off:off + n], s[:, off:off + n], as_[:, a + 9 + r:a + 10 + r], None, ALU.mult)
                last.then_inc(q_p, 1)

            def take_win(u):
                grp, i, h = units[u]
                if grp != "A":
                    return
                v.wait_ge(q_t, u + 1)
                if u >= 2:
                    v.wait_ge(q_o, u - 1)
                n = 8 * i + 7
                V.tensor_copy(PTP[u % 2][0:n, 1024:1024 + P], bank[5][0:n, 0:P])
                V.tensor_copy(PTP[u % 2][:, 512:512 + P * (i + 1)], bank[4][:, 0:P * (i + 1)]).then_inc(q_td, 1)

            def gated(u):
                grp, i, h = units[u]
                v.wait_ge(q_o, u + 1)
                m = mix3[:, h if grp == "A" else 12 + h, P * i:P * (i + 1)]
                V.tensor_tensor(m, bank[6 + u % 2][:, 0:P], m, ALU.mult).then_inc(q_m, 1)

            NU = len(units)
            for n in range(NU + 3):
                if n < NU:
                    scores(n)
                if 0 <= n - 1 < NU:
                    norm(n - 1)
                if 0 <= n - 2 < NU:
                    take_win(n - 2)
                if 0 <= n - 3 < NU:
                    gated(n - 3)
            end_phase()

            after(v, 3)
            for n in range(1, 32, 2):
                v.wait_ge(kb_tr, n + 1)
                if n >= 4:
                    v.wait_ge(kb_mm, n - 3)
                V.tensor_copy(ixT[n % 4][:, :], bank[6][0:ID, :]).then_inc(kb_d, 1)
            for f in range(5):
                v.wait_ge(si_ps, f + 2)
                if f < 4:
                    link(V.tensor_copy(wrk[:, 512 * f:512 * f + 512], bank[f][:, :]))
                else:
                    link(V.tensor_tensor(wrk[:, PAST:LS], bank[4][:, 0:TS], con[:, K_BM + 2 * TS:K_BM + 3 * TS], ALU.add))
            end_phase()

            after(v, 4)
            for n in range(18):
                for i in range(1, 8, 2):
                    if n < 16:
                        take_rows(v, V.tensor_copy, 8 * n + i, xt_d)
                if 0 <= n - 2 < 16:
                    g = n - 2
                    kv, b = g // 8, g % 8
                    if kv == 0:
                        v.wait_ge(kc_std, g + 1)
                        link(V.reciprocal(cx[:, 256:510], cx[:, 256:510]))
                        V.scalar_tensor_tensor(out=v3(kc, "p (b h c) -> p b h c", b=DB, h=2)[:, b, :, 0:NCS], in0=cx[:, 0:254].rearrange("p (h c) -> p h c", h=2),
                                               scalar=vecT[:, V_AK:V_AK + 1], in1=cx[:, 256:510].rearrange("p (h c) -> p h c", h=2), op0=ALU.mult, op1=ALU.mult).then_inc(kc_ok, 1)
                    else:
                        v.wait_ge(kc_ps, g + 1)
                        V.tensor_tensor(v3(vc, "p (b h c) -> p b h c", b=DB, h=2)[0:NCS, b], bank[6][0:NCS, 0:256].rearrange("p (h c) -> p h c", h=2),
                                        gk[0:NCS, 3 * P:4 * P].unsqueeze(1).broadcast_to([NCS, 2, P]), ALU.add).then_inc(kc_ok, 1)
                if n < 16:
                    topk(wrk[:, :], st[:, 48:56], 2)
            V.tensor_scalar(wrk[:, :], wrk[:, :], MARK, NEG, ALU.not_equal, ALU.mult)
            end_phase()

            after(v, 5)
            v.wait_ge(sb_in, 16 * 12)
            for u in range(3):
                link(V.tensor_tensor(nbias[:, u * TS:(u + 1) * TS].rearrange("p (b t) -> p b t", t=DT),
                                     sbias[u][:, PAST:PAST + DT].unsqueeze(1).broadcast_to([P, DB, DT]),
                                     con[:, K_BM + u * TS:K_BM + (u + 1) * TS].rearrange("p (b t) -> p b t", t=DT), ALU.add))
            gt = 32
            for step, u in STEPS:
                if step == "turn":
                    for gi, src in enumerate(pgroups(u)):
                        if gt % 2 == 1:
                            v.wait_ge(kb_tr, gt + 1)
                            take_p(v, V.tensor_copy, u, gi, src, kb_d)
                        gt += 1
                    v.wait_ge(pv_b, 8 * (u + 1))
                    if u < 2:
                        o5 = bank[7][:, 0:P].rearrange("p (b k t g) -> p b k t g", b=4, k=2, t=DT)
                        for h in range(AH):
                            m = mix3[:, h, T + 16 * u:T + 16 * u + 16].rearrange("p (b t) -> p b t", t=DT)
                            last = V.tensor_tensor(m, o5[:, :, h // 4, :, h % 4], m, ALU.mult)
                    else:
                        for h in range(CH):
                            m = mix3[:, 12 + h, T:TT]
                            last = V.tensor_tensor(m, bank[7][:, h:P:4], m, ALU.mult)
                    last.then_inc(un_x, 1)
                    continue
                if step == "body" and u < 2:
                    early(v, V, u, link, ttr)
                for x, n in enumerate(blocks_of(step, u)):
                    if step == "body" and u < 2 and x == 8:
                        mid(v, V, u, link)
                    if gt % 2 == 1:
                        take_k(v, V.tensor_copy, n, gt, kb_d)
                    gt += 1
                if step == "body":
                    late(v, V, u, link, ttr)
            end_phase()

            after(v, 6)
            v.wait_ge(xr_in, 32)

            def y_rows(nb):
                c, j = nb // 2, nb % 2
                v.wait_ge(y_tr, nb + 1)
                if c >= 2 and j == 0:
                    v.wait_ge(y_out, 32 * (c - 1))
                y5 = v3(yrow[c % 2], "p (i d) -> p i d", i=5)
                x5 = v3(xres, "p (i d) -> p i d", i=5)
                V.tensor_tensor(y5[:, 0:QT, j * P:(j + 1) * P], bank[4 + nb % 2][:, :].rearrange("p (i d) -> p i d", i=4), x5[:, 0:QT, nb * P:(nb + 1) * P], ALU.add).then_inc(y_fin, 1)
                V.tensor_tensor(y5[0:TS, QT, j * P:(j + 1) * P], bank[6 + nb % 2][0:TS, 0:P], x5[0:TS, QT, nb * P:(nb + 1) * P], ALU.add).then_inc(y_fin, 1)

            for nb in range(KD):
                v.wait_ge(y_ps, nb + 1)
                if nb >= 4:
                    v.wait_ge(y_tr, nb - 3)
                s = yT[nb % 4]
                gate = mod3[:, 32 + nb, 0:1]
                V.tensor_scalar(s[:, 0:HALF], bank[2 * (nb % 2)][:, 0:HALF], gate, None, ALU.mult)
                V.tensor_scalar(s[:, HALF:T], bank[2 * (nb % 2) + 1][:, 0:T - HALF], gate, None, ALU.mult)
                V.tensor_tensor(s[:, T:TT].rearrange("p (b t) -> p b t", t=DT), bank[2 * (nb % 2) + 1][:, T - HALF:HALF].rearrange("p (b t) -> p b t", t=DT),
                                bc(mod3[:, 32 + nb, 1:9], DT), ALU.mult).then_inc(y_ev, 1)
                if nb >= 1:
                    y_rows(nb - 1)
            y_rows(KD - 1)


_INS = ["x_prompt", "x_sample", "cache_a_kv", "cache_c_kv", "cache_c_kidx", "state_a_win", "state_b_pool", "page_table",
        "c_prompt", "c_sample", "rel_bias", "norm_g", "w_ada", "b_ada", "w_in", "w_out", "a_qnorm", "a_knorm",
        "a_cmp_pe", "a_cmp_w1", "a_cmp_b1", "a_cmp_w2", "a_cmp_b2", "b_pool_w", "b_scale", "c_qnorm", "c_knorm"]
_OUTS = [("y_prompt", (1, T, D)), ("y_sample", (DB, DT, D)),
         ("a_kv_p", (1, 1, T, 4, KVH, HD)), ("a_kv_s", (1, DB, DT, 4, KVH, HD)),
         ("c_kv_p", (1, 1, T, 2, HD)), ("c_kv_s", (1, DB, DT, 2, HD)),
         ("c_kidx_p", (1, 1, T, ID)), ("c_kidx_s", (1, DB, DT, ID)),
         ("a_win_p", (1, 1, T, 2, KVH, HD)), ("a_win_s", (1, DB, WIN, 2, KVH, HD)),
         ("b_pool_p", (1, 1, 15, 512)), ("b_pool_s", (1, DB, 15, 512))]


def kernel(**inputs):
    import concourse.bacc as bacc
    from concourse.bass_utils import run_bass_kernel_spmd as run

    nc = bacc.Bacc("TRN2", target_bir_lowering=False, num_devices=1)
    arrays, ins, outs = {}, {}, {}
    for name in _INS:
        arrays[f"in_{name}_dram"] = np.ascontiguousarray(inputs[name])
    for name, a in shape_constants().items():
        arrays[f"in_{name}_dram"] = a
    for name, a in arrays.items():
        ins[name[3:-5]] = nc.dram_tensor(name, a.shape, mybir.dt.from_np(a.dtype), kind="ExternalInput").ap()
    for i, (name, shape) in enumerate(_OUTS):
        outs[name] = nc.dram_tensor(f"out_{i}_dram", shape, F32, kind="ExternalOutput").ap()
    build(nc, ins, outs)
    r = run(nc, [arrays], core_ids=[0])
    return tuple(r.results[0][f"out_{i}_dram"] for i in range(len(_OUTS)))
```

```python
from contextlib import ExitStack
import math

import numpy as np

import concourse.bass as bass
from concourse import mybir

F32 = mybir.dt.float32
F32R = mybir.dt.float32r
I32 = mybir.dt.int32
ACT = mybir.ActivationFunctionType
ALU = mybir.AluOpType
AX = mybir.AxisListType

P = 128
D = 2048
KD = D // P
T = 512
QT = T // P
DB, DT = 8, 4
TS = DB * DT
TT = T + TS
HALF = TT // 2
PAST, PAGE = 2048, 128
NPG = PAST // PAGE
NPOOL = 5 * DB * NPG // 4
HD = 128
AH, KVH, G = 8, 2, 4
CH = 4
IH, ID = 4, 64
WIN = 512
NB_, MAXD = 32, 128
LS = PAST + TS
NCS = (PAST + DT) // 16 - 1
NCP = T // 16 - 1
NXP = KVH * NCP + 1
NSB = 33
TOPB = 16
NIX = 6
NKR, NVR = 4, 4
XTW = 2 * PAST + 8
KEEP_P, KEEP_S = 128, 256
EPS = 1e-6
NEG = -1e30
FLOOR = -1e29
MARK = -3e38
FORCE = 1e6
SCALE = HD ** -0.5
XOFF = PAST + DT - 1
XL = 2184
TX0 = XOFF - 384 - 127
TXL = 640
SX = 2052

C_AQ, C_AKV, C_GATE, C_ASIL, C_BIN, C_BSIL = 0, 1024, 2560, 2584, 3608, 4120
C_CQ, C_CKV, C_IQ, C_IK, C_IW, C_CSIL = 4632, 5144, 5400, 5656, 5720, 5724
CW = 256

V_BADA, V_G, V_BSC, V_B1, V_B2, V_AQ, V_CQ, V_AK, V_CK = 0, 48, 64, 68, 72, 74, 75, 76, 79
NV = 80
K_ID, K_ONE, K_GRP, K_WM, K_BM, K_WIN, K_DIAG, K_RC, K_M2, K_M3, K_FB = 0, 128, 256, 384, 512, 608, 612, 740, 804, 808, 816
K_EPS = K_FB + 33
K_SEL = K_EPS + 1
NK = K_SEL + 9
NSMALL1, NSMALL2 = 13, 11
HREADY = 2 * KD


def bucket(rel):
    rel = np.maximum(rel, 0)
    exact = NB_ // 2
    relf = np.maximum(rel, exact).astype(np.float32)
    lb = exact + (np.log(relf / np.float32(exact)) / np.float32(math.log(MAXD / exact)) * np.float32(NB_ - exact)).astype(np.int32)
    return np.where(rel < exact, rel, np.minimum(lb, NB_ - 1))


def shape_constants():
    c = np.zeros((P, NK), np.float32)
    p = np.arange(P)
    c[:, K_ID:K_ID + P] = np.eye(P)
    c[:, K_ONE:K_ONE + P] = 1.0
    c[:, K_GRP:K_GRP + P] = p[:, None] // 4 == p[None] // 4
    pb, pi, pt = p // 16, p // 4 % 4, p % 4
    qb, qt, qg = p // 16, p // 4 % 4, p % 4
    c[:, K_WM:K_WM + P] = (pb[:, None] == qb[None]) & (pt[:, None] == qt[None])
    k = np.arange(TS)
    rows_b = (p // 32, 4 + p // 32, qb)
    for u in range(3):
        c[:, K_BM + TS * u:K_BM + TS * (u + 1)] = np.where((k[None] // DT == rows_b[u][:, None]) & (k[None] % DT <= qt[:, None]), 0.0, NEG)
    c[:, K_WIN:K_WIN + 4] = np.where(np.arange(4)[None] < qt[:, None], NEG, 0.0)
    c[:, K_DIAG:K_DIAG + P] = np.where(p[None] <= p[:, None], 0.0, NEG)
    for g in range(4):
        c[:, K_RC + 16 * g:K_RC + 16 * g + 16] = 1.0 / np.minimum(np.arange(16) + 1, 2 << g)
    c[:, K_M2:K_M2 + 4] = np.arange(4)[None] == pi[:, None]
    c[:, K_M3:K_M3 + 8] = np.arange(8)[None] == (4 * (p // 16 % 2) + qg)[:, None]
    c[:, K_EPS] = EPS
    c[:, K_SEL:K_SEL + 9] = np.arange(9)[None] == (p % 32)[:, None]
    c[:, [K_FB, K_FB + 31, K_FB + 32]] = FORCE
    e = np.zeros((TS, 3 * P), np.float32)
    kb, kt = k // DT, k % DT
    for u in range(2):
        e[:, P * u:P * (u + 1)] = (kb[:, None] == rows_b[u][None]) & (kt[:, None] == qt[None])
    e[:, 2 * P:] = (kb[:, None] == pb[None]) & (kt[:, None] == pt[None])
    rel = XOFF - np.arange(XL)
    oh = np.zeros((NB_ + 1, XL), np.float32)
    oh[bucket(rel), np.arange(XL)] = (rel >= 0)
    oh[NB_] = np.where(rel < 0, NEG, 0.0)
    return {"constants": c, "expanders": e, "bucket_rows": oh}


def plan_projection():
    chunks, jobs = [], []

    def rows(kind, parts):
        chunks.append(parts)
        jobs.extend((kind, 0, t, len(chunks) - 1) for t in range(QT + 1))

    def cols(kind, first, blocks):
        for b in range(0, blocks, 2):
            chunks.append([(first + b * P, CW)])
            jobs.extend((kind, b + j, j, len(chunks) - 1) for j in range(2))

    rows("small", [(C_GATE, 24), (C_IK, ID + IH)])
    cols("iq", C_IQ, 2)
    rows("ckv", [(C_CKV, CW)])
    for n, kind in enumerate(("kcmp", "vcmp", "kslc", "vslc", "kwin", "vwin")):
        rows(kind, [(C_AKV + n * CW, CW)])
    nwhole = len(chunks)
    for kind, first, blocks in (("cq", C_CQ, CH), ("aq", C_AQ, AH), ("bin", C_BIN, 4), ("bsil", C_BSIL, 4), ("asil", C_ASIL, AH), ("csil", C_CSIL, 4)):
        for b in range(blocks):
            jobs.append((kind, b, 0, len(chunks)))
            chunks.append([(first + b * P, P)])
    return chunks, jobs, nwhole


ROW_KINDS = ("small", "ckv", "kcmp", "vcmp", "kslc", "vslc", "kwin", "vwin")
SIL_AT = {"asil": 0, "bsil": 8, "csil": 12}


class Count:

    def __init__(self, eng, sem):
        self.eng, self.sem, self.n = eng, sem, 0

    def __call__(self, ins):
        ins.then_inc(self.sem, 1)
        self.n += 1
        return self.n

    def wait(self):
        self.eng.wait_ge(self.sem, self.n)

    def link(self, ins):
        self(ins)
        self.wait()


def build(nc, I, O, debug=None):
    chunks, jobs, nwhole = plan_projection()
    njobs = len(jobs)
    J0 = next(j for j, job in enumerate(jobs) if job[3] == nwhole)
    with ExitStack() as ctx:
        sems = {}

        def sem(name):
            sems[name] = ctx.enter_context(nc.semaphore(name))
            return sems[name]

        top = [16512]
        hi = [top[0]]

        def sb(name, rows, words, dt=F32, at=None):
            where = top[0] if at is None else at
            words_r = -(-words // 8) * 8
            t = nc.alloc_sbuf_tensor_at(name, [rows, words], dt, offset=where)
            if at is None:
                top[0] += 4 * words_r
                assert top[0] <= 229344, (name, top[0])
            return t

        def region(start):
            pos = [start]

            def place(name, rows, words, dt=F32):
                t = sb(name, rows, words, dt, at=pos[0])
                pos[0] += 4 * (-(-words // 8) * 8)
                assert pos[0] <= 229344, (name, pos[0])
                return t
            return place, pos

        con = sb("con", P, NK)
        expd = sb("expd", TS, 3 * P)
        vecT = sb("vecT", P, NV)
        peT = sb("peT", P, 64)
        modT = sb("modT", P, 48 * 9)
        ascale = sb("ascale", P, KD * 9)
        gk = sb("gk", P, 4 * P)
        relb = sb("relb", NB_ + 1, 12)
        gateP = sb("gateP", P, QT * 24)
        gateS0 = sb("gateS0", TS, 24)
        gateS = sb("gateS", P, 6)
        gateS1 = sb("gateS1", P, 48)
        iwP = sb("iwP", P, QT * 4)
        iwS = sb("iwS", TS, 4)
        wiS = sb("wiS", P, 4)
        zq = sb("zq", P, 3 * 256)
        qf = sb("qf", P, P)
        zi = sb("zi", ID, DB * 32)
        qfi = sb("qfi", ID, P)
        ksN = sb("ksN", P, 5 * TS)
        kiN = sb("kiN", P, TS)
        vN = sb("vN", TS, 2 * CW)
        cvN = sb("cvN", TS, P)
        wsel = sb("wsel", P, P)
        maskC = sb("maskC", P, 256 + 384 + 512)
        wpool = sb("wpool", P, 4 * P)
        ptab = sb("ptab", 1, DB * NPG, I32)
        st = sb("st", P, 64)
        b1e = sb("b1e", P, 4)
        mix = sb("mix", P, KD * TT)
        base_free = top[0]

        data, dpos = region(base_free)
        aqT = data("aqT", P, AH * T)
        cqT = data("cqT", P, CH * T)
        kslcT = data("kslcT", P, KVH * T)
        kwinT = data("kwinT", P, KVH * T)
        ckT = data("ckT", P, T)
        vnat = data("vnat", P, QT * 2 * CW)
        cvnat = data("cvnat", P, QT * P)
        kcP = data("kcP", P, KVH * 32)
        vcP = data("vcP", 32, KVH * P)
        cmpT = data("cmpT", P, 2 * KVH * T)
        xrow = [sb(f"xrow{i}", P, D, at=base_free + i * 4 * D) for i in range(2)]
        crow = sb("crow", 9, D, at=base_free + 2 * 4 * D)
        vrow = sb("vrow", NV, P, at=base_free + 3 * 4 * D)
        prow = sb("prow", 64, P, at=base_free + 3 * 4 * D + 4 * P)
        cT = sb("cT", P, KD * 9 * 2, at=base_free + 3 * 4 * D + 8 * P)
        btmp = sb("btmp", 12, XL, at=base_free + 3 * 4 * D + 8 * P + 1280)
        ohr = sb("ohr", NB_ + 1, XL, at=base_free + 3 * 4 * D + 8 * P + 1280 + 4 * XL)
        bst = sb("bst", DB * 15, 512, at=base_free + 3 * 4 * D + 8 * P + 1280 + 8 * XL)
        cpad = sb("cpad", P, KD * 32, at=base_free + 3 * 4 * D + 8 * P + 1280 + 8 * XL + 2048)
        mpart = [sb(f"mpart{i}", P, CW, at=base_free + 3 * 4 * D + 8 * P + 1280 + 8 * XL + 4096 + 1024 * i) for i in range(2)]
        assert 6144 + 3 * 4 * D + 8 * P + 1280 + 8 * XL <= dpos[0] - base_free

        big0 = dpos[0]
        big, bpos = region(big0)
        hT = big("hT", P, KD * TT)
        wbuf = [big(f"wbuf{i}", P, KD * CW) for i in range(2)]
        big_end = bpos[0]
        h_hi = sb("h_hi", P, KD * TT, F32R, at=base_free - 4 * KD * TT)
        h_lo = sb("h_lo", P, KD * TT, F32R, at=big0)
        HW_ = KD // 2 * P
        slot0 = (3 * D // CW + nwhole) % 2
        hw_at = [big0 + 4 * KD * TT + 4 * KD * CW * ((q // 2 + slot0) % 2) + 8 * HW_ * (q % 2) for q in range(4)]
        hw_raw = [sb(f"hw_raw{q}", P, HW_, at=hw_at[q]) for q in range(4)]
        hw_lo = [sb(f"hw_lo{q}", P, HW_, F32R, at=hw_at[q]) for q in range(4)]
        hw_hi = [sb(f"hw_hi{q}", P, HW_, F32R, at=hw_at[q] + 4 * HW_) for q in range(4)]
        ext, epos = region(big_end)
        iqh = ext("iqh", ID, 2 * TS)
        iqT = ext("iqT", P, 2 * TT)
        ikT = ext("ikT", P, T)
        bT = ext("bT", P, 4 * (16 + T))
        bS = ext("bS", P, 4 * DB * 20)
        stage = [ext(f"stage{i}", P, CW) for i in range(4)]
        sq = ext("sq", P, TT)
        rs = ext("rs", P, TT)
        wk = ext("wk", P, T)
        tmp, tp = region(big0)
        pls = tmp("pls", P, 1400)
        prw = tmp("prw", TS, 1024)
        w1p, w1pos = region(tp[0])
        w1P = [w1p(f"w1P{i}", P, 32 * 256) for i in range(2)]
        w1_early = (big_end - tp[0]) // (16 * 256 * 4)
        hrow, _ = region(big0)
        hidr = [hrow(f"hidr{i}", P, 256) for i in range(2)]
        w2p, _ = region(w1pos[0])
        w2P = w2p("w2P", P, 2 * 2 * P)
        hidP = w2p("hidP", P, 4 * 64)
        cxP = w2p("cxP", P, 3 * 64)
        xpe = w2p("xpe", P, 2 * 32 * NXP)
        att, apos = region(tp[0])
        bias = att("bias", P, 12 * T)
        assert 12 * T <= 32 * 256
        SP_ = [att(f"SP{i}", P, 1056) for i in range(3)]
        PTP = [att(f"PTP{i}", P, 1152) for i in range(2)]
        as_ = att("as_", P, 64)
        smp, spos = region(base_free)
        kc = smp("kc", P, DB * KVH * P)
        vc = smp("vc", P, DB * KVH * P)
        wrk = smp("wrk", P, LS)
        s2 = spos[0]
        ix, ixpos = region(s2)
        ixn = [ix(f"ixn{i}", P, 4 * ID) for i in range(NIX)]
        ixT = [ix(f"ixT{i}", ID, 512) for i in range(4)]
        ixr = ix("ixr", P, LS)
        w1at = 229344 - 4 * 32 * 256
        assert apos[0] <= w1at
        cmw, cmpos = region(ixpos[0])
        w1S = sb("w1S", P, 32 * 256, at=w1at)
        w1lo = sb("w1lo", P, 32 * 256, F32R, at=w1at)
        w1hi = cmw("w1hi", P, 32 * 256, F32R)
        xth = [cmw("xth0", P, XTW, F32R)]
        xtl = [cmw("xtl0", P, XTW, F32R)]
        assert cmpos[0] <= w1at
        mixr, mixpos = region(base_free - 4 * KD * TT)
        xth.append(mixr("xth1", P, XTW, F32R))
        xtl.append(mixr("xtl1", P, XTW, F32R))
        assert mixpos[0] <= base_free
        cm, cpos = region(s2)
        xnat = [cm(f"xnat{i}", P, 4 * 256) for i in range(4)]
        hid = [cm(f"hid{i}", P, 2 * 256) for i in range(1)]
        w2S = cm("w2S", P, 2 * 2 * P)
        cx = cm("cx", P, 2 * 256)
        assert cpos[0] <= ixpos[0]
        at_, tpos = region(s2)
        sbias = [at_(f"sbias{i}", P, SX) for i in range(2)]
        sbias = [sbias[0], sbias[0], sbias[1]]
        nbias = at_("nbias", P, 3 * TS)
        kn = [at_(f"kn{i}", P, 1024) for i in range(NKR)]
        kT = [at_(f"kT{i}", P, 512) for i in range(4)]
        vr = [at_(f"vr{i}", P, NPG * P) for i in range(NVR)]
        win_v = at_("win_v", P, 4 * 1024)
        sS = at_("sS", P, LS)
        sW = at_("sW", P, WIN + TS)
        sC = at_("sC", P, P)
        pT = at_("pT", P, 23 * P)
        imp = at_("imp", P, 5 * 40)
        bmask = at_("bmask", P, 2 * NSB)
        us = at_("us", P, 64)
        ou, _ = region(base_free)
        wo = [ou(f"wo{i}", P, KD * CW) for i in range(3)]
        wo_lo = [sb(f"wo_lo{i}", P, KD * CW, F32R, at=base_free + 4 * KD * CW * i) for i in range(3)]
        wo_hi = [ou(f"wo_hi{i}", P, KD * CW, F32R) for i in range(2)]
        mix_hi = ou("mix_hi", P, KD * TT, F32R)
        mix_lo = sb("mix_lo", P, KD * TT, F32R, at=base_free - 4 * KD * TT)
        yT = [ou(f"yT{i}", P, TT) for i in range(4)]
        xres = [ou(f"xres{i}", P, 5 * CW) for i in range(2)]
        yrow = [ou(f"yrow{i}", P, 5 * CW) for i in range(2)]

        ident = con[:, K_ID:K_ID + P]
        ones = con[:, K_ONE:K_ONE + P]

        bank = [ctx.enter_context(nc.psum_tensor(f"bank{i}", [P, 512], F32)) for i in range(8)]

        d_rows = nc.dram_tensor("bias_rows", (12, XL), F32).ap()
        d_rep = nc.dram_tensor("bias_repeated", (P, 12 * TXL), F32).ap()
        d_mix = nc.dram_tensor("mixed", (P, KD * TT), F32).ap()
        d_smp = nc.dram_tensor("bias_sample", (3, 16, SX), F32).ap()

        s_con = sem("s_con")
        s_con2 = sem("s_con2")
        s_x = [sem(f"s_x{i}") for i in range(2)]
        dve = sem("dve")
        act_ = sem("act_")
        ph_pe, ph_act, ph_dve, ph_pool = (sem(n) for n in ("ph_pe", "ph_act", "ph_dve", "ph_pool"))
        ixp_d, ixp_r, ixp_a, r_std, g_e, gs_in, iqh_in, pl_y2, pst_t, pst_ev, un_w, h_copied = (
            sem(n) for n in ("ixp_d", "ixp_r", "ixp_a", "r_std", "g_e", "gs_in", "iqh_in", "pl_y2", "pst_t", "pst_ev", "un_w", "h_copied"))
        su_tr = sem("su_tr")
        su_ev = sem("su_ev")
        c_e = sem("c_e")
        c_s = sem("c_s")
        b_ps = sem("b_ps")
        b_ev = sem("b_ev")
        b_dma = sem("b_dma")
        x_std = sem("x_std")
        x_n = sem("x_n")
        x_tr = sem("x_tr")
        x_ev = sem("x_ev")
        w_in_ = [sem(f"w_in{i}") for i in range(2)]
        w_free = sem("w_free")
        ada_c = sem("ada_c")
        ada_ps = sem("ada_ps")
        h_ready = sem("h_ready")
        m_done = sem("m_done")
        m_free = sem("m_free")
        n_sq = sem("n_sq")
        n_sum = sem("n_sum")
        n_std = sem("n_std")
        a_done = sem("a_done")
        a_free = sem("a_free")
        st_out = [sem(f"st_out{i}") for i in range(4)]
        sil_e = sem("sil_e")
        d_out = sem("d_out")
        pl_d = sem("pl_d")
        pl_y = sem("pl_y")
        pl_t = sem("pl_t")
        pl_c = sem("pl_c")
        w1_in = sem("w1_in")
        w1p_in = [sem(f"w1p_in{i}") for i in range(4)]
        cr_x, cr_ps, cr_ev = sem("cr_x"), sem("cr_ps"), sem("cr_ev")
        cp_ps = sem("cp_ps")
        cp_ev = sem("cp_ev")
        at_in = sem("at_in")
        q_ps = sem("q_ps")
        q_s = sem("q_s")
        q_e = sem("q_e")
        q_p = sem("q_p")
        q_t = sem("q_t")
        q_ta = sem("q_ta")
        q_td = sem("q_td")
        q_o = sem("q_o")
        q_m = sem("q_m")
        si_ps = sem("si_ps")
        si_ev = sem("si_ev")
        kb_in = [sem(f"kb_in{i}") for i in range(NIX)]
        kb_tr = sem("kb_tr")
        kb_a = sem("kb_a")
        kb_d = sem("kb_d")
        kb_mm = sem("kb_mm")
        xn_in = [sem(f"xn_in{i}") for i in range(4)]
        xn_tr = sem("xn_tr")
        xt_a = sem("xt_a")
        xt_d = sem("xt_d")
        hd_ps = sem("hd_ps")
        hd_ev = sem("hd_ev")
        kc_ps = sem("kc_ps")
        kc_x = sem("kc_x")
        kc_sum = sem("kc_sum")
        kc_std = sem("kc_std")
        kc_ok = sem("kc_ok")
        w1s_in = sem("w1s_in")
        w1a_in = sem("w1a_in")
        w1q_in = [sem(f"w1q_in{i}") for i in range(4)]
        w1h_a, w1l_d = sem("w1h_a"), sem("w1l_d")
        w1_used = sem("w1_used")
        hw_in = [sem(f"hw_in{q}") for q in range(4)]
        hw_used = sem("hw_used")
        hs_a, hs_d = sem("hs_a"), sem("hs_d")
        hh_a, hl_d = sem("hh_a"), sem("hl_d")
        sx_out = [sem(f"sx_out{i}") for i in range(2)]
        mx_in = sem("mx_in")
        mx_io = sem("mx_io")
        sb_in = sem("sb_in")
        vr_in = [sem(f"vr_in{i}") for i in range(NVR)]
        vh_in = [sem(f"vh_in{i}") for i in range(2)]
        kk_in = [sem(f"kk_in{i}") for i in range(NKR)]
        wv_in = sem("wv_in")
        pv_b = sem("pv_b")
        un_ps = sem("un_ps")
        un_s = sem("un_s")
        un_e = sem("un_e")
        un_p = sem("un_p")
        un_x = sem("un_x")
        im_ps = sem("im_ps")
        im_rd = sem("im_rd")
        im_in = sem("im_in")
        wo_in = [sem(f"wo_in{i}") for i in range(3)]
        xr_in = [sem(f"xr_in{i}") for i in range(2)]
        oh_a, ol_d = sem("oh_a"), sem("ol_d")
        y_ps = sem("y_ps")
        y_ev = sem("y_ev")
        y_tr = sem("y_tr")
        y_fin = sem("y_fin")
        y_out = sem("y_out")
        BIAS_BANKS = (0, 1, 2, 3, 7)
        block = ctx.enter_context(nc.Block())

        def v3(tensor, pattern, /, **k):
            return tensor[:, :].rearrange(pattern, **k)

        hT3 = v3(hT, "p (k t) -> p k t", t=TT)
        mix3 = v3(mix, "p (k t) -> p k t", t=TT)
        mod3 = v3(modT, "p (n b) -> p n b", b=9)
        asc3 = v3(ascale, "p (n b) -> p n b", b=9)
        aqT3 = v3(aqT, "p (h t) -> p h t", t=T)
        cqT3 = v3(cqT, "p (h t) -> p h t", t=T)
        iqT3 = v3(iqT, "p (h t) -> p h t", t=TT)
        bT3 = v3(bT, "p (g t) -> p g t", t=16 + T)
        bS4 = v3(bS, "p (g b t) -> p g b t", g=4, t=20)
        cmp4 = v3(cmpT, "p (c h t) -> p c h t", c=2, h=KVH)
        vnat3 = v3(vnat, "p (i c) -> p i c", c=2 * CW)
        MOFF = (0, 0, 256, 640)

        idx_of = {}
        for j, (kind, b, t, c) in enumerate(jobs):
            idx_of[(kind, b, t)] = j
        normT = [j for j, (k, b, t, c) in enumerate(jobs) if k in ("cq", "aq")]
        staged = [j for j, (k, b, t, c) in enumerate(jobs) if k in ("small", "ckv", "kcmp", "vcmp", "kslc", "kwin")]
        turned = [j for j in staged if not (jobs[j][0] in ("kcmp", "vcmp") and jobs[j][2] == QT)]
        silj = [j for j, (k, b, t, c) in enumerate(jobs) if k in SIL_AT]
        rownorm = [j for j, (k, b, t, c) in enumerate(jobs) if k in ("ckv", "kslc", "kwin")]

        def turns(j):
            return 2 if jobs[j][0] in ("kcmp", "vcmp", "kslc", "kwin") else 1

        def width(t):
            return P if t < QT else TS

        def wchunk(c, w):
            return wbuf[c % 2][:, 0:KD * w].rearrange("p (k n) -> p k n", n=w)

        cwidth = [sum(w for _, w in parts) for parts in chunks]
        cparts = [len(parts) for parts in chunks]
        NADA = 3 * D // CW
        need, count = {}, [0, 0]
        for n in range(NADA + len(chunks)):
            parts = 1 if n < NADA else cparts[n - NADA]
            count[n % 2] += 16 * parts
            need[n] = count[n % 2]

        def w_of(n):
            return need[NADA + n] if n >= 0 else None


        turned_set, staged_set = set(turned), set(staged)
        last_job = {c: j for j, (_, _, _, c) in enumerate(jobs)}
        ix_slot, n_ = {}, 0
        for i in range(1, QT):
            for x in range(4):
                ix_slot[idx_of[("kcmp", 0, 0)] + 8 * (i - 1) + x] = ("dots", i, x, n_)
                ix_slot[idx_of[("kcmp", 0, 0)] + 8 * (i - 1) + 4 + x] = ("topk", i, x)
                n_ += 1
        units = [("A", i, h) for i in range(QT) for h in range(AH)] + [("C", i, h) for i in range(QT) for h in range(CH)]
        NUA = QT * AH
        sblocks, kloads = [], []
        for u in range(2):
            for kind, nq in (("win", 1), ("slc", 4)):
                for b in range(4 * u, 4 * u + 4):
                    for q in range(nq):
                        for k in range(KVH):
                            sblocks.append((u, kind, b, q, k, len(kloads)))
                        kloads.append((1 if kind == "win" else 4, len(sblocks) - 1, (u, kind, b, q)))
        for b in range(DB):
            for q in range(4):
                sblocks.append((2, "c", b, q, 0, len(kloads)))
                kloads.append((4, len(sblocks) - 1, (2, "c", b, q)))
        kneed, kc_ = [], [0] * NIX
        for m in range(32):
            kc_[m % NIX] += 64
            kneed.append(kc_[m % NIX])
        kkneed, kc_ = [], [0] * NKR
        for m, (k_, _, _) in enumerate(kloads):
            kc_[m % NKR] += 16 * k_
            kkneed.append(kc_[m % NKR])
        vneed, vc_ = [], [0] * NVR
        for m in range(24):
            if m < 16 or m % 2:
                vc_[m % NVR] += 16 * (8 if m < 16 else 16)
                vneed.append((vr_in[m % NVR], vc_[m % NVR]))
            else:
                vneed.append((vh_in[m % NVR // 2], 16 * NPG * (m // 4 - 3)))
        NBLK = (40, 40, 32)
        FIRSTB = (0, 40, 80)
        STEPS = (("head", 0), ("body", 0), ("head", 1), ("turn", 0), ("body", 1), ("head", 2), ("turn", 1), ("body", 2), ("turn", 2))

        def blocks_of(step, u):
            f = FIRSTB[u]
            return range(f, f + 8) if step == "head" else range(f + 8, f + NBLK[u])

        def pgroups(u):
            t = [(sS[:, i * P:(i + 1) * P], P) for i in range(16)] + [(sS[:, PAST:LS], TS)]
            if u < 2:
                t += [(sW[:, i * P:(i + 1) * P], P) for i in range(4)] + [(sW[:, WIN:WIN + TS], TS), (sC[:, 0:NCS], NCS)]
            return [t[i:i + 4] for i in range(0, len(t), 4)]

        kb_gt, g_ = {}, 32
        for step, u in STEPS:
            if step == "turn":
                g_ += len(pgroups(u))
            else:
                for n in blocks_of(step, u):
                    kb_gt[n] = g_
                    g_ += 1

        cc = I["cache_c_kv"].rearrange("l n p a c -> (l n) p a c")
        ca = I["cache_a_kv"].rearrange("l n p a h c -> (l n) p a h c")

        def pages_of(eng, regs):
            held = [None]

            def page(b, i):
                if held[0] != b:
                    eng.load(regs, ptab[0:1, b * NPG:(b + 1) * NPG])
                    held[0] = b
                return eng.snap(regs[i], min_val=0, max_val=NPOOL - 1)
            return page

        def values(eng, page, m):
            if m >= NVR:
                eng.wait_ge(pv_b, m - NVR + 1)
            slot, s = vr[m % NVR], vneed[m][0]
            if m < 16:
                for i in range(8):
                    r = page(m // 2, 8 * (m % 2) + i)
                    eng.dma_start(slot[:, i * 256:(i + 1) * 256], ca[bass.ds(r, 1), :, 3, :, :].rearrange("a p h c -> (a p) (h c)")).then_inc(s, 16)
            else:
                for i in range(NPG):
                    r = page(m - 16, i)
                    eng.dma_start(slot[:, i * P:(i + 1) * P], cc[bass.ds(r, 1), :, 1, :].rearrange("a p c -> (a p) c")).then_inc(s, 16)

        def bc(ap, n):
            return ap.unsqueeze(2).broadcast_to([ap.shape[0], ap.shape[1], n])

        def after(eng, n):
            eng.wait_ge(ph_pe, n)
            eng.wait_ge(ph_act, n)
            eng.wait_ge(ph_dve, n)
            if n == 1:
                eng.wait_ge(ph_pool, 1)

        def turned_to(kind, t, x):
            a, w = t * P, width(t)
            if kind == "small":
                return ikT[:, a:a + P] if t < QT else kiN[:, :]
            if kind == "ckv":
                return ckT[:, a:a + P] if t < QT else ksN[:, 4 * TS:5 * TS]
            if kind in ("kcmp", "vcmp"):
                return cmp4[:, 0 if kind == "kcmp" else 1, x, a:a + P]
            o = 0 if kind == "kslc" else 2
            return (kslcT, kwinT)[o // 2][:, x * T + a:x * T + a + P] if t < QT else ksN[:, (o + x) * TS:(o + x + 1) * TS]

        def evac_x(eng, A, t):
            w = width(t)
            for q in range(4):
                g = 4 * t + q
                eng.wait_ge(x_tr, g + 1)
                eng.copy(hT3[:, 4 * q:4 * q + 4, t * P:t * P + w], bank[g % 4][:, 0:4 * w].rearrange("p (k t) -> p k t", k=4)).then_inc(x_ev, 1)

        def turned_rows(x):
            n, q, h = x // 8, x % 8 // 2, x % 2
            return [t[n % 2][:, 0:2 * PAST].rearrange("p (h s c) -> p h c s", h=2, s=16)[:, h, 32 * q:32 * q + 32, :] for t in (xth, xtl)] \
                + [bank[4 + x % 2][:, :].rearrange("p (c s) -> p c s", s=16)]

        SPLIT_AT = {0: (0, 1), 1: (2,), 3: (3,)}

        def half_ahead(j, half):
            return 2 * (j - J0) + half if J0 <= j < njobs else None

        def quarter(t, i):
            return t[:, i * 8 * 256:(i + 1) * 8 * 256]

        def take_p(eng, copy, u, gi, src, s):
            if u >= 1:
                eng.wait_ge(pv_b, 8 * u)
            b, i = bank[5 + (s is kb_d)], 0
            while i < len(src):
                j = i
                while j < len(src) and src[j][1] == src[i][1]:
                    j += 1
                r = src[i][1]
                last = copy(pT[0:r, (4 * gi + i) * P:(4 * gi + j) * P], b[0:r, i * P:j * P])
                i = j
            last.then_inc(s, 1)

        def take_k(eng, copy, n, gt, s):
            eng.wait_ge(kb_tr, gt + 1)
            if n >= 4:
                eng.wait_ge(kb_mm, 32 + n - 3)
            copy(kT[n % 4][:, :], bank[5 + gt % 2][:, :]).then_inc(s, 1)

        def unit_exps(eng, A, u, when):
            if when == "early":
                eng.wait_ge(un_w, u + 1)
                A(sC[:, 0:NCS], sC[:, 0:NCS], ACT.Exp, bias=us[:, 4:5], accum_out=us[:, 8:9])
                A(sW[:, :], sW[:, :], ACT.Exp, bias=us[:, 5:6], accum_out=us[:, 9:10]).then_inc(un_e, 1)
            else:
                eng.wait_ge(un_s, u + 1)
                A(sS[:, :], sS[:, :], ACT.Exp, bias=us[:, 6:7], accum_out=us[:, 10:11]).then_inc(un_e, 1)

        def early(v, V, u, link, ttr):
            v.wait_ge(un_ps, 2 * u + 1)
            link(V.tensor_tensor(sW[:, 0:WIN], bank[0][:, :], sbias[u][:, PAST - WIN:PAST], ALU.add))
            link(V.tensor_tensor(sW[:, WIN:WIN + TS], bank[4][:, 32:64], nbias[:, u * TS:(u + 1) * TS], ALU.add))
            link(V.tensor_tensor(sW[:, 0:4], sW[:, 0:4], con[:, K_WIN:K_WIN + 4], ALU.add))
            link(ttr(sC[:, 0:NCS], bank[4][:, 64:64 + NCS], sbias[u][:, 31:31 + 16 * (NCS - 1) + 1:16], us[:, 0:1]))
            link(V.tensor_reduce(us[:, 1:2], sW[:, :], AX.X, ALU.max))
            V.tensor_scalar(us[:, 4:6], us[:, 0:2], -1.0, None, ALU.mult).then_inc(un_w, 1)

        def mid(v, V, u, link):
            v.wait_ge(un_e, 2 * u + 1)
            link(V.tensor_scalar(us[:, 12:14], us[:, 8:10], 1e-30, None, ALU.max))
            link(V.reciprocal(us[:, 12:14], us[:, 12:14]))
            V.tensor_scalar(sC[:, 0:NCS], sC[:, 0:NCS], us[:, 12:13], None, ALU.mult).then_inc(im_in, 1)
            v.wait_ge(im_in, u + 1)

        def select(v, V, u, link):
            v.wait_ge(im_ps, u + 1)
            link(V.memset(imp[:, :], 0.0))
            V.tensor_copy(imp[:, 1:1 + NCS], bank[4][:, 192:192 + NCS]).then_inc(im_rd, 1)
            v.wait_ge(im_rd, u + 1)
            at = [imp[:, k:k + 4 * (NSB - 1) + 1:4] for k in range(5)]
            t = imp[:, 136:136 + NSB]
            link(V.tensor_tensor(t, at[1], at[2], ALU.add))
            link(V.tensor_tensor(t, t, at[3], ALU.add))
            link(V.scalar_tensor_tensor(out=t, in0=t, scalar=2.0, in1=at[0], op0=ALU.mult, op1=ALU.add))
            link(V.tensor_tensor(t, t, at[4], ALU.add))
            link(V.tensor_tensor(t, t, con[:, K_FB:K_FB + NSB], ALU.max))
            for _ in range(TOPB // 8):
                link(V.max(us[:, 24:32], t))
                link(V.match_replace(t, us[:, 24:32], t, MARK))
            link(V.tensor_scalar(bmask[:, 0:NSB], t, MARK, NEG, ALU.not_equal, ALU.mult))
            link(V.tensor_scalar(sC[:, 0:NCS], sC[:, 0:NCS], gateS[:, u:u + 1], None, ALU.mult))
            link(V.tensor_scalar(sW[:, :], sW[:, :], us[:, 13:14], gateS[:, 4 + u:5 + u], ALU.mult, ALU.mult))

        def late(v, V, u, link, ttr):
            v.wait_ge(un_ps, 2 * u + 2 if u < 2 else 5)
            for f in range(4):
                V.tensor_tensor(sS[:, 512 * f:512 * f + 512], bank[f][:, :], sbias[u][:, 512 * f:512 * f + 512], ALU.add)
            link(V.tensor_tensor(sS[:, PAST:LS], bank[4][:, 0:TS], nbias[:, u * TS:(u + 1) * TS], ALU.add))
            if u < 2:
                s3 = sS[:, 0:PAST].rearrange("p (n s) -> p n s", s=64)
                link(V.tensor_tensor(s3, s3, bc(bmask[:, 0:32], 64), ALU.add))
                link(V.tensor_reduce(us[:, 2:3], sS[:, :], AX.X, ALU.max))
            else:
                link(ttr(sS[:, :], sS[:, :], wrk[:, :], us[:, 2:3]))
            V.tensor_scalar(us[:, 6:7], us[:, 2:3], -1.0, None, ALU.mult).then_inc(un_s, 1)
            v.wait_ge(un_e, 2 * u + 2 if u < 2 else 5)
            link(V.tensor_scalar(us[:, 14:15], us[:, 10:11], 1e-30, None, ALU.max))
            link(V.reciprocal(us[:, 14:15], us[:, 14:15]))
            if u < 2:
                link(V.tensor_scalar(us[:, 14:15], us[:, 14:15], gateS[:, 2 + u:3 + u], None, ALU.mult))
            V.tensor_scalar(sS[:, :], sS[:, :], us[:, 14:15], None, ALU.mult).then_inc(un_p, 1)

        out_split = [("w", 0)] + [("mix", k) for k in range(KD)] + [("w", nb) for nb in range(1, KD)]

        def out_views(kind, n):
            if kind == "mix":
                return [v3(x, "p (k t) -> p k t", t=TT)[:, n, :] for x in (mix, mix_hi, mix_lo)]
            c, cols = n // 2, slice(n % 2 * P, (n % 2 + 1) * P)
            return [v3(x, "p (k n) -> p k n", n=CW)[:, :, cols] for x in (wo[c % 3], wo_hi[c % 2], wo_lo[c % 3])]

        def pool_out(v, V, g):
            v.wait_ge(pl_y, g + 1)
            v.wait_ge(mx_in, 16)
            for f in range(2):
                m = mix3[:, 8 + g, f * HALF:(f + 1) * HALF]
                last = V.scalar_tensor_tensor(out=m, in0=bank[2 * (g % 2) + f][:, 0:HALF], scalar=vecT[:, V_BSC + g:V_BSC + g + 1], in1=m, op0=ALU.mult, op1=ALU.mult)
            last.then_inc(pl_y2, 1)

        small_loads = ([(con[:, :], I["constants"]), (crow[0:1, :], I["c_prompt"]), (crow[1:9, :], I["c_sample"]),
                        (vrow[V_BADA:V_BADA + 48, :], I["b_ada"].rearrange("a (n p) -> (a n) p", p=P)),
                        (vrow[V_G:V_G + 16, :], I["norm_g"].rearrange("a (n p) -> (a n) p", p=P)),
                        (vrow[V_BSC:V_BSC + 4, :], I["b_scale"].rearrange("a (n p) -> (a n) p", p=P)),
                        (vrow[V_B1:V_B1 + 4, :], I["a_cmp_b1"].rearrange("a c (n p) -> (a c n) p", p=P)),
                        (vrow[V_B2:V_B2 + 2, :], I["a_cmp_b2"].rearrange("a c p -> (a c) p")),
                        (vrow[V_AQ:V_AQ + 1, :], I["a_qnorm"]), (vrow[V_CQ:V_CQ + 1, :], I["c_qnorm"]),
                        (vrow[V_AK:V_AK + 3, :], I["a_knorm"].rearrange("a c p -> (a c) p")),
                        (vrow[V_CK:V_CK + 1, :], I["c_knorm"]),
                        (prow[:, :], I["a_cmp_pe"].rearrange("a c s p -> (a c s) p"))],
                       [(ohr[:, :], I["bucket_rows"]),
                        (relb[0:NB_, :], I["rel_bias"]), (relb[NB_:NB_ + 1, :], I["constants"][0:1, K_ONE:K_ONE + 12]),
                        (expd[:, :], I["expanders"]),
                        (ptab[:, :], I["page_table"].rearrange("(a b) n -> a (b n)", a=1)),
                        (bst[:, :], I["state_b_pool"].rearrange("a b t c -> (a b t) c")),
                        (v3(wpool, "p (g d) -> p g d", g=4), I["b_pool_w"][0].rearrange("g c d -> c g d"))]
                       + [(gk[:, n * P:(n + 1) * P], bass.AP(src.tensor, src.offset, [[0, P], [1, P]]))
                          for n, src in enumerate((I["a_knorm"][0, 1:2, :], I["a_knorm"][0, 2:3, :], I["c_knorm"], I["a_cmp_b2"][0, 1:2, :]))])
        assert [len(x) for x in small_loads] == [NSMALL1, NSMALL2]

        w1 = [I["a_cmp_w1"][0, n].rearrange("(s p) h -> p s h", p=P) for n in range(2)]

        @block.sync
        def _(sp):
            for o, i in small_loads[0]:
                sp.dma_start(o, i).then_inc(s_con, 16)

            wada = I["w_ada"][0].rearrange("(k p) n -> p k n", p=P)
            win = I["w_in"][0].rearrange("(k p) n -> p k n", p=P)
            for n in range(NADA + nwhole):
                if 2 <= n < NADA + 2:
                    sp.wait_ge(w_free, n - 1)
                elif n >= 2:
                    sp.wait_ge(m_done, last_job[n - 2 - NADA] + 1)
                if n < NADA:
                    sp.dma_start(v3(wbuf[n % 2], "p (k n) -> p k n", n=CW), wada[:, :, n * CW:(n + 1) * CW]).then_inc(w_in_[n % 2], 16)
                else:
                    c = n - NADA
                    off = 0
                    for col, w in chunks[c]:
                        sp.dma_start(wchunk(n, cwidth[c])[:, :, off:off + w], win[:, :, col:col + w]).then_inc(w_in_[n % 2], 16)
                        off += w

            for x in range(2 * (njobs - J0)):
                if x < 4:
                    sp.wait_ge(m_done, last_job[nwhole - 2 + x // 2] + 1)
                elif x % 2 == 0:
                    sp.wait_ge(hw_used, x // 2 - 1)
                else:
                    sp.wait_ge(m_done, J0 + x // 2 - 1)
                col = chunks[nwhole + x // 2][0][0]
                sp.dma_start(v3(hw_raw[x % 4], "p (k n) -> p k n", n=P), win[:, x % 2 * 8:x % 2 * 8 + 8, col:col + P]).then_inc(hw_in[x % 4], 16)
            sp.wait_ge(m_done, njobs)
            for i in range(2):
                sp.wait_ge(sx_out[i], 16 * KD // 2)
            sp.dma_start(mix[:, :], d_mix).then_inc(mx_in, 16)
            for i in range(4):
                if i == w1_early:
                    after(sp, 1)
                    for kv in range(2):
                        sp.dma_start(w2P[:, kv * 256:kv * 256 + 256].rearrange("p (n d) -> p n d", n=2), I["a_cmp_w2"][0, kv].rearrange("(n p) d -> p n d", p=P)).then_inc(w1_in, 16)
                kv, s0 = i // 2, i % 2 * 16
                sp.dma_start(w1P[kv][:, s0 * 256:(s0 + 16) * 256].rearrange("p (s h) -> p s h", h=256),
                             I["a_cmp_w1"][0, kv].rearrange("(s p) h -> p s h", p=P)[:, s0:s0 + 16]).then_inc(w1p_in[i], 16)
            sp.wait_ge(cr_ps, 1)
            sp.wait_ge(b_dma, 32 + 64)
            sp.dma_start(v3(bias, "p (h j) -> p h j", h=12), bass.AP(d_rep.tensor, d_rep.offset + 127, [[12 * TXL - 1, P], [TXL, 12], [1, T]])).then_inc(at_in, 16)
            after(sp, 2)
            sp.dma_start(v3(w1S, "p (s h) -> p s h", h=256), w1[0]).then_inc(w1a_in, 16)

            after(sp, 3)

            regs = [sp.alloc_register(f"page{i}") for i in range(NPG)]

            cki = I["cache_c_kidx"].rearrange("l n p c -> (l n) p c")
            for n in range(32):
                if n == 8:
                    sp.dma_start(d_mix, mix[:, :]).then_inc(mx_io, 16)
                if n >= NIX:
                    sp.wait_ge(kb_tr, n - NIX + 1)
                if n % 4 == 0:
                    sp.load(regs, ptab[0:1, n * 4:n * 4 + NPG])
                for q in range(4):
                    r = sp.snap(regs[4 * (n % 4) + q], min_val=0, max_val=NPOOL - 1)
                    sp.dma_start(ixn[n % NIX][:, q * ID:(q + 1) * ID], cki[bass.ds(r, 1), :, :].rearrange("a p c -> (a p) c")).then_inc(kb_in[n % NIX], 16)
            after(sp, 4)
            for kv in range(2):
                if kv == 0:
                    for n in range(2):
                        sp.dma_start(w2S[:, n * 256:n * 256 + 256].rearrange("p (n d) -> p n d", n=2), I["a_cmp_w2"][0, n].rearrange("(n p) d -> p n d", p=P)).then_inc(w1s_in, 16)
                for b in range(DB):
                    sp.load(regs, ptab[0:1, b * NPG:(b + 1) * NPG])
                    for q in range(4):
                        n = (kv * DB + b) * 4 + q
                        if n >= 4:
                            sp.wait_ge(xn_tr, 2 * (n - 3))
                        for i in range(4):
                            r = sp.snap(regs[4 * q + i], min_val=0, max_val=NPOOL - 1)
                            sp.dma_start(xnat[n % 4][:, i * 256:(i + 1) * 256].rearrange("p (h c) -> p h c", h=2), ca[bass.ds(r, 1), :, kv, :, :].rearrange("a p h c -> (a p) h c")).then_inc(xn_in[n % 4], 16)
            after(sp, 5)
            sp.wait_ge(b_dma, 32 + 64)
            for b in range(4):
                sp.dma_start(sbias[0][32 * b:32 * b + 32, :], d_smp[0:2].rearrange("u r x -> (u r) x")).then_inc(sb_in, 16)
            for b in range(DB):
                sp.dma_start(sbias[2][16 * b:16 * b + 16, :], d_smp[2]).then_inc(sb_in, 16)
            sw = I["state_a_win"][0]
            page = pages_of(sp, regs)

            def keys(step, u):
                for m, (_, last, (lu, kind, b, q)) in enumerate(kloads):
                    if last not in blocks_of(step, u):
                        continue
                    if m >= NKR:
                        sp.wait_ge(kb_tr, kb_gt[kloads[m - NKR][1]] + 1)
                    slot, s = kn[m % NKR], kk_in[m % NKR]
                    if kind == "win":
                        sp.dma_start(v3(slot, "p (i c) -> p i c", c=256), sw[b, :, 0, :, :].rearrange("(i p) h c -> p i (h c)", p=P)).then_inc(s, 16)
                    for i in range(4 if kind != "win" else 0):
                        r = page(b, 4 * q + i)
                        if kind == "slc":
                            sp.dma_start(slot[:, i * 256:(i + 1) * 256], ca[bass.ds(r, 1), :, 2, :, :].rearrange("a p h c -> (a p) (h c)")).then_inc(s, 16)
                        else:
                            sp.dma_start(slot[:, i * P:(i + 1) * P], cc[bass.ds(r, 1), :, 0, :].rearrange("a p c -> (a p) c")).then_inc(s, 16)

            for step, u in STEPS:
                if step == "turn":
                    continue
                keys(step, u)
                if (step, u) == ("head", 1):
                    sp.dma_start(mix[:, :], d_mix).then_inc(mx_io, 16)
                if (step, u) in (("body", 0), ("head", 2)):
                    if u == 2:
                        sp.wait_ge(pv_b, 8)
                    for b in range(2 * u, 2 * u + 4):
                        sp.dma_start(win_v[:, b % 4 * 1024:(b % 4 + 1) * 1024].rearrange("p (i c) -> p i c", c=256), sw[b, :, 1, :, :].rearrange("(i p) h c -> p i (h c)", p=P)).then_inc(wv_in, 16)
            for m in range(16, 24, 2):
                values(sp, page, m)
            after(sp, 6)
            wout = I["w_out"][0].rearrange("(k p) n -> p k n", p=P)
            for c in range(D // CW):
                if c >= 3:
                    sp.wait_ge(y_ps, 2 * (c - 2))
                sp.dma_start(v3(wo[c % 3], "p (k n) -> p k n", n=CW), wout[:, :, c * CW:(c + 1) * CW]).then_inc(wo_in[c % 3], 16)
                if c >= 2:
                    sp.wait_ge(y_fin, 4 * (c - 1))
                x5, cols = v3(xres[c % 2], "p (i d) -> p i d", i=5), slice(c * CW, (c + 1) * CW)
                sp.dma_start(x5[:, 0:QT, :], I["x_prompt"][0].rearrange("(i p) d -> p i d", p=P)[:, :, cols]).then_inc(xr_in[c % 2], 16)
                sp.dma_start(x5[0:TS, QT, :], I["x_sample"].rearrange("b t d -> (b t) d")[:, cols]).then_inc(xr_in[c % 2], 16)

        @block.gpsimd
        def _(pool):
            outs = 0

            def out(o, i, s=None):
                nonlocal outs
                ins = pool.dma_start(o, i)
                if s is None:
                    ins.then_inc(d_out, 16)
                    outs += 1
                else:
                    ins.then_inc(s, 16)

            xp = I["x_prompt"].rearrange("a (t p) d -> (a t) p d", p=P)
            for t in range(QT + 1):
                if t >= 2:
                    pool.wait_ge(x_tr, 4 * (t - 1))
                if t < QT:
                    pool.dma_start(xrow[t % 2][:, :], xp[t]).then_inc(s_x[t % 2], 16)
                else:
                    pool.dma_start(xrow[t % 2][0:TS, :], I["x_sample"].rearrange("b t d -> (b t) d")).then_inc(s_x[t % 2], 16)
                if t == 1:
                    for o, i in small_loads[1]:
                        pool.dma_start(o, i).then_inc(s_con2, 16)
            pool.wait_ge(b_ev, 5)
            pool.dma_start(d_rows, btmp[:, :]).then_inc(b_dma, 16)
            pool.wait_ge(b_dma, 16)
            pool.dma_start(d_rep.rearrange("p (h x) -> p h x", h=12), bass.AP(d_rows.tensor, d_rows.offset + TX0, [[0, P], [XL, 12], [1, TXL]])).then_inc(b_dma, 16)
            for t in range(DT):
                pool.dma_start(d_smp.rearrange("u (t g) x -> t u g x", t=DT)[t], bass.AP(d_rows.tensor, d_rows.offset + 3 - t, [[4 * XL, 3], [XL, 4], [1, SX]])).then_inc(b_dma, 16)
            o_akp = O["a_kv_p"].rearrange("l b (i p) a h c -> (l b i) p a (h c)", p=P)
            o_aks = O["a_kv_s"].rearrange("l b t a h c -> (l b t) a (h c)")
            o_ckp = O["c_kv_p"].rearrange("l b (i p) a c -> (l b i) p (a c)", p=P)
            o_cks = O["c_kv_s"].rearrange("l b t a c -> (l b t) (a c)")
            o_kip = O["c_kidx_p"].rearrange("l b (i p) c -> (l b i) p c", p=P)
            o_kis = O["c_kidx_s"].rearrange("l b t c -> (l b t) c")
            o_wp = O["a_win_p"].rearrange("l b (i p) a h c -> (l b i) p a (h c)", p=P)
            comp = {"kcmp": 0, "vcmp": 1, "kslc": 2, "vslc": 3}
            for j, (kind, b, t, c) in enumerate(jobs):
                if kind in SIL_AT:
                    n, blk = silj.index(j), SIL_AT[kind] + b
                    pool.wait_ge(m_free, j + 1)
                    pool.dma_start(d_mix[:, blk * TT:(blk + 1) * TT], (sq, rs)[n % 2][:, :]).then_inc(sx_out[n % 2], 16)
                if kind not in ROW_KINDS:
                    continue
                w = width(t)
                if j == idx_of[("kcmp", 0, 0)]:
                    out(O["a_win_s"][0, :, 0:WIN - DT].rearrange("b n a h c -> b n (a h c)"), I["state_a_win"][0, :, DT:WIN].rearrange("b n a h c -> b n (a h c)"))
                    out(O["b_pool_s"][0, :, 0:11, :], I["state_b_pool"][0, :, 4:15, :])
                    pool.dma_start(v3(iqh, "p (c t) -> p c t", c=2), iqT3[ID:2 * ID, :, T:TT]).then_inc(iqh_in, 16)
                if j in staged:
                    n = staged.index(j)
                    pool.wait_ge(m_free, j + 1)
                    s, si = stage[n % 4], st_out[n % 4]
                    if kind == "small":
                        out(o_kip[t] if t < QT else o_kis, s[0:w, 0:ID], si)
                    elif kind == "ckv":
                        out(o_ckp[t] if t < QT else o_cks, s[0:w, :], si)
                    elif kind in comp:
                        out(o_akp[t, :, comp[kind]] if t < QT else o_aks[:, comp[kind]], s[0:w, :], si)
                    elif t < QT:
                        out(o_wp[t, :, 0], s[:, :], si)
                    else:
                        for b in range(DB):
                            out(O["a_win_s"][0, b, WIN - DT:WIN, 0].rearrange("t h c -> t (h c)"), s[DT * b:DT * b + DT, :], si if b == 0 else None)
                else:
                    pool.wait_ge(m_free, j + 1)
                    v = 0 if kind == "vslc" else 1
                    src = vnat3[:, t, v * CW:(v + 1) * CW] if t < QT else vN[:, v * CW:(v + 1) * CW]
                    if kind == "vslc":
                        out(o_akp[t, :, 3] if t < QT else o_aks[:, 3], src)
                    elif t < QT:
                        out(o_wp[t, :, 1], src)
                    else:
                        for b in range(DB):
                            out(O["a_win_s"][0, b, WIN - DT:WIN, 1].rearrange("t h c -> t (h c)"), vN[DT * b:DT * b + DT, CW:2 * CW])
            pool.wait_ge(pl_c, 2)
            out(O["b_pool_p"][0, 0], prw[1:16, 0:512])
            for b in range(DB):
                out(O["b_pool_s"][0, b, 11:15, :], prw[DT * b:DT * b + DT, 512:1024])
            for i in range(4):
                pool.wait_ge(st_out[i], 16 * len(range(i, len(staged), 4)))
            pool.wait_ge(d_out, 16 * outs)
            pool.drain().then_inc(ph_pool, 1)
            for i in range(4):
                if i < 3:
                    pool.wait_ge(w1_used, i + 1)
                else:
                    pool.wait_ge(hd_ps, DB)
                pool.dma_start(quarter(w1S, i).rearrange("p (s h) -> p s h", h=256), w1[1][:, 8 * i:8 * i + 8]).then_inc(w1q_in[i], 16)
            after(pool, 5)
            page = pages_of(pool, [pool.alloc_register(f"value_page{i}") for i in range(NPG)])
            for m in [*range(16), *range(17, 24, 2)]:
                values(pool, page, m)
            oy = O["y_prompt"].rearrange("a (i p) d -> p (a i) d", p=P)
            oys = O["y_sample"].rearrange("b t d -> (b t) d")
            for c in range(D // CW):
                pool.wait_ge(y_fin, 4 * (c + 1))
                pool.dma_start(oy[:, :, c * CW:(c + 1) * CW], v3(yrow[c % 2], "p (i d) -> p i d", i=5)[:, 0:QT, :]).then_inc(y_out, 16)
                pool.dma_start(oys[:, c * CW:(c + 1) * CW], v3(yrow[c % 2], "p (i d) -> p i d", i=5)[0:TS, QT, :]).then_inc(y_out, 16)
                pool.wait_ge(y_out, 32 * (c + 1))

        @block.tensor
        def _(pe):
            mm, tr = nc.tensor.matmul, nc.tensor.transpose

            def end_phase():
                pe.drain().then_inc(ph_pe, 1)

            pe.wait_ge(s_con, 16 * NSMALL1)
            tr(bank[7][:, 0:NV], vrow[:, :], con[0:NV, 0:NV])
            tr(bank[7][:, 128:192], prow[:, :], con[0:64, 0:64])
            for k in range(KD):
                last = tr(bank[7][:, 256 + 9 * k:265 + 9 * k], crow[:, k * P:(k + 1) * P], con[0:9, 0:9])
            last.then_inc(su_tr, 1)

            def bias_rows():
                pe.wait_ge(s_con2, 16 * NSMALL2)
                for n in range(5):
                    w = min(512, XL - 512 * n)
                    mm(bank[BIAS_BANKS[n]][0:12, 0:w], relb[:, :], ohr[:, 512 * n:512 * n + w], start=True, stop=True).then_inc(b_ps, 1)

            def turn_x(t):
                w = width(t)
                pe.wait_ge(x_n, t + 1)
                for q in range(4):
                    g = 4 * t + q
                    if g < 4:
                        pe.wait_ge(b_ev, g + 1)
                    else:
                        pe.wait_ge(x_ev, g - 3)
                    for i in range(4):
                        k = 4 * q + i
                        last = tr(bank[g % 4][:, i * w:(i + 1) * w], xrow[t % 2][0:w, k * P:(k + 1) * P], con[0:w, 0:w])
                    last.then_inc(x_tr, 1)

            def ada_sum(n):
                pe.wait_ge(ada_c, n + 1)
                if n == 16:
                    pe.wait_ge(b_ev, 5)
                o = bank[5] if n < 16 else bank[7]
                for j in range(2):
                    last = mm(o[:, (2 * n + j) * 9:(2 * n + j + 1) * 9], mpart[n % 2][:, j * P:(j + 1) * P],
                              con[:, K_SEL:K_SEL + 9], start=True, stop=True)
                last.then_inc(ada_ps, 1)

            pe.wait_ge(c_s, 1)
            for n in range(NADA):
                pe.wait_ge(w_in_[n % 2], need[n])
                if n >= 2:
                    pe.wait_ge(ada_c, n - 1)
                ada_w = v3(wbuf[n % 2], "p (k n) -> p k n", n=CW)
                for k in range(KD):
                    r = 32 * (k % 4)
                    last = mm(bank[4 + 2 * (n % 2)][r:r + 32, 0:CW], cpad[:, 32 * k:32 * k + 32], ada_w[:, k, :],
                              start=(k < 4), stop=(k >= KD - 4), tile_position=(0, r))
                last.then_inc(w_free, 1)
                if n >= 1:
                    ada_sum(n - 1)
                if n % 3 == 2 and n // 3 <= QT:
                    if n == 2:
                        bias_rows()
                    turn_x(n // 3)
            ada_sum(NADA - 1)
            for g in range(4):
                last = tr(bank[6][:, g * 120:(g + 1) * 120], bst[:, g * P:(g + 1) * P], con[0:120, 0:120])
            last.then_inc(pst_t, 1)

            aux = 0

            def hook(j):
                nonlocal aux
                if j >= 1:
                    i = j - 1
                    kind, b, t, c = jobs[i]
                    if i in turned_set:
                        w = width(t)
                        pe.wait_ge(m_free, i + 1)
                        s = stage[staged.index(i) % 4]
                        for x in range(turns(i)):
                            if aux >= 2:
                                pe.wait_ge(a_free, aux - 1)
                            if aux < 2:
                                pe.wait_ge(pst_ev, 1)
                                pe.wait_ge(h_copied, 2)
                            tr(bank[6 + aux % 2][:, 0:w], s[0:w, x * P:(x + 1) * P], con[0:w, 0:w]).then_inc(a_done, 1)
                            aux += 1
                    if kind in ("cq", "aq"):
                        n = normT.index(i)
                        pe.wait_ge(n_sq, n + 1)
                        if n >= 1:
                            pe.wait_ge(n_std, n)
                        else:
                            pe.wait_ge(ixp_r, 12)
                        for f in range(2):
                            last = mm(bank[4 + f][:, 0:HALF], ones, sq[:, f * HALF:(f + 1) * HALF], start=True, stop=True)
                        last.then_inc(n_sum, 1)
                if j in ix_slot:
                    s = ix_slot[j]
                    if s[0] == "dots":
                        _, i, h, n = s
                        if n == 0:
                            pe.wait_ge(h_copied, 1)
                        if n >= 2:
                            pe.wait_ge(ixp_r, n - 1)
                        r0 = 64 * (h % 2)
                        mm(bank[4 + n % 2][:, 0:P * (i + 1)], iqT3[r0:r0 + 64, h // 2, i * P:(i + 1) * P],
                           ikT[r0:r0 + 64, 0:P * (i + 1)], start=True, stop=True).then_inc(ixp_d, 1)

            pe.wait_ge(h_ready, HREADY)
            pe.wait_ge(x_ev, 20)
            for j, (kind, b, t, c) in enumerate(jobs):
                if j >= 2:
                    pe.wait_ge(m_free, j - 1)
                if j >= J0:
                    hh = v3(h_hi, "p (k t) -> p k t", t=TT)
                    hl = v3(h_lo, "p (k t) -> p k t", t=TT)
                    for k in range(KD):
                        x = 2 * (j - J0) + k // 8
                        if k % 8 == 0:
                            pe.wait_ge(hs_d, x + 1)
                        if k == 8:
                            hook(j)
                        if j == J0:
                            pe.wait_ge(hl_d, k + 1)
                        wh, wl = (v3(t_[x % 4], "p (k n) -> p k n", n=P)[:, k % 8, :] for t_ in (hw_hi, hw_lo))
                        for f in range(2):
                            o, tc = bank[2 * (j % 2) + f][:, 0:HALF], slice(f * HALF, (f + 1) * HALF)
                            mm(o, wh, hl[:, k, tc], start=(k == 0), stop=False)
                            mm(o, wl, hh[:, k, tc], start=False, stop=False)
                            last = mm(o, wh, hh[:, k, tc], start=False, stop=(k == KD - 1))
                        if k == 7:
                            last.then_inc(hw_used, 1)
                    last.then_inc(m_done, 1)
                    continue
                n = NADA + c
                wv = wchunk(n, cwidth[c])
                pe.wait_ge(w_in_[n % 2], need[n])
                if kind in ROW_KINDS:
                    w = width(t)
                    for k in range(KD):
                        if k == 8:
                            hook(j)
                        last = mm(bank[2 * (j % 2)][0:w, 0:cwidth[c]], hT3[:, k, t * P:t * P + w], wv[:, k, :],
                                  start=(k == 0), stop=(k == KD - 1))
                else:
                    for f in range(2):
                        if f == 1:
                            hook(j)
                        for k in range(KD):
                            last = mm(bank[2 * (j % 2) + f][:, 0:HALF], wv[:, k, t * P:(t + 1) * P],
                                      hT3[:, k, f * HALF:(f + 1) * HALF], start=(k == 0), stop=(k == KD - 1))
                last.then_inc(m_done, 1)
            for g in range(4):
                pe.wait_ge(pl_d, g + 1)
                if g < 2:
                    pe.wait_ge(m_free, njobs)
                else:
                    pe.wait_ge(pl_y2, g - 1)
                for f in range(2):
                    last = mm(bank[2 * (g % 2) + f][:, 0:HALF], wpool[:, g * P:(g + 1) * P],
                              (sq if g % 2 == 0 else rs)[:, f * HALF:(f + 1) * HALF], start=True, stop=True)
                last.then_inc(pl_y, 1)
            pe.wait_ge(a_free, aux)
            for g in range(4):
                tr(bank[6][0:16, g * P:(g + 1) * P], bT3[:, g, T:T + 16], ident)
                last = tr(bank[7][0:TS, g * P:(g + 1) * P], wk[:, g * TS:(g + 1) * TS], ident)
            last.then_inc(pl_t, 1)
            for u in range(2):
                mm(bank[4][:, 24 * u:24 * u + 24], expd[:, u * P:(u + 1) * P], gateS0[:, :], start=True, stop=True)
            mm(bank[5][:, 0:4], expd[:, 2 * P:3 * P], iwS[:, :], start=True, stop=True).then_inc(pl_t, 1)
            end_phase()

            after(pe, 1)
            def turn_hidden(kv):
                pe.wait_ge(cr_ev, kv + 1)
                for hb in range(2):
                    tr(bank[2 + kv][:, 64 * hb:64 * hb + NXP], hidr[kv][0:NXP, hb * P:(hb + 1) * P], con[0:NXP, 0:NXP]).then_inc(cp_ps, 1)

            for kv in range(2):
                pe.wait_ge(cr_x, kv + 1)
                for s in range(32):
                    if s % 16 == 0:
                        pe.wait_ge(w1p_in[2 * kv + s // 16], 16)
                    last = mm(bank[kv][0:NXP, 0:256], xpe[:, (32 * kv + s) * NXP:(32 * kv + s + 1) * NXP], w1P[kv][:, s * 256:(s + 1) * 256],
                              start=(s == 0), stop=(s == 31))
                last.then_inc(cr_ps, 1)
            turn_hidden(0)
            turn_hidden(1)
            pe.wait_ge(w1_in, 32)
            pe.wait_ge(cp_ev, 4)
            for hb in range(2):
                last = mm(bank[4][:, 0:62], w2P[:, hb * P:(hb + 1) * P], hidP[:, hb * 64:hb * 64 + 62], start=(hb == 0), stop=(hb == 1))
            last.then_inc(cp_ps, 1)
            for h in range(KVH):
                for hb in range(2):
                    last = mm(bank[5][0:NCP, h * P:(h + 1) * P], hidP[:, (2 + hb) * 64 + NCP * h:(2 + hb) * 64 + NCP * h + NCP],
                              w2P[:, 256 + hb * P:256 + (hb + 1) * P], start=(hb == 0), stop=(hb == 1))
            last.then_inc(cp_ps, 1)
            pe.wait_ge(cp_ev, 5)
            mm(bank[6][:, 0:62], ones, cxP[:, 64:126], start=True, stop=True).then_inc(cp_ps, 1)
            end_phase()

            after(pe, 2)

            def qk(u):
                grp, i, h = units[u]
                nk = P * (i + 1)
                if u >= 1:
                    pe.wait_ge(q_s, u)
                if grp == "A":
                    q = aqT3[:, h, i * P:(i + 1) * P]
                    k = h // G
                    mm(bank[2][:, 0:8 * i + 7], q, kcP[:, 32 * k:32 * k + 8 * i + 7], start=True, stop=True)
                    mm(bank[0][:, 0:nk], q, kslcT[:, k * T:k * T + nk], start=True, stop=True)
                    mm(bank[1][:, 0:nk], q, kwinT[:, k * T:k * T + nk], start=True, stop=True).then_inc(q_ps, 1)
                else:
                    mm(bank[0][:, 0:nk], cqT3[:, h, i * P:(i + 1) * P], ckT[:, 0:nk], start=True, stop=True).then_inc(q_ps, 1)

            def turn_p(u):
                grp, i, h = units[u]
                pe.wait_ge(q_p, u + 1)
                if u >= 1:
                    pe.wait_ge(q_ta, u)
                    pe.wait_ge(q_td, min(u, NUA))
                s = SP_[u % 3]
                if grp == "A":
                    for x in range(i + 1):
                        tr(bank[4][:, x * P:(x + 1) * P], s[:, 512 + x * P:512 + (x + 1) * P], ident)
                    tr(bank[5][0:8 * i + 7, 0:P], s[:, 1024:1024 + 8 * i + 7], ident)
                for x in range(i + 1):
                    last = tr(bank[3][:, x * P:(x + 1) * P], s[:, x * P:(x + 1) * P], ident)
                last.then_inc(q_t, 1)

            def pv(u):
                grp, i, h = units[u]
                pe.wait_ge(q_ta, u + 1)
                pe.wait_ge(q_td, min(u + 1, NUA))
                if u >= 2:
                    pe.wait_ge(q_m, u - 1)
                o = bank[6 + u % 2][:, 0:P]
                s = PTP[u % 2]
                if grp == "A":
                    k = h // G
                    nc_ = 8 * i + 7
                    mm(o, vcP[0:nc_, k * P:(k + 1) * P], s[0:nc_, 1024:1024 + P], start=True, stop=False)
                    for x in range(i + 1):
                        mm(o, vnat3[:, x, CW + k * P:CW + (k + 1) * P], s[:, 512 + x * P:512 + (x + 1) * P], start=False, stop=False)
                    for x in range(i + 1):
                        last = mm(o, vnat3[:, x, k * P:(k + 1) * P], s[:, x * P:(x + 1) * P], start=False, stop=(x == i))
                else:
                    for x in range(i + 1):
                        last = mm(o, cvnat[:, x * P:(x + 1) * P], s[:, x * P:(x + 1) * P], start=(x == 0), stop=(x == i))
                last.then_inc(q_o, 1)

            for n in range(len(units) + 3):
                if n < len(units):
                    qk(n)
                if 0 <= n - 2 < len(units):
                    turn_p(n - 2)
                if 0 <= n - 3 < len(units):
                    pv(n - 3)
            end_phase()

            after(pe, 3)

            def kturn(g, rows_out):
                if g >= 2:
                    pe.wait_ge(kb_d if g % 2 else kb_a, (g - 2) // 2 + 1)

            def evacuated(g):
                pe.wait_ge(kb_d if g % 2 else kb_a, g // 2 + 1)

            def ix_mm(n):
                b, q = n // 4, n % 4
                evacuated(n)
                mm(bank[q][32 * (b // 2):32 * (b // 2) + 32, :], zi[:, b * 32:(b + 1) * 32], ixT[n % 4][:, :],
                   start=(b % 2 == 0), stop=(b % 2 == 1), tile_position=(0, 32 * (b // 2))).then_inc(kb_mm, 1)

            for n in range(32):
                pe.wait_ge(kb_in[n % NIX], kneed[n])
                kturn(n, ID)
                for i in range(4):
                    last = tr(bank[5 + n % 2][0:ID, i * P:(i + 1) * P], ixn[n % NIX][:, i * ID:(i + 1) * ID], ident)
                last.then_inc(kb_tr, 1)
                if n >= 1:
                    ix_mm(n - 1)
            ix_mm(31)
            mm(bank[4][:, 0:TS], qfi[:, :], kiN[0:ID, :], start=True, stop=True).then_inc(si_ps, 1)
            for f in range(5):
                pe.wait_ge(si_ev, f + 1)
                w = 512 if f < 4 else TS
                mm(bank[f][:, 0:w], wsel[:, :], ixr[:, 512 * f:512 * f + w], start=True, stop=True).then_inc(si_ps, 1)
            end_phase()

            after(pe, 4)

            def row_turn(x):
                n, q, h = x // 8, x % 8 // 2, x % 2
                m = 4 * n + q
                pe.wait_ge(xn_in[m % 4], 64 * (m // 4 + 1))
                if x >= 2:
                    pe.wait_ge(xt_d, x - 1)
                for i in range(4):
                    last = tr(bank[4 + x % 2][:, i * P:(i + 1) * P], xnat[m % 4][:, i * 256 + h * P:i * 256 + (h + 1) * P], ident)
                last.then_inc(xn_tr, 1)

            def w2_mm(n):
                kv = n // 8
                pe.wait_ge(hd_ev, 2 * (n + 1))
                if n == 0:
                    pe.wait_ge(w1s_in, 32)
                if n >= 1:
                    pe.wait_ge(kc_ok, n)
                if kv == 0:
                    for hb in range(2):
                        last = mm(bank[6][:, 0:256], w2S[:, hb * P:(hb + 1) * P], hid[0][:, hb * 256:hb * 256 + 256], start=(hb == 0), stop=(hb == 1))
                else:
                    for h in range(KVH):
                        for hb in range(2):
                            last = mm(bank[6][0:NCS, h * P:(h + 1) * P], hid[0][:, hb * 256 + P * h:hb * 256 + P * h + NCS],
                                      w2S[:, 256 + hb * P:256 + (hb + 1) * P], start=(hb == 0), stop=(hb == 1))
                last.then_inc(kc_ps, 1)

            for n in range(18):
                for i in range(8):
                    g = n - 1
                    if 0 <= g < 16:
                        kv = g // 8
                        if i == 0:
                            pe.wait_ge(xt_d, 8 * (g + 1))
                            if g >= 2:
                                pe.wait_ge(hd_ev, 2 * (g - 1))
                        if g % 8 == 0 and i % 2 == 0:
                            pe.wait_ge(w1l_d, 4 * kv + i // 2 + 1)
                        for s in range(4 * i, 4 * i + 4):
                            first = xth[g % 2][:, s % 16 * P + s // 16:s % 16 * P + s // 16 + 1]
                            xh, xl = (bass.AP(t[g % 2][:, :].tensor, first.offset, [first.ap[0], [PAST, 2], [1, P]]) for t in (xth, xtl))
                            for hb in range(2):
                                cols = slice(s * 256 + hb * P, s * 256 + (hb + 1) * P)
                                o = bank[2 * (g % 2) + hb][:, 0:256]
                                mm(o, w1hi[:, cols], xl, start=(s == 0), stop=False)
                                mm(o, w1lo[:, cols], xh, start=False, stop=False)
                                last = mm(o, w1hi[:, cols], xh, start=False, stop=(s == 31))
                        if g == DB - 1 and i % 2 == 1 and i < 7:
                            last.then_inc(w1_used, 1)
                        if i == 7:
                            last.then_inc(hd_ps, 1)
                    if n < 16:
                        row_turn(8 * n + i)
                    if 0 <= n - 2 < 16 and i == 3:
                        w2_mm(n - 2)
                    if 0 <= n - 2 < 8 and i == 6:
                        pe.wait_ge(kc_x, n - 1)
                        mm(bank[7][:, 0:256], ones, cx[:, 256:512], start=True, stop=True).then_inc(kc_sum, 1)
            end_phase()

            after(pe, 5)
            gt = 32

            def kb(n):
                nonlocal gt
                u, kind, b, q, k, m = sblocks[n]
                pe.wait_ge(kk_in[m % NKR], kkneed[m])
                kturn(gt, HD)
                w = 256 if u < 2 else P
                for i in range(4):
                    last = tr(bank[5 + gt % 2][:, i * P:(i + 1) * P], kn[m % NKR][:, i * w + k * P:i * w + (k + 1) * P], ident)
                last.then_inc(kb_tr, 1)
                gt += 1

            def kmm(n):
                u, kind, b, q, k, m = sblocks[n]
                evacuated(kb_gt[n])
                if u < 2:
                    r = 32 * (b % 4)
                    lhs, st_, sp_ = zq[:, u * 256 + k * P + r:u * 256 + k * P + r + 32], k == 0, k == 1
                else:
                    r = 32 * (b // 2)
                    lhs, st_, sp_ = zq[:, 512 + 32 * b:512 + 32 * b + 32], b % 2 == 0, b % 2 == 1
                mm(bank[q][r:r + 32, :], lhs, kT[n % 4][:, :], start=st_, stop=sp_, tile_position=(0, r)).then_inc(kb_mm, 1)

            def pv(u, x):
                if x == 0 and u >= 1:
                    pe.wait_ge(un_x, u)
                if x == 0 and u < 2:
                    pe.wait_ge(wv_in, 64 * (u + 1))
                cs = slice(16 * x, 16 * x + 16)
                o = bank[7][:, cs]

                def p_of(tile, rows):
                    return pT[0:rows, tile * P + cs.start:tile * P + cs.stop]
                if u < 2:
                    b, k = x // 2, x % 2
                    mm(o, vN[:, k * P:(k + 1) * P], p_of(16, TS), start=True, stop=False)
                    mm(o, vN[:, CW + k * P:CW + (k + 1) * P], p_of(21, TS), start=False, stop=False)
                    c0 = ((4 * u + b) * KVH + k) * P
                    mm(o, vc[0:NCS, c0:c0 + P], p_of(22, NCS), start=False, stop=False)
                    for i in range(4):
                        mm(o, win_v[:, b * 1024 + i * 256 + k * P:b * 1024 + i * 256 + (k + 1) * P], p_of(17 + i, P), start=False, stop=False)
                    for i in range(NPG):
                        m = 8 * u + 2 * b + i // 8
                        if k == 0 and i % 8 == 0:
                            pe.wait_ge(*vneed[m])
                        last = mm(o, vr[m % NVR][:, i % 8 * 256 + k * P:i % 8 * 256 + (k + 1) * P], p_of(i, P), start=False, stop=(i == NPG - 1))
                        if k == 1 and i % 8 == 7:
                            last.then_inc(pv_b, 1)
                else:
                    m = 16 + x
                    pe.wait_ge(*vneed[m])
                    mm(o, cvN[:, :], p_of(16, TS), start=True, stop=False)
                    for i in range(NPG):
                        last = mm(o, vr[m % NVR][:, i * P:(i + 1) * P], p_of(i, P), start=False, stop=(i == NPG - 1))
                    last.then_inc(pv_b, 1)

            for step, u in STEPS:
                if step == "head" and u >= 1:
                    pe.wait_ge(un_s, u)
                if step == "body" and u < 2:
                    pe.wait_ge(un_w, u + 1)
                if step == "turn":
                    pe.wait_ge(un_p, u + 1)
                    for src in pgroups(u):
                        kturn(gt, HD)
                        for i, (t, rows) in enumerate(src):
                            last = tr(bank[5 + gt % 2][0:rows, i * P:(i + 1) * P], t, ident)
                        last.then_inc(kb_tr, 1)
                        gt += 1
                    evacuated(gt - 1)
                    evacuated(gt - 2)
                    if u == 2:
                        for x in range(8):
                            pv(u, x)
                    continue
                ns = blocks_of(step, u)
                every = len(ns) // 6
                for n in ns:
                    kb(n)
                    if n > ns[0]:
                        kmm(n - 1)
                    y = n - ns[0] + 1
                    if step == "body" and u < 2 and y == 13:
                        pe.wait_ge(im_in, u + 1)
                        mm(bank[4][:, 192:192 + NCS], con[:, K_GRP:K_GRP + P], sC[:, 0:NCS], start=True, stop=True).then_inc(im_ps, 1)
                    if step == "body" and u >= 1 and y % every == 0 and y // every <= 6:
                        pv(u - 1, y // every - 1)
                kmm(ns[-1])
                if u < 2:
                    col, kind = (32, 2) if step == "head" else (0, 0)
                    if step == "body":
                        pe.wait_ge(im_rd, u + 1)
                    for k in range(KVH):
                        last = mm(bank[4][:, col:col + TS], zq[:, u * 256 + k * P:u * 256 + (k + 1) * P], ksN[:, (kind + k) * TS:(kind + k + 1) * TS],
                                  start=(k == 0), stop=(k == 1))
                    if step == "head":
                        for b in range(4):
                            for k in range(KVH):
                                c0 = ((4 * u + b) * KVH + k) * P
                                last = mm(bank[4][32 * b:32 * b + 32, 64:64 + NCS], zq[:, u * 256 + k * P + 32 * b:u * 256 + k * P + 32 * b + 32],
                                          kc[:, c0:c0 + NCS], start=(k == 0), stop=(k == 1), tile_position=(0, 32 * b))
                    last.then_inc(un_ps, 1)
                elif step == "body":
                    mm(bank[4][:, 0:TS], qf[:, :], ksN[:, 4 * TS:5 * TS], start=True, stop=True).then_inc(un_ps, 1)
                if step == "body" and u >= 1:
                    pv(u - 1, 6)
                    pv(u - 1, 7)
            end_phase()

            after(pe, 6)

            def y_turn(nb):
                pe.wait_ge(y_ev, nb + 1)
                if nb >= 2:
                    pe.wait_ge(y_fin, 2 * (nb - 1))
                s = yT[nb % 4]
                for i in range(QT):
                    tr(bank[4 + nb % 2][:, i * P:(i + 1) * P], s[:, i * P:(i + 1) * P], ident)
                tr(bank[6 + nb % 2][0:TS, 0:P], s[:, T:TT], ident).then_inc(y_tr, 1)

            mh = v3(mix_hi, "p (k t) -> p k t", t=TT)
            ml = v3(mix_lo, "p (k t) -> p k t", t=TT)
            for nb in range(KD):
                pe.wait_ge(ol_d, out_split.index(("w", nb)) + 1)
                if nb >= 2:
                    pe.wait_ge(y_ev, nb - 1)
                _, wh, wl = out_views("w", nb)
                for f in range(2):
                    o, cols = bank[2 * (nb % 2) + f][:, 0:HALF], slice(f * HALF, (f + 1) * HALF)
                    for k in range(KD):
                        if nb == 0 and f == 0:
                            pe.wait_ge(ol_d, out_split.index(("mix", k)) + 1)
                        mm(o, wh[:, k, :], ml[:, k, cols], start=(k == 0), stop=False)
                        mm(o, wl[:, k, :], mh[:, k, cols], start=False, stop=False)
                        last = mm(o, wh[:, k, :], mh[:, k, cols], start=False, stop=(k == KD - 1))
                    if f == 0 and nb >= 1:
                        y_turn(nb - 1)
                last.then_inc(y_ps, 1)
            y_turn(KD - 1)

        @block.scalar
        def _(act):
            A = nc.scalar.activation
            mine = Count(act, act_)
            eps = con[:, K_EPS:K_EPS + 1]

            def end_phase():
                act.drain().then_inc(ph_act, 1)

            act.wait_ge(su_ev, 1)
            A(cT[:, 144:288], bank[7][:, 256:400], ACT.Exp, scale=-1.0).then_inc(c_e, 1)

            def square_x(t):
                w = width(t)
                act.wait_ge(s_x[t % 2], 16 * (t // 2 + 1))
                mine.link(A(mix[0:w, 0:D], xrow[t % 2][0:w, :], ACT.Square, accum_out=st[0:w, t:t + 1]))
                A(st[0:w, 8 + t:9 + t], st[0:w, t:t + 1], ACT.Sqrt, scale=1.0 / D, bias=con[0:w, K_EPS:K_EPS + 1]).then_inc(x_std, 1)

            square_x(0)
            for n in range(NADA):
                act.wait_ge(w_free, n + 1)
                if n >= 2:
                    act.wait_ge(ada_ps, n - 1)
                act.copy(mpart[n % 2][:, :], bank[4 + 2 * (n % 2)][:, 0:CW]).then_inc(ada_c, 1)
                if n % 3 == 2 and n // 3 <= QT:
                    t = n // 3
                    if t == 0:
                        for i in range(5):
                            w = min(512, XL - 512 * i)
                            act.wait_ge(b_ps, i + 1)
                            A(btmp[:, 512 * i:512 * i + w], bank[BIAS_BANKS[i]][0:12, 0:w], ACT.Copy).then_inc(b_ev, 1)
                    if t < QT:
                        square_x(t + 1)
                    evac_x(act, A, t)
            act.wait_ge(pst_t, 1)
            for g in range(4):
                last = act.copy(bS4[:, g, :, 0:15], bank[6][:, g * 120:(g + 1) * 120].rearrange("p (b t) -> p b t", t=15))
            last.then_inc(pst_ev, 1)

            aux = 0
            nr = 0

            def hook(j):
                nonlocal aux
                if j >= 1:
                    i = j - 1
                    kind, b, t, c = jobs[i]
                    if i in turned_set:
                        w = width(t)
                        for x in range(turns(i)):
                            act.wait_ge(a_done, aux + 1)
                            act.copy(turned_to(kind, t, x), bank[6 + aux % 2][:, 0:w]).then_inc(a_free, 1)
                            aux += 1
                    if kind in ("cq", "aq"):
                        n = normT.index(i)
                        act.wait_ge(n_sum, n + 1)
                        if n >= 1:
                            act.wait_ge(m_free, normT[n - 1] + 1)
                        for f in range(2):
                            last = A(rs[:, f * HALF:(f + 1) * HALF], bank[4 + f][:, 0:HALF], ACT.Sqrt, scale=1.0 / HD, bias=eps)
                        last.then_inc(n_std, 1)
                if j in ix_slot and ix_slot[j][0] == "dots":
                    _, i, h, n = ix_slot[j]
                    act.wait_ge(ixp_d, n + 1)
                    if n >= 1:
                        act.wait_ge(ixp_a, n)
                    A(rs[:, 0:P * (i + 1)], bank[4 + n % 2][:, 0:P * (i + 1)], ACT.Relu).then_inc(ixp_r, 1)

            def round_half(x):
                if x is not None:
                    act.wait_ge(hw_in[x % 4], 16 * (x // 4 + 1))
                    act.copy(hw_hi[x % 4][:, :], hw_raw[x % 4][:, :]).then_inc(hs_a, 1)

            for j, (kind, b, t, c) in enumerate(jobs):
                if j >= 1:
                    round_half(half_ahead(j + 1, 0))
                hook(j)
                round_half(half_ahead(j + 1, 1))
                if j == J0 - 1:
                    for k in range(KD):
                        act.copy(v3(h_hi, "p (k t) -> p k t", t=TT)[:, k, :], hT3[:, k, :]).then_inc(hh_a, 1)
                if j in rownorm:
                    w = width(t)
                    act.wait_ge(m_done, j + 1)
                    nh = 1 if kind == "ckv" else 2
                    o = 24 + 4 * (nr % 2)
                    if nr >= 2:
                        act.wait_ge(m_free, rownorm[nr - 2] + 1)
                    for h in range(nh):
                        mine(A(sq[0:w, 0:P], bank[2 * (j % 2)][0:w, h * P:(h + 1) * P], ACT.Square, accum_out=st[0:w, o + h:o + h + 1]))
                        mine.wait()
                    A(st[0:w, o + 2:o + 2 + nh], st[0:w, o:o + nh], ACT.Sqrt, scale=1.0 / HD, bias=con[0:w, K_EPS:K_EPS + 1]).then_inc(r_std, 1)
                    nr += 1
                elif kind in ("cq", "aq"):
                    n = normT.index(j)
                    act.wait_ge(m_done, j + 1)
                    if n >= 1:
                        act.wait_ge(n_sum, n)
                    for f in range(2):
                        last = A(sq[:, f * HALF:(f + 1) * HALF], bank[2 * (j % 2) + f][:, 0:HALF], ACT.Square)
                    last.then_inc(n_sq, 1)
                elif kind in SIL_AT:
                    n = silj.index(j)
                    act.wait_ge(m_done, j + 1)
                    if n >= 2:
                        act.wait_ge(sx_out[n % 2], 16 * (n // 2))
                    elif n == 0:
                        act.wait_ge(n_sum, len(normT))
                        act.wait_ge(m_free, normT[-1] + 1)
                    for f in range(2):
                        last = A((sq, rs)[n % 2][:, f * HALF:(f + 1) * HALF], bank[2 * (j % 2) + f][:, 0:HALF], ACT.Exp, scale=-1.0)
                    last.then_inc(sil_e, 1)
            hook(njobs)
            A(gateP[:, :], gateP[:, :], ACT.Exp, scale=-1.0).then_inc(g_e, 1)
            act.wait_ge(gs_in, 1)
            A(gateS[:, :], gateS[:, :], ACT.Exp, scale=-1.0).then_inc(g_e, 1)
            end_phase()

            after(act, 1)
            for kv in range(2):
                act.wait_ge(cr_ps, kv + 1)
                act.copy(hidr[kv][0:NXP, :], bank[kv][0:NXP, 0:256]).then_inc(cr_ev, 1)
            for n in range(4):
                bk, c0 = bank[2 + n // 2], 64 * (n % 2)
                act.wait_ge(cp_ps, 2 * (n // 2) + 2)
                b1 = vecT[:, V_B1 + n:V_B1 + n + 1]
                A(b1e[:, n:n + 1], bk[:, c0 + NXP - 1:c0 + NXP], ACT.Identity, bias=b1)
                A(hidP[:, n * 64:n * 64 + 62], bk[:, c0:c0 + 62], ACT.Gelu_apprx_tanh, bias=b1).then_inc(cp_ev, 1)
            act.wait_ge(cp_ps, 5)
            mine(A(cxP[:, 0:62], bank[4][:, 0:62], ACT.Identity, bias=vecT[:, V_B2:V_B2 + 1]))
            A(cxP[:, 64:126], bank[4][:, 0:62], ACT.Square, bias=vecT[:, V_B2:V_B2 + 1]).then_inc(cp_ev, 1)
            act.wait_ge(cp_ps, 7)
            A(cxP[:, 128:190], bank[6][:, 0:62], ACT.Sqrt, scale=1.0 / HD, bias=eps).then_inc(cp_ev, 1)
            end_phase()

            after(act, 2)

            def exps(u):
                grp, i, h = units[u]
                nk = P * (i + 1)
                s, a = SP_[u % 3], 16 * (u % 4)
                act.wait_ge(q_s, u + 1)
                parts = ((1024, 8 * i + 7, 0), (0, nk, 1), (512, nk, 2)) if grp == "A" else ((0, nk, 1),)
                for off, n, r in parts:
                    last = A(s[:, off:off + n], s[:, off:off + n], ACT.Exp, bias=as_[:, a + 3 + r:a + 4 + r], accum_out=as_[:, a + 6 + r:a + 7 + r])
                last.then_inc(q_e, 1)

            def take_slc(u):
                grp, i, h = units[u]
                act.wait_ge(q_t, u + 1)
                if u >= 2:
                    act.wait_ge(q_o, u - 1)
                act.copy(PTP[u % 2][:, 0:P * (i + 1)], bank[3][:, 0:P * (i + 1)]).then_inc(q_ta, 1)

            for n in range(len(units) + 2):
                if n < len(units):
                    exps(n)
                if 0 <= n - 2 < len(units):
                    take_slc(n - 2)
            end_phase()

            after(act, 3)
            act.wait_ge(w1a_in, 16)
            for i in range(4):
                act.copy(quarter(w1hi, i), quarter(w1S, i)).then_inc(w1h_a, 1)
            for n in range(0, 32, 2):
                act.wait_ge(kb_tr, n + 1)
                if n >= 4:
                    act.wait_ge(kb_mm, n - 3)
                act.copy(ixT[n % 4][:, :], bank[5][0:ID, :]).then_inc(kb_a, 1)
            act.wait_ge(kb_mm, 32)
            act.wait_ge(si_ps, 1)
            for f in range(5):
                w = 512 if f < 4 else TS
                A(ixr[:, 512 * f:512 * f + w], bank[f][:, 0:w], ACT.Relu).then_inc(si_ev, 1)
            end_phase()

            after(act, 4)

            def hidden(g):
                act.wait_ge(hd_ps, g + 1)
                if g >= 1:
                    act.wait_ge(kc_ps, g)
                for hb in range(2):
                    A(hid[0][:, hb * 256:hb * 256 + 256], bank[2 * (g % 2) + hb][:, 0:256], ACT.Gelu_apprx_tanh,
                      bias=b1e[:, 2 * (g // 8) + hb:2 * (g // 8) + hb + 1]).then_inc(hd_ev, 1)

            for n in range(18):
                if 0 <= n - 2 < 16:
                    hidden(n - 2)
                for i in range(8):
                    if n == DB + 1:
                        for q in SPLIT_AT.get(i, ()):
                            act.wait_ge(w1q_in[q], 16)
                            act.copy(quarter(w1hi, q), quarter(w1S, q)).then_inc(w1h_a, 1)
                    if n < 16:
                        act.wait_ge(xn_tr, 8 * n + i + 1)
                        if n == 1 and i == 0:
                            act.wait_ge(mx_io, 16)
                        if n >= 2 and i == 0:
                            act.wait_ge(hd_ps, n - 1)
                        hi, _, src = turned_rows(8 * n + i)
                        act.copy(hi, src).then_inc(xt_a, 1)
                    if 0 <= n - 2 < 8 and i == 4:
                        g = n - 2
                        act.wait_ge(kc_ps, g + 1)
                        if g >= 1:
                            act.wait_ge(kc_ok, g)
                        mine(A(cx[:, 0:256], bank[6][:, 0:256], ACT.Identity, bias=vecT[:, V_B2:V_B2 + 1]))
                        A(cx[:, 256:512], bank[6][:, 0:256], ACT.Square, bias=vecT[:, V_B2:V_B2 + 1]).then_inc(kc_x, 1)
                if 0 <= n - 2 < 8:
                    act.wait_ge(kc_sum, n - 1)
                    A(cx[:, 256:512], bank[7][:, 0:256], ACT.Sqrt, scale=1.0 / HD, bias=eps).then_inc(kc_std, 1)
            end_phase()

            after(act, 5)
            gt = 32
            for step, u in STEPS:
                if step == "turn":
                    for gi, src in enumerate(pgroups(u)):
                        if gt % 2 == 0:
                            act.wait_ge(kb_tr, gt + 1)
                            take_p(act, act.copy, u, gi, src, kb_a)
                        gt += 1
                    continue
                if step == "body" and u < 2:
                    unit_exps(act, A, u, "early")
                for n in blocks_of(step, u):
                    if gt % 2 == 0:
                        take_k(act, act.copy, n, gt, kb_a)
                    gt += 1
                if step == "body":
                    unit_exps(act, A, u, "late")
            end_phase()

            after(act, 6)
            for kind, n in out_split:
                if kind == "w":
                    c = n // 2
                    act.wait_ge(wo_in[c % 3], 16 * (c // 3 + 1))
                    if c >= 2:
                        act.wait_ge(y_ps, 2 * (c - 1))
                whole, hi, _ = out_views(kind, n)
                act.copy(hi, whole).then_inc(oh_a, 1)

        @block.vector
        def _(v):
            V = nc.vector
            mine = Count(v, dve)
            link = mine.link

            def end_phase():
                v.drain().then_inc(ph_dve, 1)

            def ttr(out, a, b, acc):
                return V.tensor_tensor_reduce(out=out, in0=a, in1=b, scale=1.0, scalar=FLOOR, op0=ALU.add, op1=ALU.max, accum_out=acc)

            v.wait_ge(su_tr, 1)
            link(V.tensor_copy(vecT[:, :], bank[7][:, 0:NV]))
            V.tensor_copy(peT[:, :], bank[7][:, 128:192]).then_inc(su_ev, 1)
            v.wait_ge(c_e, 1)
            link(V.tensor_scalar(cT[:, 144:288], cT[:, 144:288], 1.0, None, ALU.add))
            link(V.reciprocal(cT[:, 144:288], cT[:, 144:288]))
            link(V.memset(cpad[:, :], 0.0))
            V.tensor_tensor(v3(cpad, "p (k b) -> p k b", b=32)[:, :, 0:9], bank[7][:, 256:400].rearrange("p (k b) -> p k b", b=9),
                            cT[:, 144:288].rearrange("p (k b) -> p k b", b=9), ALU.mult).then_inc(c_s, 1)
            link(V.tensor_scalar(vecT[:, V_AQ:V_CQ + 1], vecT[:, V_AQ:V_CQ + 1], SCALE, None, ALU.mult))
            for t in range(QT + 1):
                w = width(t)
                v.wait_ge(x_std, t + 1)
                link(V.reciprocal(st[0:w, 16 + t:17 + t], st[0:w, 8 + t:9 + t]))
                V.tensor_scalar(xrow[t % 2][0:w, :], xrow[t % 2][0:w, :], st[0:w, 16 + t:17 + t], None, ALU.mult).then_inc(x_n, 1)
            link(V.memset(zq[:, :], 0.0))
            link(V.memset(zi[:, :], 0.0))
            link(V.memset(bT[:, :], 0.0))
            v.wait_ge(ada_ps, 16)
            link(V.tensor_tensor(mod3[:, 0:32], bank[5][:, 0:288].rearrange("p (n b) -> p n b", b=9), bc(vecT[:, 0:32], 9), ALU.add))
            V.tensor_scalar(ascale[:, :], modT[:, 144:288], 1.0, None, ALU.add).then_inc(h_copied, 1)
            v.wait_ge(h_copied, 1)
            link(V.tensor_tensor(asc3, asc3, bc(vecT[:, V_G:V_G + 16], 9), ALU.mult))
            v.wait_ge(x_ev, 20)
            for k in range(KD):
                V.tensor_scalar(hT3[:, k, 0:T], hT3[:, k, 0:T], asc3[:, k, 0:1], mod3[:, k, 0:1], ALU.mult, ALU.add).then_inc(h_ready, 1)
            for k in range(KD):
                hs = hT3[:, k, T:TT].rearrange("p (b t) -> p b t", t=DT)
                link(V.tensor_tensor(hs, hs, bc(asc3[:, k, 1:9], DT), ALU.mult))
                V.tensor_tensor(hs, hs, bc(mod3[:, k, 1:9], DT), ALU.add).then_inc(h_ready, 1)
            v.wait_ge(ada_ps, NADA)
            V.tensor_tensor(mod3[:, 32:48], bank[7][:, 288:432].rearrange("p (n b) -> p n b", b=9), bc(vecT[:, 32:48], 9), ALU.add).then_inc(h_copied, 1)

            nr = 0

            def topk(w, out8, times):
                for _ in range(times):
                    link(V.max(out8, w))
                    link(V.match_replace(w, out8, w, MARK))

            def rest_half(x):
                if x is not None:
                    v.wait_ge(hs_a, x + 1)
                    V.tensor_tensor(hw_lo[x % 4][:, :], hw_raw[x % 4][:, :], hw_hi[x % 4][:, :].bitcast(F32), ALU.subtract).then_inc(hs_d, 1)

            for j, (kind, b, t, c) in enumerate(jobs):
                if j >= 1:
                    rest_half(half_ahead(j + 1, 1))
                bk = bank[2 * (j % 2)]
                if j in ix_slot:
                    s = ix_slot[j]
                    i = s[1]
                    nk = P * (i + 1)
                    if s[0] == "dots":
                        _, i, h, n = s
                        v.wait_ge(ixp_r, n + 1)
                        wi = iwP[:, 4 * i + h:4 * i + h + 1]
                        if h == 0:
                            link(V.tensor_scalar(wk[:, 0:nk], rs[:, 0:nk], wi, None, ALU.mult))
                            V.tensor_tensor(wk[:, P * i:nk], wk[:, P * i:nk], con[:, K_DIAG:K_DIAG + P], ALU.add).then_inc(ixp_a, 1)
                        else:
                            V.scalar_tensor_tensor(out=wk[:, 0:nk], in0=rs[:, 0:nk], scalar=wi, in1=wk[:, 0:nk], op0=ALU.mult, op1=ALU.add).then_inc(ixp_a, 1)
                        v.wait_ge(ixp_a, n + 1)
                    else:
                        topk(wk[:, 0:nk], st[:, 48:56], 4)
                        if s[2] == 3:
                            link(V.tensor_scalar(maskC[:, MOFF[i]:MOFF[i] + nk], wk[:, 0:nk], MARK, NEG, ALU.not_equal, ALU.mult))
                v.wait_ge(m_done, j + 1)
                if j == J0 - 1:
                    for k in range(KD):
                        v.wait_ge(hh_a, k + 1)
                        hk = [v3(t_, "p (k t) -> p k t", t=TT)[:, k, :] for t_ in (h_lo, hT, h_hi)]
                        V.tensor_tensor(hk[0], hk[1], hk[2].bitcast(F32), ALU.subtract).then_inc(hl_d, 1)
                rest_half(half_ahead(j + 2, 0))
                w = width(t)
                if j in staged_set:
                    n = staged.index(j)
                    if n >= 4:
                        v.wait_ge(st_out[n % 4], 16 * (n // 4))
                        i = staged[n - 4]
                        if i in turned_set:
                            v.wait_ge(a_done, sum(turns(x) for x in turned if x <= i))
                    s = stage[n % 4]
                if kind == "small":
                    V.tensor_copy(s[0:w, 0:ID], bk[0:w, 24:24 + ID])
                    V.tensor_copy(s[0:w, ID:2 * ID], bk[0:w, 24:24 + ID])
                    V.tensor_copy(gateP[:, 24 * t:24 * t + 24] if t < QT else gateS0[:, :], bk[0:w, 0:24])
                    V.tensor_copy(iwP[:, 4 * t:4 * t + 4] if t < QT else iwS[:, :], bk[0:w, 24 + ID:24 + ID + 4]).then_inc(m_free, 1)
                elif j in rownorm:
                    nh = 1 if kind == "ckv" else 2
                    o = 24 + 4 * (nr % 2)
                    nr += 1
                    v.wait_ge(r_std, nr)
                    link(V.reciprocal(st[0:w, o + 2:o + 2 + nh], st[0:w, o + 2:o + 2 + nh]))
                    gr = {"kslc": 0, "kwin": 1, "ckv": 2}[kind]
                    if kind == "ckv":
                        V.tensor_copy(s[0:w, P:2 * P], bk[0:w, P:2 * P])
                        V.tensor_copy(cvnat[:, t * P:(t + 1) * P] if t < QT else cvN[:, :], bk[0:w, P:2 * P])
                    for h in range(nh):
                        last = V.scalar_tensor_tensor(out=s[0:w, h * P:(h + 1) * P], in0=bk[0:w, h * P:(h + 1) * P], scalar=st[0:w, o + 2 + h:o + 3 + h],
                                                      in1=gk[0:w, gr * P:(gr + 1) * P], op0=ALU.mult, op1=ALU.mult)
                    last.then_inc(m_free, 1)
                elif kind in ("kcmp", "vcmp"):
                    V.tensor_copy(s[0:w, :], bk[0:w, 0:CW]).then_inc(m_free, 1)
                elif kind in ("vslc", "vwin"):
                    x = 0 if kind == "vslc" else CW
                    V.tensor_copy(vnat3[:, t, x:x + CW] if t < QT else vN[:, x:x + CW], bk[0:w, 0:CW]).then_inc(m_free, 1)
                else:
                    b2 = bank[2 * (j % 2) + 1]
                    if kind == "iq":
                        V.tensor_copy(iqT3[:, b, 0:HALF], bk[:, 0:HALF])
                        V.tensor_copy(iqT3[:, b, HALF:TT], b2[:, 0:HALF]).then_inc(m_free, 1)
                    elif kind in ("cq", "aq"):
                        n = normT.index(j)
                        v.wait_ge(n_std, n + 1)
                        link(V.reciprocal(rs[:, :], rs[:, :]))
                        dst = aqT3 if kind == "aq" else cqT3
                        col = vecT[:, V_AQ:V_AQ + 1] if kind == "aq" else vecT[:, V_CQ:V_CQ + 1]
                        parts = [(dst[:, b, 0:HALF], bk[:, 0:HALF], rs[:, 0:HALF]), (dst[:, b, HALF:T], b2[:, 0:T - HALF], rs[:, HALF:T])]
                        if kind == "cq":
                            parts.append((qf[:, b:P:4], b2[:, T - HALF:HALF], rs[:, T:TT]))
                        else:
                            k, g = b // G, b % G
                            z5 = v3(zq, "p (u k b x t g) -> p u k b x t g", u=3, k=2, b=4, x=2, t=DT)
                            for u in range(2):
                                a, e = T - HALF + 16 * u, T + 16 * u
                                parts.append((z5[:, u, k, :, k, :, g], b2[:, a:a + 16].rearrange("p (b t) -> p b t", t=DT), rs[:, e:e + 16].rearrange("p (b t) -> p b t", t=DT)))
                        for o, i, r in parts:
                            last = V.scalar_tensor_tensor(out=o, in0=i, scalar=col, in1=r, op0=ALU.mult, op1=ALU.mult)
                        last.then_inc(m_free, 1)
                    elif kind == "bin":
                        V.tensor_copy(bT3[:, b, 16:16 + HALF], bk[:, 0:HALF])
                        V.tensor_copy(bT3[:, b, 16 + HALF:16 + T], b2[:, 0:T - HALF])
                        V.tensor_copy(wk[:, b * TS:(b + 1) * TS], b2[:, T - HALF:HALF])
                        V.tensor_copy(bS4[:, b, :, 15:19], b2[:, T - HALF:HALF].rearrange("p (b t) -> p b t", t=DT)).then_inc(m_free, 1)
                    else:
                        n = silj.index(j)
                        e = (sq, rs)[n % 2]
                        v.wait_ge(sil_e, n + 1)
                        link(V.tensor_scalar(e[:, :], e[:, :], 1.0, None, ALU.add))
                        link(V.reciprocal(e[:, :], e[:, :]))
                        V.tensor_tensor(e[:, 0:HALF], bk[:, 0:HALF], e[:, 0:HALF], ALU.mult)
                        V.tensor_tensor(e[:, HALF:TT], b2[:, 0:HALF], e[:, HALF:TT], ALU.mult).then_inc(m_free, 1)
            v.wait_ge(m_free, njobs)
            v.wait_ge(iqh_in, 16)
            for h in range(IH):
                src = (iqT3[0:ID, h // 2, T:TT] if h % 2 == 0 else iqh[:, (h // 2) * TS:(h // 2 + 1) * TS]).rearrange("p (b t) -> p b t", t=DT)
                last = V.tensor_copy(qfi[:, :].rearrange("p (b h t) -> p b h t", h=IH, t=DT)[:, :, h, :], src)
            link(last)
            for par in range(2):
                V.tensor_copy(v3(zi, "p (c e r) -> p c e r", e=2, r=32)[:, :, par, 16 * par:16 * par + 16], v3(qfi, "p (c e r) -> p c e r", e=2, r=16)[:, :, par, :])
                V.tensor_copy(zq[:, 512:768].rearrange("p (c e r) -> p c e r", e=2, r=32)[:, :, par, 16 * par:16 * par + 16], v3(qf, "p (c e r) -> p c e r", e=2, r=16)[:, :, par, :])
            v.wait_ge(pst_ev, 1)
            for i in range(2):
                v.wait_ge(sx_out[i], 16 * KD // 2)
            for g in range(4):
                o = (sq, rs)[g % 2]
                if g >= 2:
                    v.wait_ge(pl_y, g - 1)
                win_w = 2 << g
                cur = bT3[:, g, :]
                lo = 16
                step = 1
                src_p, src_s = cur, bS4[:, g, :, :]
                pa, pb_ = pls[:, 0:528], pls[:, 528:1056]
                sa, sb_ = pls[:, 1056:1056 + 160], pls[:, 1216:1216 + 160]
                flip = 0
                while step < win_w:
                    dp = (pa, pb_)[flip]
                    ds_ = (sa, sb_)[flip].rearrange("p (b t) -> p b t", t=20)
                    link(V.tensor_tensor(dp[:, 2 * step - 1:528], src_p[:, 2 * step - 1:528], src_p[:, step - 1:528 - step], ALU.add))
                    link(V.tensor_tensor(ds_[:, :, 2 * step - 1:19], src_s[:, :, 2 * step - 1:19], src_s[:, :, step - 1:19 - step], ALU.add))
                    src_p, src_s = dp, ds_
                    flip ^= 1
                    step *= 2
                V.scalar_tensor_tensor(out=o[:, 0:T], in0=src_p[:, 16:528], scalar=1.0 / win_w, in1=cur[:, 16:528], op0=ALU.mult, op1=ALU.subtract)
                link(V.scalar_tensor_tensor(out=o[:, T:TT].rearrange("p (b t) -> p b t", t=DT), in0=src_s[:, :, 15:19], scalar=1.0 / win_w,
                                            in1=bS4[:, g, :, 15:19], op0=ALU.mult, op1=ALU.subtract))
                link(V.tensor_tensor(pls[:, 1376:1392], src_p[:, 16:32], con[:, K_RC + 16 * g:K_RC + 16 * g + 16], ALU.mult))
                V.tensor_tensor(o[:, 0:16], pls[:, 1376:1392], cur[:, 16:32], ALU.subtract).then_inc(pl_d, 1)
                if g >= 1:
                    pool_out(v, V, g - 1)
            pool_out(v, V, 3)
            v.wait_ge(pl_t, 1)
            v.wait_ge(pl_y, 4)
            V.tensor_copy(prw[0:16, 0:512], bank[6][0:16, :]).then_inc(pl_c, 1)
            V.tensor_copy(prw[0:TS, 512:1024], bank[7][0:TS, :]).then_inc(pl_c, 1)
            v.wait_ge(pl_t, 2)
            link(V.tensor_copy(gateS1[:, :], bank[4][:, 0:48]))
            for r in range(3):
                for k in range(2):
                    link(V.tensor_tensor_reduce(out=st[:, 32:40], in0=gateS1[:, 24 * k + 8 * r:24 * k + 8 * r + 8], in1=con[:, K_M3:K_M3 + 8], scale=1.0, scalar=0.0,
                                                op0=ALU.mult, op1=ALU.add, accum_out=gateS[:, 2 * r + k:2 * r + k + 1]))
            V.tensor_tensor_reduce(out=st[:, 60:64], in0=bank[5][:, 0:4], in1=con[:, K_M2:K_M2 + 4], scale=1.0, scalar=0.0,
                                   op0=ALU.mult, op1=ALU.add, accum_out=wiS[:, 0:1]).then_inc(gs_in, 1)
            v.wait_ge(gs_in, 1)
            link(V.tensor_scalar(wsel[:, :], con[:, K_WM:K_WM + P], wiS[:, 0:1], None, ALU.mult))
            v.wait_ge(g_e, 2)
            for gt_ in (gateP, gateS):
                link(V.tensor_scalar(gt_[:, :], gt_[:, :], 1.0, None, ALU.add))
                link(V.reciprocal(gt_[:, :], gt_[:, :]))
            end_phase()

            after(v, 1)
            chunks5 = cmpT[:, :].rearrange("p (v x c s) -> p v s x c", v=2, x=KVH, s=16)
            for kv in range(2):
                xp5 = xpe[:, 32 * kv * NXP:32 * (kv + 1) * NXP].rearrange("p (s n) -> p s n", n=NXP)
                for a in range(2):
                    at = peT[:, 32 * kv + 16 * a:32 * kv + 16 * a + 16]
                    for x in range(KVH):
                        V.tensor_tensor(xp5[:, 16 * a:16 * a + 16, NCP * x:NCP * (x + 1)], chunks5[:, kv, :, x, a:a + NCP], bc(at, NCP), ALU.add)
                V.tensor_copy(xp5[:, :, NXP - 1:NXP], peT[:, 32 * kv:32 * kv + 32].unsqueeze(2)).then_inc(cr_x, 1)
            v.wait_ge(cp_ps, 6)
            V.tensor_tensor(vcP[0:NCP, :].rearrange("p (h c) -> p h c", h=2), bank[5][0:NCP, 0:256].rearrange("p (h c) -> p h c", h=2),
                            gk[0:NCP, 3 * P:4 * P].unsqueeze(1).broadcast_to([NCP, 2, P]), ALU.add)
            v.wait_ge(cp_ev, 6)
            link(V.reciprocal(cxP[:, 128:190], cxP[:, 128:190]))
            for h in range(2):
                V.scalar_tensor_tensor(out=kcP[:, 32 * h:32 * h + NCP], in0=cxP[:, NCP * h:NCP * (h + 1)], scalar=vecT[:, V_AK:V_AK + 1],
                                       in1=cxP[:, 128 + NCP * h:128 + NCP * (h + 1)], op0=ALU.mult, op1=ALU.mult)
            end_phase()

            after(v, 2)
            v.wait_ge(at_in, 16)
            b3 = v3(bias, "p (h j) -> p h j", h=12)

            def scores(u):
                grp, i, h = units[u]
                nk = P * (i + 1)
                s, a = SP_[u % 3], 16 * (u % 4)
                off = 384 - P * i
                v.wait_ge(q_ps, u + 1)
                if u >= 3:
                    v.wait_ge(q_t, u - 2)
                if grp == "A":
                    n = 8 * i + 7
                    ttr(s[:, 1024:1024 + n], bank[2][:, 0:n], b3[:, h, off + 31:off + 31 + 16 * (n - 1) + 1:16], as_[:, a:a + 1])
                    ttr(s[:, 0:nk], bank[0][:, 0:nk], b3[:, h, off:off + nk], as_[:, a + 1:a + 2])
                    link(ttr(s[:, 512:512 + nk], bank[1][:, 0:nk], b3[:, h, off:off + nk], as_[:, a + 2:a + 3]))
                    V.tensor_scalar(as_[:, a + 3:a + 6], as_[:, a:a + 3], -1.0, None, ALU.mult).then_inc(q_s, 1)
                else:
                    if i == 0:
                        link(ttr(s[:, 0:nk], bank[0][:, 0:nk], b3[:, 8 + h, off:off + nk], as_[:, a + 1:a + 2]))
                    else:
                        link(V.tensor_tensor(s[:, 0:nk], bank[0][:, 0:nk], b3[:, 8 + h, off:off + nk], ALU.add))
                        link(ttr(s[:, 0:nk], s[:, 0:nk], maskC[:, MOFF[i]:MOFF[i] + nk], as_[:, a + 1:a + 2]))
                    V.tensor_scalar(as_[:, a + 4:a + 5], as_[:, a + 1:a + 2], -1.0, None, ALU.mult).then_inc(q_s, 1)

            def norm(u):
                grp, i, h = units[u]
                nk = P * (i + 1)
                s, a = SP_[u % 3], 16 * (u % 4)
                v.wait_ge(q_e, u + 1)
                r0, r1 = (0, 3) if grp == "A" else (1, 2)
                link(V.tensor_scalar(as_[:, a + 6 + r0:a + 6 + r1], as_[:, a + 6 + r0:a + 6 + r1], 1e-30, None, ALU.max))
                link(V.reciprocal(as_[:, a + 9 + r0:a + 9 + r1], as_[:, a + 6 + r0:a + 6 + r1]))
                if grp == "A":
                    link(V.tensor_tensor(as_[:, a + 9:a + 12], as_[:, a + 9:a + 12], gateP[:, 24 * i + h:24 * i + h + 17:8], ALU.mult))
                parts = ((1024, 8 * i + 7, 0), (512, nk, 2), (0, nk, 1)) if grp == "A" else ((0, nk, 1),)
                for off, n, r in parts:
                    last = V.tensor_scalar(s[:, off:off + n], s[:, off:off + n], as_[:, a + 9 + r:a + 10 + r], None, ALU.mult)
                last.then_inc(q_p, 1)

            def take_win(u):
                grp, i, h = units[u]
                if grp != "A":
                    return
                v.wait_ge(q_t, u + 1)
                if u >= 2:
                    v.wait_ge(q_o, u - 1)
                n = 8 * i + 7
                V.tensor_copy(PTP[u % 2][0:n, 1024:1024 + P], bank[5][0:n, 0:P])
                V.tensor_copy(PTP[u % 2][:, 512:512 + P * (i + 1)], bank[4][:, 0:P * (i + 1)]).then_inc(q_td, 1)

            def gated(u):
                grp, i, h = units[u]
                v.wait_ge(q_o, u + 1)
                m = mix3[:, h if grp == "A" else 12 + h, P * i:P * (i + 1)]
                V.tensor_tensor(m, bank[6 + u % 2][:, 0:P], m, ALU.mult).then_inc(q_m, 1)

            NU = len(units)
            for n in range(NU + 3):
                if n < NU:
                    scores(n)
                if 0 <= n - 1 < NU:
                    norm(n - 1)
                if 0 <= n - 2 < NU:
                    take_win(n - 2)
                if 0 <= n - 3 < NU:
                    gated(n - 3)
            end_phase()

            after(v, 3)

            def rest_of_weights(kv, i):
                v.wait_ge(w1h_a, 4 * kv + i + 1)
                V.tensor_tensor(quarter(w1lo, i), quarter(w1S, i), quarter(w1hi, i).bitcast(F32), ALU.subtract).then_inc(w1l_d, 1)

            for i in range(4):
                rest_of_weights(0, i)
            for n in range(1, 32, 2):
                v.wait_ge(kb_tr, n + 1)
                if n >= 4:
                    v.wait_ge(kb_mm, n - 3)
                V.tensor_copy(ixT[n % 4][:, :], bank[6][0:ID, :]).then_inc(kb_d, 1)
            for f in range(5):
                v.wait_ge(si_ps, f + 2)
                if f < 4:
                    link(V.tensor_copy(wrk[:, 512 * f:512 * f + 512], bank[f][:, :]))
                else:
                    link(V.tensor_tensor(wrk[:, PAST:LS], bank[4][:, 0:TS], con[:, K_BM + 2 * TS:K_BM + 3 * TS], ALU.add))
            end_phase()

            after(v, 4)
            V.tensor_scalar(xth[0][:, 2 * PAST:XTW], ident[:, 0:8], 0.0, None, ALU.mult)
            V.tensor_scalar(xtl[0][:, 2 * PAST:XTW], ident[:, 0:8], 0.0, None, ALU.mult)
            for n in range(18):
                if n == 1:
                    v.wait_ge(mx_io, 16)
                    V.tensor_scalar(xth[1][:, 2 * PAST:XTW], ident[:, 0:8], 0.0, None, ALU.mult)
                    V.tensor_scalar(xtl[1][:, 2 * PAST:XTW], ident[:, 0:8], 0.0, None, ALU.mult)
                for i in range(8):
                    if n == DB + 1:
                        for q in SPLIT_AT.get(i, ()):
                            rest_of_weights(1, q)
                    if n < 16:
                        v.wait_ge(xt_a, 8 * n + i + 1)
                        hi, lo, src = turned_rows(8 * n + i)
                        V.tensor_tensor(lo, src, hi.bitcast(F32), ALU.subtract).then_inc(xt_d, 1)
                        if i % 4 == 1:
                            link(V.max(st[:, 48:56], wrk[:, :]))
                        if i % 4 == 3:
                            link(V.match_replace(wrk[:, :], st[:, 48:56], wrk[:, :], MARK))
                if 0 <= n - 2 < 16:
                    g = n - 2
                    kv, b = g // 8, g % 8
                    if kv == 0:
                        v.wait_ge(kc_std, g + 1)
                        link(V.reciprocal(cx[:, 256:512], cx[:, 256:512]))
                        V.scalar_tensor_tensor(out=v3(kc, "p (b h c) -> p b h c", b=DB, h=2)[:, b, :, 0:NCS], in0=cx[:, 0:256].rearrange("p (h c) -> p h c", h=2)[:, :, 0:NCS],
                                               scalar=vecT[:, V_AK:V_AK + 1], in1=cx[:, 256:512].rearrange("p (h c) -> p h c", h=2)[:, :, 0:NCS], op0=ALU.mult, op1=ALU.mult).then_inc(kc_ok, 1)
                    else:
                        v.wait_ge(kc_ps, g + 1)
                        V.tensor_tensor(v3(vc, "p (b h c) -> p b h c", b=DB, h=2)[0:NCS, b], bank[6][0:NCS, 0:256].rearrange("p (h c) -> p h c", h=2),
                                        gk[0:NCS, 3 * P:4 * P].unsqueeze(1).broadcast_to([NCS, 2, P]), ALU.add).then_inc(kc_ok, 1)
            V.tensor_scalar(wrk[:, :], wrk[:, :], MARK, NEG, ALU.not_equal, ALU.mult)
            end_phase()

            after(v, 5)
            v.wait_ge(sb_in, 16 * 12)
            for u in range(3):
                link(V.tensor_tensor(nbias[:, u * TS:(u + 1) * TS].rearrange("p (b t) -> p b t", t=DT),
                                     sbias[u][:, PAST:PAST + DT].unsqueeze(1).broadcast_to([P, DB, DT]),
                                     con[:, K_BM + u * TS:K_BM + (u + 1) * TS].rearrange("p (b t) -> p b t", t=DT), ALU.add))
            def outputs(u):
                v.wait_ge(pv_b, 8 * (u + 1))
                if u == 0:
                    v.wait_ge(mx_io, 32)
                if u < 2:
                    o5 = bank[7][:, 0:P].rearrange("p (b k t g) -> p b k t g", b=4, k=2, t=DT)
                    for h in range(AH):
                        m = mix3[:, h, T + 16 * u:T + 16 * u + 16].rearrange("p (b t) -> p b t", t=DT)
                        last = V.tensor_tensor(m, o5[:, :, h // 4, :, h % 4], m, ALU.mult)
                else:
                    for h in range(CH):
                        m = mix3[:, 12 + h, T:TT]
                        last = V.tensor_tensor(m, bank[7][:, h:P:4], m, ALU.mult)
                last.then_inc(un_x, 1)

            gt = 32
            for step, u in STEPS:
                if step == "turn":
                    for gi, src in enumerate(pgroups(u)):
                        if gt % 2 == 1:
                            v.wait_ge(kb_tr, gt + 1)
                            take_p(v, V.tensor_copy, u, gi, src, kb_d)
                        gt += 1
                    if u == 2:
                        outputs(2)
                    continue
                if step == "body" and u < 2:
                    early(v, V, u, link, ttr)
                for x, n in enumerate(blocks_of(step, u)):
                    if step == "body" and u < 2 and x == 8:
                        mid(v, V, u, link)
                    if step == "body" and u < 2 and x == 20:
                        select(v, V, u, link)
                    if gt % 2 == 1:
                        take_k(v, V.tensor_copy, n, gt, kb_d)
                    gt += 1
                if step == "body":
                    late(v, V, u, link, ttr)
                    if u >= 1:
                        outputs(u - 1)
            end_phase()

            after(v, 6)

            def rest(i):
                v.wait_ge(oh_a, i + 1)
                whole, hi, lo = out_views(*out_split[i])
                V.tensor_tensor(lo, whole, hi.bitcast(F32), ALU.subtract).then_inc(ol_d, 1)

            def y_rows(nb):
                c, j = nb // 2, nb % 2
                v.wait_ge(y_tr, nb + 1)
                if j == 0:
                    v.wait_ge(xr_in[c % 2], 32 * (c // 2 + 1))
                if c >= 2 and j == 0:
                    v.wait_ge(y_out, 32 * (c - 1))
                y5 = v3(yrow[c % 2], "p (i d) -> p i d", i=5)
                x5 = v3(xres[c % 2], "p (i d) -> p i d", i=5)
                V.tensor_tensor(y5[:, 0:QT, j * P:(j + 1) * P], bank[4 + nb % 2][:, :].rearrange("p (i d) -> p i d", i=4), x5[:, 0:QT, j * P:(j + 1) * P], ALU.add).then_inc(y_fin, 1)
                V.tensor_tensor(y5[0:TS, QT, j * P:(j + 1) * P], bank[6 + nb % 2][0:TS, 0:P], x5[0:TS, QT, j * P:(j + 1) * P], ALU.add).then_inc(y_fin, 1)

            for i in range(KD + 2):
                rest(i)
            for nb in range(KD):
                if nb + 2 < KD:
                    rest(KD + nb + 2)
                v.wait_ge(y_ps, nb + 1)
                if nb >= 4:
                    v.wait_ge(y_tr, nb - 3)
                s = yT[nb % 4]
                gate = mod3[:, 32 + nb, 0:1]
                V.tensor_scalar(s[:, 0:HALF], bank[2 * (nb % 2)][:, 0:HALF], gate, None, ALU.mult)
                V.tensor_scalar(s[:, HALF:T], bank[2 * (nb % 2) + 1][:, 0:T - HALF], gate, None, ALU.mult)
                V.tensor_tensor(s[:, T:TT].rearrange("p (b t) -> p b t", t=DT), bank[2 * (nb % 2) + 1][:, T - HALF:HALF].rearrange("p (b t) -> p b t", t=DT),
                                bc(mod3[:, 32 + nb, 1:9], DT), ALU.mult).then_inc(y_ev, 1)
                if nb >= 1:
                    y_rows(nb - 1)
            y_rows(KD - 1)


_INS = ["x_prompt", "x_sample", "cache_a_kv", "cache_c_kv", "cache_c_kidx", "state_a_win", "state_b_pool", "page_table",
        "c_prompt", "c_sample", "rel_bias", "norm_g", "w_ada", "b_ada", "w_in", "w_out", "a_qnorm", "a_knorm",
        "a_cmp_pe", "a_cmp_w1", "a_cmp_b1", "a_cmp_w2", "a_cmp_b2", "b_pool_w", "b_scale", "c_qnorm", "c_knorm"]
_OUTS = [("y_prompt", (1, T, D)), ("y_sample", (DB, DT, D)),
         ("a_kv_p", (1, 1, T, 4, KVH, HD)), ("a_kv_s", (1, DB, DT, 4, KVH, HD)),
         ("c_kv_p", (1, 1, T, 2, HD)), ("c_kv_s", (1, DB, DT, 2, HD)),
         ("c_kidx_p", (1, 1, T, ID)), ("c_kidx_s", (1, DB, DT, ID)),
         ("a_win_p", (1, 1, T, 2, KVH, HD)), ("a_win_s", (1, DB, WIN, 2, KVH, HD)),
         ("b_pool_p", (1, 1, 15, 512)), ("b_pool_s", (1, DB, 15, 512))]


def kernel(**inputs):
    import concourse.bacc as bacc
    from concourse.bass_utils import run_bass_kernel_spmd as run

    nc = bacc.Bacc("TRN2", target_bir_lowering=False, num_devices=1)
    arrays, ins, outs = {}, {}, {}
    for name in _INS:
        arrays[f"in_{name}_dram"] = np.ascontiguousarray(inputs[name])
    for name, a in shape_constants().items():
        arrays[f"in_{name}_dram"] = a
    for name, a in arrays.items():
        ins[name[3:-5]] = nc.dram_tensor(name, a.shape, mybir.dt.from_np(a.dtype), kind="ExternalInput").ap()
    for i, (name, shape) in enumerate(_OUTS):
        outs[name] = nc.dram_tensor(f"out_{i}_dram", shape, F32, kind="ExternalOutput").ap()
    build(nc, ins, outs)
    r = run(nc, [arrays], core_ids=[0])
    return tuple(r.results[0][f"out_{i}_dram"] for i in range(len(_OUTS)))
```
